# Optimizing a Trainium2 kernel written in Bass

```python
import jax
import jax.numpy as jnp
from jax import lax
import numpy as np

D_MODEL = 1024
BATCH = 1
SEQ = 512
DEPTH = 4
DEC_BATCH = 8
DEC_SEQ = 1
PAST_LEN = 2048
PAGE_SIZE = 128

N_MIXERS = 3
N_NSA = (DEPTH + 2) // 3
N_RWKV = (DEPTH + 1) // 3
N_CONV = DEPTH // 3

HEAD_DIM = 64
N_HEADS = D_MODEL // HEAD_DIM
N_KV_HEADS = 4
GROUP = N_HEADS // N_KV_HEADS
KV_W = N_KV_HEADS * HEAD_DIM
CMP_LEN = 32
CMP_STRIDE = 16
CMP_RATIO = CMP_LEN // CMP_STRIDE
CMP_HIDDEN = 2 * HEAD_DIM
SEL_BLOCK = 64
N_SEL = 16
WINDOW = 512
Q_BLOCK = 32
ROPE_THETA = 10000.0
NSA_IN = N_HEADS * HEAD_DIM + 6 * KV_W + 3 * N_HEADS

RWKV_HEAD = 64
RWKV_HEADS = D_MODEL // RWKV_HEAD
DECAY_LORA = 64
AAA_LORA = 64
GATE_LORA = 128
GN_EPS = RWKV_HEAD * 1e-5

CONV_W = 31
D_FF = -(-8 * D_MODEL // (3 * 256)) * 256
RMS_EPS = 1e-6
LN_EPS = 1e-5

kernel_name = 'hybrid_nsa_rwkv7_conformer_step'

def rmsnorm(x, g):
    xf = x.astype(jnp.float32)
    y = xf * lax.rsqrt(jnp.mean(xf * xf, axis=-1, keepdims=True) + RMS_EPS)
    return (y * g.astype(jnp.float32)).astype(x.dtype)

def layernorm_f32(x, g, b, eps):
    xf = x.astype(jnp.float32)
    mu = jnp.mean(xf, axis=-1, keepdims=True)
    var = jnp.mean(jnp.square(xf - mu), axis=-1, keepdims=True)
    return (xf - mu) * lax.rsqrt(var + eps) * g.astype(jnp.float32) + b.astype(jnp.float32)

def masked_softmax(s, mask):
    s = jnp.where(mask, s, -jnp.inf)
    m = jnp.max(s, axis=-1, keepdims=True)
    m = jnp.where(jnp.isfinite(m), m, 0.0)
    e = jnp.where(mask, jnp.exp(s - m), 0.0)
    d = jnp.sum(e, axis=-1, keepdims=True)
    return e / jnp.where(d > 0.0, d, 1.0)

def rope(x, pos):
    half = HEAD_DIM // 2
    inv = ROPE_THETA ** (-jnp.arange(half, dtype=jnp.float32) / half)
    ang = pos.astype(jnp.float32)[:, None] * inv
    cos = jnp.cos(ang)[None, :, None, :]
    sin = jnp.sin(ang)[None, :, None, :]
    xf = x.astype(jnp.float32)
    x1, x2 = xf[..., :half], xf[..., half:]
    return jnp.concatenate([x1 * cos - x2 * sin, x2 * cos + x1 * sin], axis=-1).astype(x.dtype)

def swiglu(h, w_gu, w_down):
    gu = h @ w_gu
    return (jax.nn.silu(gu[..., :D_FF]) * gu[..., D_FF:]) @ w_down

def cmp_to_sel(n_cmp, n_slc):
    c0 = jnp.arange(n_cmp)[:, None] * CMP_STRIDE
    j0 = jnp.arange(n_slc)[None, :] * SEL_BLOCK
    return ((c0 < j0 + SEL_BLOCK) & (c0 + CMP_LEN > j0)).astype(jnp.float32)

def nsa_project(h, pos, w_in, q_norm, k_norm):
    B, T, _ = h.shape
    qd = N_HEADS * HEAD_DIM
    proj = h @ w_in
    q = rmsnorm(proj[..., :qd].reshape(B, T, N_HEADS, HEAD_DIM), q_norm)
    kv = proj[..., qd:qd + 6 * KV_W].reshape(B, T, 6, N_KV_HEADS, HEAD_DIM)
    gates = jax.nn.sigmoid(proj[..., qd + 6 * KV_W:].astype(jnp.float32)).reshape(B, T, N_HEADS, 3)
    k_sel = rope(rmsnorm(kv[:, :, 2], k_norm[1]), pos)
    k_win = rope(rmsnorm(kv[:, :, 4], k_norm[2]), pos)
    rows = jnp.stack([kv[:, :, 0], kv[:, :, 1], k_sel, kv[:, :, 3]], axis=2)
    wrows = jnp.stack([k_win, kv[:, :, 5]], axis=2)
    return q, rope(q, pos), gates, rows, wrows

def compress(rows, pe, w1, w2, k_gain):
    B, L = rows.shape[:2]
    n_cmp = (L - CMP_LEN) // CMP_STRIDE + 1
    n_seg = -(-L // CMP_STRIDE)
    rows = jnp.pad(rows, ((0, 0), (0, n_seg * CMP_STRIDE - L), (0, 0), (0, 0), (0, 0)))
    seg = rows.reshape(B, n_seg, CMP_STRIDE, 2, N_KV_HEADS, HEAD_DIM)
    w1r = w1.reshape(2, CMP_RATIO, CMP_STRIDE, HEAD_DIM, CMP_HIDDEN)
    part = jnp.einsum('bnlsgd,srldf->bnrsgf', seg, w1r)
    hid = jnp.einsum('sld,sldf->sf', pe, w1)[:, None, :]
    for r in range(CMP_RATIO):
        hid = hid + part[:, r:r + n_cmp, r]
    out = jnp.einsum('bcsgf,sfd->bcsgd', jax.nn.silu(hid), w2)
    return rmsnorm(out[:, :, 0], k_gain), out[:, :, 1]

def nsa_attend(q_nope, q_rope, gates, pos_q, kc, vc, gather_sel, n_slc, kw, vw, pos_w):
    B, Tq = q_nope.shape[:2]
    f32 = jnp.float32
    scale = HEAD_DIM ** -0.5
    grp = lambda a: a.reshape(B, Tq, N_KV_HEADS, GROUP, HEAD_DIM)
    t = pos_q[:, None]
    n_cmp = kc.shape[1]
    cmp_end = jnp.arange(n_cmp) * CMP_STRIDE + (CMP_LEN - 1)
    s = jnp.einsum('btgnd,bcgd->btgnc', grp(q_nope), kc, preferred_element_type=f32) * scale
    p_cmp = masked_softmax(s, (cmp_end[None, :] <= t)[None, :, None, None, :])
    o_cmp = jnp.einsum('btgnc,bcgd->btgnd', p_cmp.astype(vc.dtype), vc, preferred_element_type=f32)
    score = jnp.einsum('btgnc,cj->btgj', p_cmp, cmp_to_sel(n_cmp, n_slc))
    blk = jnp.arange(n_slc)[None, :]
    cur = t // SEL_BLOCK
    adm = blk * SEL_BLOCK <= t
    forced = adm & ((blk == 0) | (blk == cur) | (blk == cur - 1))
    score = jnp.where(forced[None, :, None, :], jnp.inf, jnp.where(adm[None, :, None, :], score, -jnp.inf))
    top, idx = lax.top_k(score, min(N_SEL, n_slc))
    n_top = idx.shape[-1]
    kv = gather_sel(idx)
    tok = idx[..., None] * SEL_BLOCK + jnp.arange(SEL_BLOCK)
    m_sel = (top > -jnp.inf)[..., None] & (tok <= pos_q[None, :, None, None, None])
    m_sel = m_sel.reshape(B, Tq, N_KV_HEADS, 1, n_top * SEL_BLOCK)
    k_s = kv[..., 0, :].reshape(B, Tq, N_KV_HEADS, n_top * SEL_BLOCK, HEAD_DIM)
    v_s = kv[..., 1, :].reshape(B, Tq, N_KV_HEADS, n_top * SEL_BLOCK, HEAD_DIM)
    s = jnp.einsum('btgnd,btgxd->btgnx', grp(q_rope), k_s, preferred_element_type=f32) * scale
    p = masked_softmax(s, m_sel)
    o_sel = jnp.einsum('btgnx,btgxd->btgnd', p.astype(v_s.dtype), v_s, preferred_element_type=f32)
    pw = pos_w[None, :]
    m_w = (pw <= t) & (pw > t - WINDOW) & (pw >= 0)
    s = jnp.einsum('btgnd,bsgd->btgns', grp(q_rope), kw, preferred_element_type=f32) * scale
    p = masked_softmax(s, m_w[None, :, None, None, :])
    o_win = jnp.einsum('btgns,bsgd->btgnd', p.astype(vw.dtype), vw, preferred_element_type=f32)
    g = gates.reshape(B, Tq, N_KV_HEADS, GROUP, 3)
    o = g[..., 0:1] * o_cmp + g[..., 1:2] * o_sel + g[..., 2:3] * o_win
    return o.reshape(B, Tq, N_HEADS, HEAD_DIM).astype(q_nope.dtype)

def nsa_prompt(h, w_in, q_norm, k_norm, cmp_pe, cmp_w1, cmp_w2, w_out):
    B, T, _ = h.shape
    q, q_rope, gates, rows, wrows = nsa_project(h, jnp.arange(T), w_in, q_norm, k_norm)
    kc, vc = compress(rows[:, :, :2], cmp_pe, cmp_w1, cmp_w2, k_norm[0])
    n_slc = T // SEL_BLOCK
    blocks = rows[:, :, 2:].reshape(B, n_slc, SEL_BLOCK, 2, N_KV_HEADS, HEAD_DIM).transpose(0, 1, 4, 2, 3, 5)
    b_ix = jnp.arange(B)[:, None, None, None]
    g_ix = jnp.arange(N_KV_HEADS)[None, None, :, None]

    def gather_sel(idx):
        return blocks[b_ix, idx, g_ix]

    wpad = jnp.pad(wrows, ((0, 0), (WINDOW, 0), (0, 0), (0, 0), (0, 0)))

    def one_block(c):
        s0 = c * Q_BLOCK
        sl = lambda a: lax.dynamic_slice_in_dim(a, s0, Q_BLOCK, axis=1)
        wk = lax.dynamic_slice_in_dim(wpad, s0, WINDOW + Q_BLOCK, axis=1)
        return nsa_attend(sl(q), sl(q_rope), sl(gates), s0 + jnp.arange(Q_BLOCK), kc, vc, gather_sel, n_slc,
                          wk[:, :, 0], wk[:, :, 1], s0 - WINDOW + jnp.arange(WINDOW + Q_BLOCK))

    o = lax.map(one_block, jnp.arange(T // Q_BLOCK))
    o = o.transpose(1, 0, 2, 3, 4).reshape(B, T, N_HEADS * HEAD_DIM)
    return o @ w_out, rows, wrows[:, T - min(WINDOW, T):]

def nsa_sample(h, cache, j, win_buf, page_table, w_in, q_norm, k_norm, cmp_pe, cmp_w1, cmp_w2, w_out):
    B, T, _ = h.shape
    n_pages = PAST_LEN // PAGE_SIZE
    past_len = n_pages * PAGE_SIZE
    pos = past_len + jnp.arange(T)
    q, q_rope, gates, rows, wrows = nsa_project(h, pos, w_in, q_norm, k_norm)
    past_cmp = cache[j, page_table, :, :2].reshape(B, past_len, 2, N_KV_HEADS, HEAD_DIM)
    kc, vc = compress(jnp.concatenate([past_cmp, rows[:, :, :2]], axis=1), cmp_pe, cmp_w1, cmp_w2, k_norm[0])
    n_slc = -(-(past_len + T) // SEL_BLOCK)
    n_past_blk = past_len // SEL_BLOCK
    n_new_blk = n_slc - n_past_blk
    per_page = PAGE_SIZE // SEL_BLOCK
    new = jnp.pad(rows[:, :, 2:], ((0, 0), (0, n_new_blk * SEL_BLOCK - T), (0, 0), (0, 0), (0, 0)))
    new_blocks = new.reshape(B, n_new_blk, SEL_BLOCK, 2, N_KV_HEADS, HEAD_DIM).transpose(0, 1, 4, 2, 3, 5)
    b_ix = jnp.arange(B)[:, None, None, None]
    g_ix = jnp.arange(N_KV_HEADS)[None, None, :, None]
    g_ix6 = jnp.arange(N_KV_HEADS)[None, None, :, None, None, None]
    slot_ix = jnp.array([2, 3], dtype=jnp.int32)

    def gather_sel(idx):
        is_past = idx < n_past_blk
        ip = jnp.minimum(idx, n_past_blk - 1)
        page = page_table[b_ix, ip // per_page]
        off = (ip % per_page)[..., None] * SEL_BLOCK + jnp.arange(SEL_BLOCK)
        kv_past = cache[j, page[..., None, None], off[..., None], slot_ix, g_ix6]
        kv_new = new_blocks[b_ix, jnp.clip(idx - n_past_blk, 0, n_new_blk - 1), g_ix]
        return jnp.where(is_past[..., None, None, None], kv_past, kv_new)

    wk = jnp.concatenate([win_buf.astype(wrows.dtype), wrows], axis=1)
    wb = win_buf.shape[1]
    o = nsa_attend(q, q_rope, gates, pos, kc, vc, gather_sel, n_slc, wk[:, :, 0], wk[:, :, 1],
                   past_len - wb + jnp.arange(wb + T))
    return o.reshape(B, T, N_HEADS * HEAD_DIM) @ w_out, rows, wk[:, T:]

def rwkv7_mix(h, shift_prev, wkv0, mix, w_rkv, w0, w1, w2, a0, a1, a2, g1, g2, k_k, k_a, r_k, ln_w, ln_b, w_out):
    B, T, D = h.shape
    f32 = jnp.float32
    heads = lambda z: z.astype(f32).reshape(B, T, RWKV_HEADS, RWKV_HEAD)
    prev = jnp.concatenate([shift_prev[:, None].astype(h.dtype), h[:, :-1]], axis=1)
    xm = h[:, :, None] + (prev - h)[:, :, None] * mix
    rkv = jnp.einsum('btsd,sde->btse', xm[:, :, :3], w_rkv)
    r, k, v = heads(rkv[:, :, 0]), rkv[:, :, 1].astype(f32), heads(rkv[:, :, 2])
    w_log = -jax.nn.softplus(-(w0 + jnp.tanh(xm[:, :, 3] @ w1) @ w2).astype(f32)) - 0.5
    decay = heads(jnp.exp(-jnp.exp(w_log)))
    a = jax.nn.sigmoid((a0 + (xm[:, :, 4] @ a1) @ a2).astype(f32))
    g = (jax.nn.sigmoid(xm[:, :, 5] @ g1) @ g2).astype(f32)
    kk = heads(k * k_k)
    kk = kk / jnp.maximum(jnp.sqrt(jnp.sum(kk * kk, axis=-1, keepdims=True)), 1e-12)
    k = heads(k * (1.0 + (a - 1.0) * k_a))
    a = heads(a)

    def step(S, inp):
        r_t, w_t, k_t, v_t, kk_t, a_t = inp
        sa = jnp.einsum('bhij,bhj->bhi', S, -kk_t)
        S = S * w_t[:, :, None, :] + sa[..., None] * (kk_t * a_t)[:, :, None, :] + v_t[..., None] * k_t[:, :, None, :]
        return S, jnp.einsum('bhij,bhj->bhi', S, r_t)

    tm = lambda z: jnp.moveaxis(z, 1, 0)
    S_T, y = lax.scan(step, wkv0.astype(f32), (tm(r), tm(decay), tm(k), tm(v), tm(kk), tm(a)))
    y = jnp.moveaxis(y, 0, 1)
    y = layernorm_f32(y, ln_w.reshape(RWKV_HEADS, RWKV_HEAD), ln_b.reshape(RWKV_HEADS, RWKV_HEAD), GN_EPS)
    y = y + jnp.sum(r * k * r_k, axis=-1, keepdims=True) * v
    out = (y.reshape(B, T, D) * g).astype(h.dtype) @ w_out
    return out, h[:, -1], S_T.astype(wkv0.dtype)

def conv_module(h, buf, w_pw1, b_pw1, w_dw, b_dw, ln_w, ln_b, w_pw2, b_pw2):
    u = h @ w_pw1 + b_pw1
    glu = u[..., :D_MODEL] * jax.nn.sigmoid(u[..., D_MODEL:])
    ext = jnp.concatenate([buf.astype(glu.dtype), glu], axis=1)
    y = lax.conv_general_dilated(ext, w_dw[:, None, :].astype(ext.dtype), window_strides=(1,), padding='VALID',
                                 dimension_numbers=('NWC', 'WIO', 'NWC'), feature_group_count=D_MODEL) + b_dw
    y = jax.nn.silu(layernorm_f32(y, ln_w, ln_b, LN_EPS)).astype(h.dtype)
    return y @ w_pw2 + b_pw2, ext[:, -(CONV_W - 1):]

def setup_inputs(seed: int = 0) -> dict:
    key = jax.random.key(seed)
    keys = iter(jax.random.split(key, 48))
    f32 = jnp.float32

    def nrm(shape, scale):
        return jax.random.normal(next(keys), shape, f32) * scale

    def gain(shape):
        return 1.0 + nrm(shape, 0.02)

    n_pages = PAST_LEN // PAGE_SIZE
    n_used = DEC_BATCH * n_pages
    n_pool = n_used + -(-n_used // 4)
    win_buf = min(WINDOW, PAST_LEN)
    page_table = jax.random.permutation(next(keys), n_pool)[:n_used].reshape(DEC_BATCH, n_pages).astype(jnp.int32)
    return {
        'x_prompt': nrm((BATCH, SEQ, D_MODEL), 1.0),
        'x_sample': nrm((DEC_BATCH, DEC_SEQ, D_MODEL), 1.0),
        'cache_nsa': nrm((N_NSA, n_pool, PAGE_SIZE, 4, N_KV_HEADS, HEAD_DIM), 1.0),
        'cache_nsa_win': nrm((N_NSA, DEC_BATCH, win_buf, 2, N_KV_HEADS, HEAD_DIM), 1.0),
        'state_rwkv_wkv': nrm((N_RWKV, DEC_BATCH, RWKV_HEADS, RWKV_HEAD, RWKV_HEAD), 0.3),
        'state_rwkv_shift': nrm((N_RWKV, DEC_BATCH, D_MODEL), 1.0),
        'state_conv': nrm((N_CONV, DEC_BATCH, CONV_W - 1, D_MODEL), 0.5),
        'page_table': page_table,
        'norms': gain((DEPTH, 2, D_MODEL)),
        'ffn_w_gu': nrm((DEPTH, D_MODEL, 2 * D_FF), D_MODEL ** -0.5),
        'ffn_w_down': nrm((DEPTH, D_FF, D_MODEL), D_FF ** -0.5),
        'nsa_w_in': nrm((N_NSA, D_MODEL, NSA_IN), D_MODEL ** -0.5),
        'nsa_q_norm': gain((N_NSA, HEAD_DIM)),
        'nsa_k_norm': gain((N_NSA, 3, HEAD_DIM)),
        'nsa_cmp_pe': nrm((N_NSA, 2, CMP_LEN, HEAD_DIM), 0.5),
        'nsa_cmp_w1': nrm((N_NSA, 2, CMP_LEN, HEAD_DIM, CMP_HIDDEN), (CMP_LEN * HEAD_DIM) ** -0.5),
        'nsa_cmp_w2': nrm((N_NSA, 2, CMP_HIDDEN, HEAD_DIM), CMP_HIDDEN ** -0.5),
        'nsa_w_out': nrm((N_NSA, N_HEADS * HEAD_DIM, D_MODEL), (N_HEADS * HEAD_DIM) ** -0.5),
        'rwkv_mix': jax.random.uniform(next(keys), (N_RWKV, 6, D_MODEL), f32),
        'rwkv_w_rkv': nrm((N_RWKV, 3, D_MODEL, D_MODEL), D_MODEL ** -0.5),
        'rwkv_w0': nrm((N_RWKV, D_MODEL), 0.5),
        'rwkv_w1': nrm((N_RWKV, D_MODEL, DECAY_LORA), D_MODEL ** -0.5),
        'rwkv_w2': nrm((N_RWKV, DECAY_LORA, D_MODEL), 0.5 * DECAY_LORA ** -0.5),
        'rwkv_a0': nrm((N_RWKV, D_MODEL), 0.5),
        'rwkv_a1': nrm((N_RWKV, D_MODEL, AAA_LORA), D_MODEL ** -0.5),
        'rwkv_a2': nrm((N_RWKV, AAA_LORA, D_MODEL), 0.5 * AAA_LORA ** -0.5),
        'rwkv_g1': nrm((N_RWKV, D_MODEL, GATE_LORA), D_MODEL ** -0.5),
        'rwkv_g2': nrm((N_RWKV, GATE_LORA, D_MODEL), GATE_LORA ** -0.5),
        'rwkv_k_k': 0.85 + nrm((N_RWKV, D_MODEL), 0.05),
        'rwkv_k_a': 1.0 + nrm((N_RWKV, D_MODEL), 0.05),
        'rwkv_r_k': nrm((N_RWKV, RWKV_HEADS, RWKV_HEAD), 0.1),
        'rwkv_ln_w': gain((N_RWKV, D_MODEL)),
        'rwkv_ln_b': nrm((N_RWKV, D_MODEL), 0.02),
        'rwkv_w_out': nrm((N_RWKV, D_MODEL, D_MODEL), D_MODEL ** -0.5),
        'conv_w_pw1': nrm((N_CONV, D_MODEL, 2 * D_MODEL), D_MODEL ** -0.5),
        'conv_b_pw1': nrm((N_CONV, 2 * D_MODEL), 0.02),
        'conv_w_dw': nrm((N_CONV, CONV_W, D_MODEL), CONV_W ** -0.5),
        'conv_b_dw': nrm((N_CONV, D_MODEL), 0.02),
        'conv_ln_w': gain((N_CONV, D_MODEL)),
        'conv_ln_b': nrm((N_CONV, D_MODEL), 0.02),
        'conv_w_pw2': nrm((N_CONV, D_MODEL, D_MODEL), D_MODEL ** -0.5),
        'conv_b_pw2': nrm((N_CONV, D_MODEL), 0.02),
    }

def reference(x_prompt, x_sample, cache_nsa, cache_nsa_win, state_rwkv_wkv, state_rwkv_shift, state_conv,
              page_table, norms, ffn_w_gu, ffn_w_down,
              nsa_w_in, nsa_q_norm, nsa_k_norm, nsa_cmp_pe, nsa_cmp_w1, nsa_cmp_w2, nsa_w_out,
              rwkv_mix, rwkv_w_rkv, rwkv_w0, rwkv_w1, rwkv_w2, rwkv_a0, rwkv_a1, rwkv_a2, rwkv_g1, rwkv_g2,
              rwkv_k_k, rwkv_k_a, rwkv_r_k, rwkv_ln_w, rwkv_ln_b, rwkv_w_out,
              conv_w_pw1, conv_b_pw1, conv_w_dw, conv_b_dw, conv_ln_w, conv_ln_b, conv_w_pw2, conv_b_pw2):
    xp, xs = x_prompt, x_sample
    bp = xp.shape[0]
    rows_p, rows_s, win_p, win_s = [], [], [], []
    wkv_p, wkv_s, shift_p, shift_s, conv_p, conv_s = [], [], [], [], [], []
    for i in range(DEPTH):
        kind, j = i % N_MIXERS, i // N_MIXERS
        hp = rmsnorm(xp, norms[i, 0])
        hs = rmsnorm(xs, norms[i, 0])
        if kind == 0:
            w = (nsa_w_in[j], nsa_q_norm[j], nsa_k_norm[j], nsa_cmp_pe[j], nsa_cmp_w1[j], nsa_cmp_w2[j], nsa_w_out[j])
            mp, r_p, wn_p = nsa_prompt(hp, *w)
            ms, r_s, wn_s = nsa_sample(hs, cache_nsa, j, cache_nsa_win[j], page_table, *w)
            rows_p.append(r_p)
            rows_s.append(r_s)
            win_p.append(wn_p)
            win_s.append(wn_s)
        elif kind == 1:
            w = (rwkv_mix[j], rwkv_w_rkv[j], rwkv_w0[j], rwkv_w1[j], rwkv_w2[j], rwkv_a0[j], rwkv_a1[j], rwkv_a2[j],
                 rwkv_g1[j], rwkv_g2[j], rwkv_k_k[j], rwkv_k_a[j], rwkv_r_k[j], rwkv_ln_w[j], rwkv_ln_b[j], rwkv_w_out[j])
            mp, sh_p, st_p = rwkv7_mix(hp, jnp.zeros((bp, D_MODEL), hp.dtype),
                                       jnp.zeros((bp, RWKV_HEADS, RWKV_HEAD, RWKV_HEAD), jnp.float32), *w)
            ms, sh_s, st_s = rwkv7_mix(hs, state_rwkv_shift[j], state_rwkv_wkv[j], *w)
            wkv_p.append(st_p)
            wkv_s.append(st_s)
            shift_p.append(sh_p)
            shift_s.append(sh_s)
        else:
            w = (conv_w_pw1[j], conv_b_pw1[j], conv_w_dw[j], conv_b_dw[j], conv_ln_w[j], conv_ln_b[j],
                 conv_w_pw2[j], conv_b_pw2[j])
            mp, cb_p = conv_module(hp, jnp.zeros((bp, CONV_W - 1, D_MODEL), hp.dtype), *w)
            ms, cb_s = conv_module(hs, state_conv[j], *w)
            conv_p.append(cb_p)
            conv_s.append(cb_s)
        xp = xp + mp
        xs = xs + ms
        xp = xp + swiglu(rmsnorm(xp, norms[i, 1]), ffn_w_gu[i], ffn_w_down[i])
        xs = xs + swiglu(rmsnorm(xs, norms[i, 1]), ffn_w_gu[i], ffn_w_down[i])
    return (xp, xs, jnp.stack(rows_p), jnp.stack(rows_s), jnp.stack(win_p), jnp.stack(win_s),
            jnp.stack(wkv_p), jnp.stack(wkv_s), jnp.stack(shift_p), jnp.stack(shift_s),
            jnp.stack(conv_p), jnp.stack(conv_s))


_drawn_inputs = setup_inputs


def setup_inputs(seed=0):
    import zlib

    import numpy as np

    out = dict(_drawn_inputs(seed))
    spreads = {}
    factors = {'nsa_q_norm': 8.0,
     'nsa_k_norm': 4.2,
     'rwkv_k_k': 13.604,
     'rwkv_ln_w': 5.855,
     'rwkv_ln_b': 5.278,
     'conv_b_pw1': 2.734,
     'conv_b_dw': 2.815,
     'conv_ln_w': 5.291,
     'conv_ln_b': 5.867,
     'conv_b_pw2': 10.566}
    for name, (base, spread) in spreads.items():
        noise = np.random.default_rng([zlib.crc32(name.encode()), seed]).standard_normal(out[name].shape)
        drawn = base * np.exp(spread * noise) if base else spread * noise
        out[name] = jnp.asarray(drawn.astype(out[name].dtype))
    for name, factor in factors.items():
        out[name] = (out[name] * factor).astype(out[name].dtype)
    return out
```

```python
from contextlib import ExitStack

import concourse.bass as bass
from concourse import mybir
import numpy as np

F32 = mybir.dt.float32
I32 = mybir.dt.int32
ALU = mybir.AluOpType
ACT = mybir.ActivationFunctionType
AXX = mybir.AxisListType.X

P = 128
D = 1024
KC = D // P
SEQ = 512
NB = 8
T = SEQ + NB
HALF = T // 2
DEPTH = 4
D_FF = 2816
FC = D_FF // P
HD = 64
NH = 16
NG = 4
KVW = NG * HD
PROJ = D + 6 * KVW + 3 * NH
PAST = 2048
PAGE = 128
NPAGE = PAST // PAGE
SCALE = HD ** -0.5
RMS_EPS = 1e-6
LN_EPS = 1e-5
GN_EPS = HD * 1e-5
NEG = -1e30


class Signal:

    def __init__(self, sem):
        self.sem = sem
        self.base = 0

    def at(self, n):
        return self.base + n

    def close(self, n):
        self.base += n


class Core:

    def __init__(self, nc, ctx, io):
        self.nc, self.ctx, self.io = nc, ctx, io
        self.signals, self.kept, self.idle = {}, {}, []
        self.uid = 0

    def sig(self, name, pool_dma=False):
        found = self.kept if pool_dma else self.signals
        if name not in found:
            if self.idle and not pool_dma:
                found[name] = self.idle.pop()
            else:
                self.uid += 1
                found[name] = Signal(self.ctx.enter_context(self.nc.semaphore(f"{name}_{self.uid}")))
        return found[name]

    def end_stage(self):
        self.idle += self.signals.values()
        self.signals = {}


class Chain:

    def __init__(self, core, eng, name):
        self.eng, self.done, self.n = eng, core.sig(name), 0

    def link(self, ins):
        self.n += 1
        ins.then_inc(self.done.sem, 1)
        self.eng.wait_ge(self.done.sem, self.done.at(self.n))

    def close(self):
        self.done.close(self.n)


def tiles(core, stage):
    nc = core.nc

    def sb(name, shape, dt=F32):
        core.uid += 1
        return stage.enter_context(nc.sbuf_tensor(f"{name}_{core.uid}", shape, dt))

    def ps(name, shape, dt=F32):
        core.uid += 1
        return stage.enter_context(nc.psum_tensor(f"{name}_{core.uid}", shape, dt))

    return sb, ps



def norm_act(core, act, sq, std, ps):
    sq_ready, sum_ready, std_ready = core.sig("norm_sq_ready"), core.sig("norm_sum_ready"), core.sig("norm_std_ready")
    for k in range(KC):
        act.activation(sq[:, k, :], core.xT[:, k, :], ACT.Square).then_inc(sq_ready.sem, 1)
    act.wait_ge(sum_ready.sem, sum_ready.at(1))
    act.activation(std[:, :].rearrange("p (a t) -> p a t", a=2), ps[:, 0:2, 0:HALF], ACT.Sqrt, bias=core.col("eps_rms"),
                   scale=1.0 / D).then_inc(std_ready.sem, 1)


def norm_pe(core, pe, sq, ps):
    sq_ready, sum_ready = core.sig("norm_sq_ready"), core.sig("norm_sum_ready")
    for k in range(KC):
        pe.wait_ge(sq_ready.sem, sq_ready.at(k + 1))
        for a in range(2):
            mm = pe.matmul(ps[:, a, 0:HALF], core.ones[:, :], sq[:, k, a * HALF:(a + 1) * HALF],
                           start=(k == 0), stop=(k == KC - 1))
    mm.then_inc(sum_ready.sem, 1)


def norm_dve(core, dve, std, gain):
    std_ready, inv_ready, h_ready = core.sig("norm_std_ready"), core.sig("norm_inv_ready"), core.sig("norm_h_ready")
    dve.wait_ge(std_ready.sem, std_ready.at(1))
    dve.reciprocal(std[:, :], std[:, :]).then_inc(inv_ready.sem, 1)
    dve.wait_ge(inv_ready.sem, inv_ready.at(1))
    for k in range(KC):
        dve.scalar_tensor_tensor(out=core.hT[:, k, :], in0=core.xT[:, k, :], scalar=gain[:, k:k + 1],
                                 in1=std[:, :], op0=ALU.mult, op1=ALU.mult).then_inc(h_ready.sem, 1)


def norm_close(core):
    for name, n in (("norm_sq_ready", KC), ("norm_sum_ready", 1), ("norm_std_ready", 1), ("norm_inv_ready", 1),
                    ("norm_h_ready", KC)):
        core.sig(name).close(n)



def ffn_stage(core, layer):
    nc = core.nc
    w_gu, w_down = core.io["w_gu"], core.io["w_down"]
    gain = core.gains[:, 2 * layer + 1, :]
    h_ready = core.sig("norm_h_ready")
    up_in = [core.sig(f"ffn_up_in{u}") for u in range(2)]
    down_in = [core.sig(f"ffn_down_in{u}") for u in range(2)]
    gate_ready, up_ready = core.sig("ffn_gate_ready"), core.sig("ffn_up_ready")
    silu_ready, gu_done = core.sig("ffn_silu_ready"), core.sig("ffn_gu_done")
    down_ready, add_done = core.sig("ffn_down_ready"), core.sig("ffn_add_done")
    with ExitStack() as stage:
        sb, ps = tiles(core, stage)
        sq = sb("sq", [P, KC, T])
        std = sb("std", [P, T])
        wu = [sb(f"wu{u}", [P, 2, KC, P]) for u in range(2)]
        wd = [sb(f"wd{u}", [P, FC, P]) for u in range(2)]
        guT = sb("guT", [P, FC, T])
        silu = [sb(f"silu{u}", [P, T]) for u in range(2)]
        acc = [ps(f"acc{u}", [P, 4, 512]) for u in range(2)]
        block = stage.enter_context(nc.Block())

        @block.sync
        def _(sync):
            for u in range(2):
                sync.dma_start(wu[u][:], w_gu[layer, u]).then_inc(up_in[u].sem, 16)
            with sync.Fori(1, FC // 2) as j:
                for u in range(2):
                    sync.wait_ge(up_ready.sem, up_ready.at(0) + j * 2 + (u - 1))
                    sync.dma_start(wu[u][:], w_gu[layer, bass.ds(j * 2 + u, 1)].rearrange("o p m k n -> (o p) m k n")
                                   ).then_inc(up_in[u].sem, 16)
            for u in range(2):
                sync.dma_start(wd[u][:], w_down[layer, u]).then_inc(down_in[u].sem, 16)
            with sync.Fori(1, KC // 2) as j:
                for u in range(2):
                    sync.wait_ge(down_ready.sem, down_ready.at(0) + j * 2 + (u - 1))
                    sync.dma_start(wd[u][:], w_down[layer, bass.ds(j * 2 + u, 1)].rearrange("o p k n -> (o p) k n")
                                   ).then_inc(down_in[u].sem, 16)

        @block.tensor
        def _(pe):
            norm_pe(core, pe, sq, acc[0])
            pe.wait_ge(h_ready.sem, h_ready.at(KC))
            with pe.Fori(0, FC // 2) as j:
                for u in range(2):
                    pe.wait_ge(up_in[u].sem, up_in[u].at(16) + j * 16)
                    pe.wait_ge(gu_done.sem, gu_done.at(1) + j * 2 + u)
                    for m, ready in ((0, gate_ready), (1, up_ready)):
                        for a in range(2):
                            for k in range(KC):
                                mm = pe.matmul(acc[u][:, 2 * m + a, 0:HALF], wu[u][:, m, k, :],
                                               core.hT[:, k, a * HALF:(a + 1) * HALF],
                                               start=(k == 0), stop=(k == KC - 1))
                        mm.then_inc(ready.sem, 1)
            pe.wait_ge(gu_done.sem, gu_done.at(FC + 2))
            with pe.Fori(0, KC // 2) as j:
                for u in range(2):
                    pe.wait_ge(down_in[u].sem, down_in[u].at(16) + j * 16)
                    pe.wait_ge(add_done.sem, add_done.at(1) + j * 2 + u)
                    for a in range(2):
                        for k in range(FC):
                            mm = pe.matmul(acc[u][:, a, 0:HALF], wd[u][:, k, :], guT[:, k, a * HALF:(a + 1) * HALF],
                                           start=(k == 0), stop=(k == FC - 1))
                    mm.then_inc(down_ready.sem, 1)

        @block.scalar
        def _(act):
            norm_act(core, act, sq, std, acc[0])
            with act.Fori(0, FC // 2) as j:
                for u in range(2):
                    act.wait_ge(gate_ready.sem, gate_ready.at(1) + j * 2 + u)
                    act.wait_ge(gu_done.sem, gu_done.at(1) + j * 2 + u)
                    act.activation(silu[u][:, :].rearrange("p (a t) -> p a t", a=2), acc[u][:, 0:2, 0:HALF],
                                   ACT.Silu).then_inc(silu_ready.sem, 1)

        @block.vector
        def _(dve):
            dve.sem_inc(gu_done.sem, 2)
            dve.sem_inc(add_done.sem, 2)
            norm_dve(core, dve, std, gain)
            with dve.Fori(0, FC // 2) as j:
                for u in range(2):
                    dve.wait_ge(silu_ready.sem, silu_ready.at(1) + j * 2 + u)
                    dve.wait_ge(up_ready.sem, up_ready.at(1) + j * 2 + u)
                    dve.tensor_tensor(
                        guT[:, bass.ds(j * 2 + u, 1), :].rearrange("p o (a t) -> p (o a) t", a=2),
                        silu[u][:, :].rearrange("p (a t) -> p a t", a=2), acc[u][:, 2:4, 0:HALF], ALU.mult
                    ).then_inc(gu_done.sem, 1)
            with dve.Fori(0, KC // 2) as j:
                for u in range(2):
                    dve.wait_ge(down_ready.sem, down_ready.at(1) + j * 2 + u)
                    xk = core.xT[:, bass.ds(j * 2 + u, 1), :].rearrange("p o (a t) -> p (o a) t", a=2)
                    dve.tensor_tensor(xk, xk, acc[u][:, 0:2, 0:HALF], ALU.add).then_inc(add_done.sem, 1)

    norm_close(core)
    for u in range(2):
        up_in[u].close(16 * FC // 2)
        down_in[u].close(16 * KC // 2)
    gate_ready.close(FC)
    up_ready.close(FC)
    silu_ready.close(FC)
    gu_done.close(FC + 2)
    down_ready.close(KC)
    add_done.close(KC + 2)
    core.end_stage()



def linear_sync(core, sync, slots, w, n, first):
    ready = core.sig("lin_ready")
    for u in range(2):
        if first:
            sync.wait_ge(ready.sem, ready.at(first - 1 + u))
        sync.dma_start(slots[u][:], w[u]).then_inc(core.sig(f"lin_in{u}").sem, 16)
    if n > 2:
        with sync.Fori(1, n // 2) as j:
            for u in range(2):
                sync.wait_ge(ready.sem, ready.at(first - 1 + u) + j * 2)
                sync.dma_start(slots[u][:], w[bass.ds(j * 2 + u, 1)].rearrange("o p k n -> (o p) k n")
                               ).then_inc(core.sig(f"lin_in{u}").sem, 16)


def linear_pe(core, pe, slots, src, acc, n, first, K=KC):
    ready, used = core.sig("lin_ready"), core.sig("lin_used")
    with pe.Fori(0, n // 2) as j:
        for u in range(2):
            w_in = core.sig(f"lin_in{u}")
            pe.wait_ge(w_in.sem, w_in.at(16 * (first // 2 + 1)) + j * 16)
            pe.wait_ge(used.sem, used.at(first + 1 + u) + j * 2)
            for a in range(2):
                for k in range(K):
                    mm = pe.matmul(acc[u][:, a, 0:HALF], slots[u][:, k, :], src[:, k, a * HALF:(a + 1) * HALF],
                                   start=(k == 0), stop=(k == K - 1))
            mm.then_inc(ready.sem, 1)


def linear_close(core, n):
    for u in range(2):
        core.sig(f"lin_in{u}").close(16 * n // 2)
    core.sig("lin_ready").close(n)
    core.sig("lin_used").close(n + 2)


def halves(ap):
    return ap.rearrange("p (a t) -> p a t", a=2)



TAPS = 31
HIST = TAPS - 1
PE_TAP_CHUNKS = 3


def conv_stage(core, _):
    nc, io = core.nc, core.io
    gain = core.gains[:, 4, :]
    h_ready, h_used = core.sig("norm_h_ready"), core.sig("conv_h_used")
    pw_in = [core.sig(f"conv_pw_in{u}") for u in range(2)]
    par_in = core.sig("conv_par_in")
    val_ready, gate_ready = core.sig("conv_val_ready"), core.sig("conv_gate_ready")
    sig_ready, glu_ready = core.sig("conv_sig_ready"), core.sig("conv_glu_ready")
    zero_ready, diag_ready, diag_used = core.sig("conv_zero_ready"), core.sig("conv_diag_ready"), core.sig("conv_diag_used")
    tap_ready = core.sig("conv_tap_ready")
    y_ready, mean_ready, yc_ready, sq_ready = (core.sig("conv_" + n) for n in ("y_ready", "mean_ready", "yc_ready", "sq_ready"))
    var_ready, std_ready, n_ready, z_ready = (core.sig("conv_" + n) for n in ("var_ready", "std_ready", "n_ready", "z_ready"))
    lin_ready, lin_used = core.sig("lin_ready"), core.sig("lin_used")
    stored, hist_ready = core.sig("conv_stored"), core.sig("conv_hist_ready")
    dve_taps = KC - PE_TAP_CHUNKS
    with ExitStack() as stage:
        sb, ps = tiles(core, stage)
        sq = sb("sq", [P, KC, T])
        std = sb("std", [P, T])
        w1 = [sb(f"w1{u}", [P, 2, KC, P]) for u in range(2)]
        w2 = [sb(f"w2{u}", [P, KC, P]) for u in range(2)]
        gate = [sb(f"gate{u}", [P, T]) for u in range(2)]
        ext = sb("ext", [P, KC, HIST + T])
        hist = sb("hist", [P, KC, NB, TAPS])
        prod = sb("prod", [P, NB, TAPS])
        newhist = sb("newhist", [P, KC, NB, HIST])
        taps = sb("taps", [P, KC, TAPS])
        par = sb("par", [P, 6, KC])
        diag = [sb(f"diag{u}", [P, P]) for u in range(4)]
        acc = [ps(f"acc{u}", [P, 4, 512]) for u in range(2)]
        y = core.hT
        B_VAL, B_GATE, B_DW, LN_W, LN_B, B_PW2 = range(6)
        block = stage.enter_context(nc.Block())

        @block.sync
        def _(sync):
            sync.dma_start(par[:], io["conv_par"]).then_inc(par_in.sem, 16)
            sync.dma_start(taps[:], io["conv_taps"]).then_inc(par_in.sem, 16)
            sync.dma_start(hist[:, :, :, 0:HIST], io["conv_hist"]).then_inc(par_in.sem, 16)
            for c in range(KC):
                if c >= 2:
                    sync.wait_ge(val_ready.sem, val_ready.at(c - 1))
                sync.dma_start(w1[c % 2][:], io["conv_w1"][c]).then_inc(pw_in[c % 2].sem, 16)
            linear_sync(core, sync, w2, io["conv_w2"], KC, 0)
            sync.wait_ge(glu_ready.sem, glu_ready.at(KC))
            sync.dma_start(io["conv_prompt"], ext[:, :, SEQ:SEQ + HIST]).then_inc(stored.sem, 16)
            sync.wait_ge(hist_ready.sem, hist_ready.at(1))
            sync.dma_start(io["conv_sample"], newhist[:]).then_inc(stored.sem, 16)
            sync.wait_ge(stored.sem, stored.at(32))

        @block.tensor
        def _(pe):
            norm_pe(core, pe, sq, acc[0])
            pe.wait_ge(h_ready.sem, h_ready.at(KC))
            for c in range(KC):
                u = c % 2
                pe.wait_ge(pw_in[u].sem, pw_in[u].at(16 * (c // 2 + 1)))
                if c >= 2:
                    pe.wait_ge(glu_ready.sem, glu_ready.at(c - 1))
                for m, ready in ((1, gate_ready), (0, val_ready)):
                    for a in range(2):
                        for k in range(KC):
                            mm = pe.matmul(acc[u][:, 2 * m + a, 0:HALF], w1[u][:, m, k, :],
                                           core.hT[:, k, a * HALF:(a + 1) * HALF], start=(k == 0), stop=(k == KC - 1))
                    mm.then_inc(ready.sem, 1)
            pe.wait_ge(glu_ready.sem, glu_ready.at(KC))
            for n in range(PE_TAP_CHUNKS):
                for i in range(TAPS):
                    m = n * TAPS + i
                    pe.wait_ge(diag_ready.sem, diag_ready.at(m + 1))
                    mm = pe.matmul(acc[0][:, n, :], diag[m % 4][:, :], ext[:, dve_taps + n, i:i + SEQ],
                                   start=(i == 0), stop=(i == TAPS - 1))
                    mm.then_inc(diag_used.sem, 1)
            for k in range(KC):
                pe.wait_ge(y_ready.sem, y_ready.at(k + 1))
                for a in range(2):
                    mm = pe.matmul(acc[1][:, a, 0:HALF], core.ones[:, :], y[:, k, a * HALF:(a + 1) * HALF],
                                   start=(k == 0), stop=(k == KC - 1))
            mm.then_inc(mean_ready.sem, 1)
            for k in range(KC):
                pe.wait_ge(sq_ready.sem, sq_ready.at(k + 1))
                for a in range(2):
                    mm = pe.matmul(acc[1][:, 2 + a, 0:HALF], core.ones[:, :], sq[:, k, a * HALF:(a + 1) * HALF],
                                   start=(k == 0), stop=(k == KC - 1))
            mm.then_inc(var_ready.sem, 1)
            pe.wait_ge(z_ready.sem, z_ready.at(KC))
            linear_pe(core, pe, w2, y, acc, KC, 0)

        @block.scalar
        def _(act):
            norm_act(core, act, sq, std, acc[0])
            act.wait_ge(par_in.sem, par_in.at(48))
            for c in range(KC):
                act.wait_ge(gate_ready.sem, gate_ready.at(c + 1))
                if c >= 2:
                    act.wait_ge(glu_ready.sem, glu_ready.at(c - 1))
                act.activation(halves(gate[c % 2][:, :]), acc[c % 2][:, 2:4, 0:HALF], ACT.Sigmoid,
                               bias=par[:, B_GATE, c:c + 1]).then_inc(sig_ready.sem, 1)
            for m in range(PE_TAP_CHUNKS * TAPS):
                if m >= 4:
                    act.wait_ge(diag_used.sem, diag_used.at(m - 3))
                act.activation(diag[m % 4][:, :], core.ident[:, :], ACT.Copy,
                               scale=taps[:, dve_taps + m // TAPS, m % TAPS:m % TAPS + 1]).then_inc(diag_ready.sem, 1)
            for k in range(KC):
                act.wait_ge(yc_ready.sem, yc_ready.at(k + 1))
                act.activation(sq[:, k, :], y[:, k, :], ACT.Square).then_inc(sq_ready.sem, 1)
            act.wait_ge(var_ready.sem, var_ready.at(1))
            act.activation(halves(std[:, :]), acc[1][:, 2:4, 0:HALF], ACT.Sqrt, bias=core.col("eps_ln"),
                           scale=1.0 / D).then_inc(std_ready.sem, 1)
            for k in range(KC):
                act.wait_ge(n_ready.sem, n_ready.at(k + 1))
                act.activation(y[:, k, :], y[:, k, :], ACT.Silu, bias=par[:, LN_B, k:k + 1],
                               scale=par[:, LN_W, k:k + 1]).then_inc(z_ready.sem, 1)

        @block.vector
        def _(dve):
            chain = Chain(core, dve, "dve_chain")
            dve.sem_inc(lin_used.sem, 2)
            norm_dve(core, dve, std, gain)
            chain.link(dve.memset(ext[:, :, 0:HIST], 0.0))
            dve.wait_ge(par_in.sem, par_in.at(48))
            for c in range(KC):
                dve.wait_ge(sig_ready.sem, sig_ready.at(c + 1))
                dve.wait_ge(val_ready.sem, val_ready.at(c + 1))
                dve.scalar_tensor_tensor(out=halves(ext[:, c, HIST:]), in0=acc[c % 2][:, 0:2, 0:HALF],
                                         scalar=par[:, B_VAL, c:c + 1], in1=halves(gate[c % 2][:, :]),
                                         op0=ALU.add, op1=ALU.mult).then_inc(glu_ready.sem, 1)
            dve.wait_ge(glu_ready.sem, glu_ready.at(KC))
            chain.link(dve.tensor_copy(hist[:, :, :, HIST:TAPS].rearrange("p k b o -> p k (b o)"), ext[:, :, HIST + SEQ:]))
            dve.tensor_copy(newhist[:], hist[:, :, :, 1:TAPS]).then_inc(hist_ready.sem, 1)
            for k in range(KC):
                chain.link(dve.tensor_tensor(prod[:], hist[:, k], taps[:, k, :].rearrange("p (o i) -> p o i", o=1)
                                             .broadcast_to([P, NB, TAPS]), ALU.mult))
                chain.link(dve.tensor_reduce(y[:, k, SEQ:T], prod[:], AXX, ALU.add))
                if k < dve_taps:
                    for i in range(TAPS):
                        e = ext[:, k, i:i + SEQ]
                        if i == 0:
                            ins = dve.tensor_scalar(y[:, k, 0:SEQ], e, taps[:, k, 0:1], None, ALU.mult)
                        else:
                            ins = dve.scalar_tensor_tensor(out=y[:, k, 0:SEQ], in0=e, scalar=taps[:, k, i:i + 1],
                                                           in1=y[:, k, 0:SEQ], op0=ALU.mult, op1=ALU.add)
                        chain.link(ins)
                else:
                    n = k - dve_taps
                    dve.wait_ge(diag_used.sem, diag_used.at((n + 1) * TAPS))
                    chain.link(dve.tensor_copy(y[:, k, 0:SEQ], acc[0][:, n, :]))
                dve.tensor_scalar(y[:, k, :], y[:, k, :], par[:, B_DW, k:k + 1], None, ALU.add).then_inc(y_ready.sem, 1)
            dve.wait_ge(mean_ready.sem, mean_ready.at(1))
            dve.wait_ge(y_ready.sem, y_ready.at(KC))
            for k in range(KC):
                dve.scalar_tensor_tensor(out=halves(y[:, k, :]), in0=acc[1][:, 0:2, 0:HALF], scalar=-1.0 / D,
                                         in1=halves(y[:, k, :]), op0=ALU.mult, op1=ALU.add).then_inc(yc_ready.sem, 1)
            dve.wait_ge(std_ready.sem, std_ready.at(1))
            chain.link(dve.reciprocal(std[:, :], std[:, :]))
            dve.wait_ge(sq_ready.sem, sq_ready.at(KC))
            for k in range(KC):
                dve.tensor_tensor(y[:, k, :], y[:, k, :], std[:, :], ALU.mult).then_inc(n_ready.sem, 1)
            for c in range(KC):
                dve.wait_ge(lin_ready.sem, lin_ready.at(c + 1))
                xk = halves(core.xT[:, c, :])
                dve.scalar_tensor_tensor(out=xk, in0=acc[c % 2][:, 0:2, 0:HALF], scalar=par[:, B_PW2, c:c + 1], in1=xk,
                                         op0=ALU.add, op1=ALU.add).then_inc(lin_used.sem, 1)
            chain.close()

    norm_close(core)
    linear_close(core, KC)
    for u in range(2):
        pw_in[u].close(16 * KC // 2)
    par_in.close(48)
    for s in (val_ready, gate_ready, sig_ready, glu_ready, y_ready, yc_ready, sq_ready, n_ready, z_ready):
        s.close(KC)
    for s in (diag_ready, diag_used):
        s.close(PE_TAP_CHUNKS * TAPS)
    for s in (mean_ready, var_ready, std_ready, hist_ready):
        s.close(1)
    stored.close(32)
    core.end_stage()




CH = 64
NCH = SEQ // CH
NT = SEQ // P
HP = NH // 2
DECAY = float(np.exp(-0.5))
LEVELS = 6
MIX = ["k_k", "k_a", "r_k", "ln_w", "ln_b", "w0", "a0", "mix0", "mix1", "mix2", "mix3", "mix4", "mix5"]


def rwkv_project(core, stage, r, k, v, s, a, par):
    nc, io = core.nc, core.io
    h_ready, par_in, lora_in = core.sig("norm_h_ready"), core.sig("rwkv_par_in"), core.sig("rwkv_lora_in", pool_dma=True)
    mix_ready, lin_ready, lin_used = core.sig("rwkv_mix_ready"), core.sig("lin_ready"), core.sig("lin_used")
    low_ready, act_ready = core.sig("rwkv_low_ready"), core.sig("rwkv_act_ready")
    lora_ready, lora_used = core.sig("rwkv_lora_ready"), core.sig("rwkv_lora_used")
    stored = core.sig("rwkv_proj_stored")
    gain = core.gains[:, 2, :]
    with ExitStack() as inner:
        sb, ps = tiles(core, inner)
        diff = sb("diff", [P, KC, T])
        g = diff
        std = sb("std", [P, T])
        mixed = [sb(f"mixed{u}", [P, KC, T]) for u in range(2)]
        shift = sb("shift", [P, KC, NB])
        slots = [sb(f"w{u}", [P, KC, P]) for u in range(2)]
        down = [sb("down_w", [P, KC, 64]), sb("down_a", [P, KC, 64]), sb("down_g", [P, KC, P])]
        up = [sb("up_w", [64, D]), sb("up_a", [64, D]), sb("up_g", [P, D])]
        low = [sb("low_w", [64, T]), sb("low_a", [64, T]), sb("low_g", [P, T])]
        acc = [ps(f"acc{u}", [P, 4, 512]) for u in range(2)]
        sq = mixed[1]
        low_acc = [acc[0][0:64, 0:2, 0:HALF], acc[0][0:64, 2:4, 0:HALF], acc[1][:, 0:2, 0:HALF]]
        block = inner.enter_context(nc.Block())

        @block.sync
        def _(sync):
            sync.dma_start(par[:], io["rwkv_par"]).then_inc(par_in.sem, 16)
            sync.dma_start(shift[:], io["rwkv_shift"]).then_inc(par_in.sem, 16)
            linear_sync(core, sync, slots, io["rwkv_rkv"], 3 * KC, 0)
            sync.wait_ge(h_ready.sem, h_ready.at(KC))
            sync.dma_start(io["shift_out"], core.hT[:, :, SEQ - 1:T]).then_inc(stored.sem, 16)
            sync.wait_ge(lora_used.sem, lora_used.at(3 * KC))
            sync.dma_start(io["s_gate"], g[:]).then_inc(stored.sem, 16)
            sync.wait_ge(stored.sem, stored.at(32))

        @block.gpsimd
        def _(pool):
            for m in range(3):
                pool.dma_start(down[m][:], io[f"rwkv_down{m}"]).then_inc(lora_in.sem, 16)
                pool.dma_start(up[m][:], io[f"rwkv_up{m}"]).then_inc(lora_in.sem, 16)

        @block.tensor
        def _(pe):
            norm_pe(core, pe, sq, acc[0])
            for m in range(3):
                pe.wait_ge(mix_ready.sem, mix_ready.at(KC * (m + 1)))
                linear_pe(core, pe, slots, mixed[m % 2], acc, KC, KC * m)
            pe.wait_ge(lin_used.sem, lin_used.at(3 * KC + 2))
            pe.wait_ge(lora_in.sem, lora_in.at(96))
            for m in range(3):
                pe.wait_ge(mix_ready.sem, mix_ready.at(KC * (m + 4)))
                for half in range(2):
                    for i in range(KC):
                        mm = pe.matmul(low_acc[m][:, half, :], down[m][:, i, :],
                                       mixed[(m + 3) % 2][:, i, half * HALF:(half + 1) * HALF],
                                       start=(i == 0), stop=(i == KC - 1))
                mm.then_inc(low_ready.sem, 1)
            pe.wait_ge(act_ready.sem, act_ready.at(3))
            for n in range(3 * KC):
                m, c, q = n // KC, n % KC, n % 4
                if n >= 4:
                    pe.wait_ge(lora_used.sem, lora_used.at(n - 3))
                for half in range(2):
                    mm = pe.matmul(acc[q // 2][:, 2 * (q % 2) + half, 0:HALF], up[m][:, c * P:(c + 1) * P],
                                   low[m][:, half * HALF:(half + 1) * HALF], start=True, stop=True)
                mm.then_inc(lora_ready.sem, 1)

        @block.scalar
        def _(act):
            norm_act(core, act, sq, std, acc[0])
            for n in range(3 * KC):
                act.wait_ge(lin_ready.sem, lin_ready.at(n + 1))
                act.activation(halves((r, k, v)[n // KC][:, n % KC, :]), acc[n % 2][:, 0:2, 0:HALF], ACT.Copy
                               ).then_inc(lin_used.sem, 1)
            for m, func in enumerate((ACT.Tanh, ACT.Copy, ACT.Sigmoid)):
                act.wait_ge(low_ready.sem, low_ready.at(m + 1))
                act.activation(halves(low[m][:, :]), low_acc[m], func).then_inc(act_ready.sem, 1)
            act.wait_ge(par_in.sem, par_in.at(32))
            for n in range(3 * KC):
                m, c, q = n // KC, n % KC, n % 4
                act.wait_ge(lora_ready.sem, lora_ready.at(n + 1))
                src = acc[q // 2][:, 2 * (q % 2):2 * (q % 2) + 2, 0:HALF]
                if m < 2:
                    bias = par[:, MIX.index(("w0", "a0")[m]), c:c + 1]
                    ins = act.activation(halves((s, a)[m][:, c, :]), src, ACT.Sigmoid, bias=bias)
                else:
                    ins = act.activation(halves(g[:, c, :]), src, ACT.Copy)
                ins.then_inc(lora_used.sem, 1)

        @block.vector
        def _(dve):
            chain = Chain(core, dve, "dve_chain")
            dve.sem_inc(lin_used.sem, 2)
            norm_dve(core, dve, std, gain)
            dve.wait_ge(h_ready.sem, h_ready.at(KC))
            dve.wait_ge(par_in.sem, par_in.at(32))
            h = core.hT
            dve.tensor_scalar(diff[:, :, 0:1], h[:, :, 0:1], -1.0, None, ALU.mult)
            dve.tensor_tensor(diff[:, :, 1:SEQ], h[:, :, 0:SEQ - 1], h[:, :, 1:SEQ], ALU.subtract)
            chain.link(dve.tensor_tensor(diff[:, :, SEQ:T], shift[:], h[:, :, SEQ:T], ALU.subtract))
            chain.link(dve.engine_nop())
            for m in range(6):
                if 2 <= m <= 4:
                    dve.wait_ge(lin_ready.sem, lin_ready.at(KC * (m - 1)))
                if m == 5:
                    dve.wait_ge(low_ready.sem, low_ready.at(1))
                for c in range(KC):
                    dve.scalar_tensor_tensor(out=mixed[m % 2][:, c, :], in0=diff[:, c, :],
                                             scalar=par[:, MIX.index(f"mix{m}"), c:c + 1], in1=h[:, c, :],
                                             op0=ALU.mult, op1=ALU.add).then_inc(mix_ready.sem, 1)
            chain.close()

    norm_close(core)
    linear_close(core, 3 * KC)
    par_in.close(32)
    lora_in.close(96)
    mix_ready.close(6 * KC)
    low_ready.close(3)
    act_ready.close(3)
    lora_ready.close(3 * KC)
    lora_used.close(3 * KC)
    stored.close(32)
    core.end_stage()


def rwkv_prepare(core, stage, r, k, v, s, a, wc, par):
    nc, io = core.nc, core.io
    kk = core.hT
    names = ("kk_ready", "kksq_ready", "nsum_ready", "norm_ready", "inv_ready", "bc_ready", "kkn_ready", "cs_ready",
             "dcs_ready", "exp_ready", "exp_used", "rk_ready", "dot_ready", "bonus_ready")
    sg = {n: core.sig("rwkv_" + n) for n in names}
    const_in, stored = core.sig("rwkv_const_in"), core.sig("rwkv_bonus_stored")
    with ExitStack() as inner:
        sb, ps = tiles(core, inner)
        sel = sb("sel", [P, KC, NH])
        selT = sb("selT", [NH, KC, P])
        blk = sb("blk", [P, P])
        reset = sb("reset", [P, SEQ])
        bonus = sb("bonus", [P, KC, T])
        sq = [sb(f"sq{u}", [P, T]) for u in range(2)]
        cs = [sb(f"cs{u}", [P, SEQ]) for u in range(2)]
        dcs = [sb(f"dcs{u}", [P, SEQ]) for u in range(2)]
        W, Wp, iW = ([sb(f"{n}{u}", [P, SEQ]) for u in range(2)] for n in ("W", "Wp", "iW"))
        tmp = sb("tmp", [P, T])
        rk = [sb(f"rk{u}", [P, T]) for u in range(2)]
        inv = sb("inv", [NH, T])
        nsum = ps("nsum", [NH, 2, 512])
        bc = ps("bc", [P, 2, 512])
        dot = [ps(f"dot{u}", [P, 2, 512]) for u in range(2)]
        block = inner.enter_context(nc.Block())

        @block.sync
        def _(sync):
            sync.dma_start(sel[:], io["c_sel"]).then_inc(const_in.sem, 16)
            sync.dma_start(selT[:], io["c_selT"]).then_inc(const_in.sem, 16)
            sync.dma_start(blk[:], io["c_blk"]).then_inc(const_in.sem, 16)
            sync.dma_start(reset[:], io["c_reset"]).then_inc(const_in.sem, 16)
            sync.wait_ge(sg["bonus_ready"].sem, sg["bonus_ready"].at(KC))
            sync.dma_start(io["s_bonus"], bonus[:]).then_inc(stored.sem, 16)
            sync.wait_ge(stored.sem, stored.at(16))

        @block.tensor
        def _(pe):
            pe.wait_ge(const_in.sem, const_in.at(64))
            for c in range(KC):
                pe.wait_ge(sg["kksq_ready"].sem, sg["kksq_ready"].at(c + 1))
                for half in range(2):
                    mm = pe.matmul(nsum[:, half, 0:HALF], sel[:, c, :], sq[c % 2][:, half * HALF:(half + 1) * HALF],
                                   start=(c == 0), stop=(c == KC - 1))
                mm.then_inc(sg["nsum_ready"].sem, 1)
            pe.wait_ge(sg["inv_ready"].sem, sg["inv_ready"].at(1))
            for c in range(KC):
                if c:
                    pe.wait_ge(sg["kkn_ready"].sem, sg["kkn_ready"].at(c))
                for half in range(2):
                    mm = pe.matmul(bc[:, half, 0:HALF], selT[:, c, :], inv[:, half * HALF:(half + 1) * HALF],
                                   start=True, stop=True)
                mm.then_inc(sg["bc_ready"].sem, 1)
            for c in range(KC):
                pe.wait_ge(sg["rk_ready"].sem, sg["rk_ready"].at(c + 1))
                if c >= 2:
                    pe.wait_ge(sg["bonus_ready"].sem, sg["bonus_ready"].at(c - 1))
                for half in range(2):
                    mm = pe.matmul(dot[c % 2][:, half, 0:HALF], blk[:, :], rk[c % 2][:, half * HALF:(half + 1) * HALF],
                                   start=True, stop=True)
                mm.then_inc(sg["dot_ready"].sem, 1)

        @block.scalar
        def _(act):
            for c in range(KC):
                act.wait_ge(sg["kk_ready"].sem, sg["kk_ready"].at(c + 1))
                if c >= 2:
                    act.wait_ge(sg["nsum_ready"].sem, sg["nsum_ready"].at(c - 1))
                act.activation(sq[c % 2][:, :], kk[:, c, :], ACT.Square).then_inc(sg["kksq_ready"].sem, 1)
            act.wait_ge(sg["nsum_ready"].sem, sg["nsum_ready"].at(KC))
            act.activation(halves(inv[:, :]), nsum[:, :, 0:HALF], ACT.Sqrt).then_inc(sg["norm_ready"].sem, 1)
            for c in range(KC):
                u = c % 2
                act.wait_ge(sg["cs_ready"].sem, sg["cs_ready"].at(c + 1))
                act.wait_ge(sg["dcs_ready"].sem, sg["dcs_ready"].at(c + 1))
                if c >= 2:
                    act.wait_ge(sg["exp_used"].sem, sg["exp_used"].at(c - 1))
                act.activation(W[u][:, :], cs[u][:, :], ACT.Exp, scale=-DECAY)
                act.activation(iW[u][:, :], cs[u][:, :], ACT.Exp, scale=DECAY)
                act.activation(Wp[u][:, :], dcs[u][:, :], ACT.Exp, scale=-DECAY)
                act.activation(s[:, c, SEQ:T], s[:, c, SEQ:T], ACT.Exp, scale=-DECAY).then_inc(sg["exp_ready"].sem, 1)

        @block.vector
        def _(dve):
            chain = Chain(core, dve, "dve_chain")
            for c in range(KC):
                dve.tensor_scalar(kk[:, c, :], k[:, c, :], par[:, MIX.index("k_k"), c:c + 1], None, ALU.mult
                                  ).then_inc(sg["kk_ready"].sem, 1)
            dve.wait_ge(sg["norm_ready"].sem, sg["norm_ready"].at(1))
            chain.link(dve.tensor_scalar(inv[:, :], inv[:, :], 1e-12, None, ALU.max))
            dve.reciprocal(inv[:, :], inv[:, :]).then_inc(sg["inv_ready"].sem, 1)
            for c in range(KC):
                dve.wait_ge(sg["bc_ready"].sem, sg["bc_ready"].at(c + 1))
                dve.wait_ge(sg["kksq_ready"].sem, sg["kksq_ready"].at(c + 1))
                dve.tensor_tensor(halves(kk[:, c, :]), halves(kk[:, c, :]), bc[:, :, 0:HALF], ALU.mult
                                  ).then_inc(sg["kkn_ready"].sem, 1)
            dve.wait_ge(sg["kkn_ready"].sem, sg["kkn_ready"].at(KC))
            dve.wait_ge(const_in.sem, const_in.at(64))

            def sums(c):
                if c >= 2:
                    dve.wait_ge(sg["exp_ready"].sem, sg["exp_ready"].at(c - 1))
                dve.tensor_tensor_scan(out=cs[c % 2][:, :], data0=reset[:, :], data1=s[:, c, 0:SEQ], initial=0.0,
                                       op0=ALU.mult, op1=ALU.add).then_inc(sg["cs_ready"].sem, 1)
                dve.wait_ge(sg["cs_ready"].sem, sg["cs_ready"].at(c + 1))
                dve.tensor_tensor(dcs[c % 2][:, :], cs[c % 2][:, :], s[:, c, 0:SEQ], ALU.subtract
                                  ).then_inc(sg["dcs_ready"].sem, 1)

            def bonuses(c):
                dve.wait_ge(sg["dot_ready"].sem, sg["dot_ready"].at(c + 1))
                dve.tensor_tensor(halves(bonus[:, c, :]), dot[c % 2][:, :, 0:HALF], halves(v[:, c, :]), ALU.mult
                                  ).then_inc(sg["bonus_ready"].sem, 1)

            sums(0)
            for c in range(KC):
                u = c % 2
                if c + 1 < KC:
                    sums(c + 1)
                chain.link(dve.tensor_scalar(tmp[:, :], a[:, c, :], 1.0, par[:, MIX.index("k_a"), c:c + 1],
                                             ALU.subtract, ALU.mult))
                chain.link(dve.scalar_tensor_tensor(out=k[:, c, :], in0=tmp[:, :], scalar=1.0, in1=k[:, c, :],
                                                    op0=ALU.add, op1=ALU.mult))
                if c >= 2:
                    dve.wait_ge(sg["dot_ready"].sem, sg["dot_ready"].at(c - 1))
                dve.scalar_tensor_tensor(out=rk[u][:, :], in0=r[:, c, :], scalar=par[:, MIX.index("r_k"), c:c + 1],
                                         in1=k[:, c, :], op0=ALU.mult, op1=ALU.mult).then_inc(sg["rk_ready"].sem, 1)
                chain.link(dve.tensor_tensor(a[:, c, :], a[:, c, :], kk[:, c, :], ALU.mult))
                if c:
                    bonuses(c - 1)
                dve.wait_ge(sg["exp_ready"].sem, sg["exp_ready"].at(c + 1))
                dve.wait_ge(sg["rk_ready"].sem, sg["rk_ready"].at(c + 1))
                chain.link(dve.tensor_copy(wc[:, c, :].rearrange("p (n o) -> p n o", o=1),
                                           W[u][:, :].rearrange("p (n i) -> p n i", i=CH)[:, :, CH - 1:CH]))
                for x, f in ((kk, Wp), (r, W), (a, iW), (k, iW)):
                    ins = dve.tensor_tensor(x[:, c, 0:SEQ], x[:, c, 0:SEQ], f[u][:, :], ALU.mult)
                ins.then_inc(sg["exp_used"].sem, 1)
            bonuses(KC - 1)
            chain.close()

    for n in names:
        sg[n].close({"norm_ready": 1, "inv_ready": 1}.get(n, KC))
    const_in.close(64)
    stored.close(16)
    core.end_stage()


def rwkv_sample(core, stage, r, k, v, s, a):
    nc, io = core.nc, core.io
    tr_ready, tok_ready = core.sig("rws_tr_ready"), core.sig("rws_tok_ready")
    spilled, vec_in, state_in = core.sig("rws_spilled"), core.sig("rws_vec_in"), core.sig("rws_state_in")
    y_ready, y_out, y_in = core.sig("rws_y_ready"), core.sig("rws_y_out"), core.sig("rws_y_in")
    back_ready, s_ready, stored = core.sig("rws_back_ready"), core.sig("rws_s_ready"), core.sig("rws_stored")
    with ExitStack() as inner:
        sb, ps = tiles(core, inner)
        tok = sb("tok", [NB, 6, D])
        vec = sb("vec", [P, 6, HD])
        S = sb("S", [P, HD, HD])
        tmp = sb("tmp", [P, HD, HD])
        sa = sb("sa", [P, HD])
        y = sb("y", [P, HD])
        ytok = sb("ytok", [NB, D])
        pt = [ps(f"pt{i}", [NB, D]) for i in range(3)]
        pb = ps("pb", [P, KC * NB])
        R, W, K, V, KK, B = range(6)
        block = inner.enter_context(nc.Block())

        @block.sync
        def _(sync):
            sync.dma_start(S[:], io["rwkv_state"]).then_inc(state_in.sem, 16)
            for i in range(6):
                sync.wait_ge(tok_ready.sem, tok_ready.at(i + 1))
            sync.dma_start(io["s_vec"], tok[:]).then_inc(spilled.sem, 16)
            sync.wait_ge(spilled.sem, spilled.at(16))
            for b in range(NB):
                sync.dma_start(vec[NH * b:NH * (b + 1)], io["s_vec"][b].rearrange("a (h d) -> h a d", d=HD)
                               ).then_inc(vec_in.sem, 16)
            sync.wait_ge(s_ready.sem, s_ready.at(1))
            sync.dma_start(io["wkv_sample"], S[:]).then_inc(stored.sem, 16)
            sync.wait_ge(y_ready.sem, y_ready.at(1))
            sync.dma_start(io["s_y"].rearrange("b (h d) -> (b h) d", d=HD), y[:]).then_inc(y_out.sem, 16)
            sync.wait_ge(y_out.sem, y_out.at(16))
            sync.dma_start(ytok[:], io["s_y"]).then_inc(y_in.sem, 16)
            sync.wait_ge(stored.sem, stored.at(16))

        @block.tensor
        def _(pe):
            for i, x in enumerate((r, s, k, v, core.hT, a)):
                if i >= 3:
                    pe.wait_ge(tok_ready.sem, tok_ready.at(i - 2))
                for c in range(KC):
                    mm = pe.transpose(pt[i % 3][:, c * P:(c + 1) * P], x[:, c, SEQ:T], core.ident[:, :])
                mm.then_inc(tr_ready.sem, 1)
            pe.wait_ge(y_in.sem, y_in.at(16))
            for c in range(KC):
                mm = pe.transpose(pb[:, c * NB:(c + 1) * NB], ytok[:, c * P:(c + 1) * P], core.ident[0:NB, 0:NB])
            mm.then_inc(back_ready.sem, 1)

        @block.scalar
        def _(act):
            for i in range(6):
                act.wait_ge(tr_ready.sem, tr_ready.at(i + 1))
                act.activation(tok[:, i, :], pt[i % 3][:, :], ACT.Copy).then_inc(tok_ready.sem, 1)

        @block.vector
        def _(dve):
            chain = Chain(core, dve, "dve_chain")

            def row(i):
                return vec[:, i, :].rearrange("p (o j) -> p o j", o=1).broadcast_to([P, HD, HD])

            def column(ap):
                return ap.rearrange("p (i o) -> p i o", o=1).broadcast_to([P, HD, HD])

            dve.wait_ge(state_in.sem, state_in.at(16))
            dve.wait_ge(vec_in.sem, vec_in.at(16 * NB))
            chain.link(dve.tensor_tensor(tmp[:], S[:], row(KK), ALU.mult))
            chain.link(dve.tensor_reduce(sa[:, :], tmp[:], AXX, ALU.add))
            chain.link(dve.tensor_tensor(S[:], S[:], row(W), ALU.mult))
            chain.link(dve.tensor_tensor(tmp[:], column(sa[:, :]), row(B), ALU.mult))
            chain.link(dve.tensor_tensor(S[:], S[:], tmp[:], ALU.subtract))
            chain.link(dve.tensor_tensor(tmp[:], column(vec[:, V, :]), row(K), ALU.mult))
            dve.tensor_tensor(S[:], S[:], tmp[:], ALU.add).then_inc(s_ready.sem, 1)
            dve.wait_ge(s_ready.sem, s_ready.at(1))
            chain.link(dve.tensor_tensor(tmp[:], S[:], row(R), ALU.mult))
            dve.tensor_reduce(y[:, :], tmp[:], AXX, ALU.add).then_inc(y_ready.sem, 1)
            dve.wait_ge(back_ready.sem, back_ready.at(1))
            dve.tensor_copy(r[:, :, SEQ:T], pb[:, :].rearrange("p (k b) -> p k b", b=NB))
            chain.close()

    for s_, n in ((tr_ready, 6), (tok_ready, 6), (spilled, 16), (vec_in, 16 * NB), (state_in, 16), (y_ready, 1),
                  (y_out, 16), (y_in, 16), (back_ready, 1), (s_ready, 1), (stored, 16)):
        s_.close(n)
    core.end_stage()


def rwkv_chunks(core, stage, r, k, v, b, wc):
    nc, io = core.nc, core.io
    kk = core.hT
    const_in = core.sig("rwc_const_in")
    names = ("tok_tr", "tok_done", "gram", "gram_done", "nv", "nv_done", "ltm", "m", "m_done", "d", "d_done",
             "eye_done", "a", "r1_done", "u", "u_done", "x", "x_done", "y", "y_done", "zero", "out_tr", "out_done")
    sg = {n: core.sig("rwc_" + n) for n in names}
    cnt = dict.fromkeys(names, 0)
    stored = core.sig("rwc_stored")
    NL = 4 * LEVELS
    with ExitStack() as inner:
        sb, ps = tiles(core, inner)
        mask = sb("mask", [P, 4, P])
        level = sb("level", [P, LEVELS, P])
        LT, MB, MK = (sb(n, [P, NH, P]) for n in ("LT", "MB", "MK"))
        NTr = [sb(f"NTr{u}", [P, P]) for u in range(2)]
        inv, invT = sb("inv", [P, NH, P]), sb("invT", [P, NH, P])
        Bz, Kz = sb("Bz", [P, 2, D]), sb("Kz", [P, 2, D])
        Vt, NV, R1, U = (sb(n, [P, D]) for n in ("Vt", "NV", "R1", "U"))
        X = [sb(f"X{u}", [P, HP, P]) for u in range(2)]
        Lm = [sb(f"Lm{u}", [P, 4, P]) for u in range(2)]
        Ms = [sb(f"Ms{u}", [P, 4, P]) for u in range(2)]
        bank = ps("bank", [P, 8, 512])
        block = inner.enter_context(nc.Block())

        def at(name, n):
            return sg[name].sem, sg[name].at(n)

        def row_half(q):
            return slice(64 * q, 64 * q + 64)

        @block.sync
        def _(sync):
            sync.dma_start(mask[:], io["c_mask4"]).then_inc(const_in.sem, 16)
            sync.dma_start(level[:], io["c_level"]).then_inc(const_in.sem, 16)
            sync.wait_ge(*at("out_done", 2))
            sync.dma_start(io["wkv_prompt"], R1[:, 0:HP * HD].rearrange("p (h j) -> p h j", j=HD)).then_inc(stored.sem, 16)
            sync.wait_ge(stored.sem, stored.at(16))

        @block.gpsimd
        def _(pool):
            for x in (Bz[:], Kz[:], X[0][:], X[1][:], R1[:], U[:]):
                pool.memset(x, 0.0).then_inc(sg["zero"].sem, 1)
            pool.wait_ge(const_in.sem, const_in.at(32))
            for t in range(NT):
                for n in range(NL):
                    lv, q = n // 4, n % 4
                    if n < 4:
                        pool.wait_ge(*at("gram_done", NH * t + 4 * q + 4))
                    i = NL * t + n
                    if i >= 2:
                        pool.wait_ge(*at("m", i - 1))
                    pool.tensor_tensor(Lm[n % 2][:], LT[:, 4 * q:4 * q + 4, :],
                                       level[:, lv:lv + 1, :].broadcast_to([P, 4, P]), ALU.mult
                                       ).then_inc(sg["ltm"].sem, 1)

        def pe_nv(pe, t, h):
            pe.wait_ge(*at("gram_done", NH * t + h + 1))
            if h == 0:
                pe.wait_ge(*at("tok_done", 5 * t + 5))
            if h == NH // 2:
                pe.wait_ge(*at("nv_done", 2 * t + 1))
            mm = pe.matmul(bank[:, 7, (h % 8) * HD:(h % 8 + 1) * HD], NTr[h % 2][:, :], Vt[:, h * HD:(h + 1) * HD],
                           start=True, stop=True)
            mm.then_inc(sg["nv"].sem, 1)

        @block.tensor
        def _(pe):
            pe.wait_ge(*at("zero", 6))
            for t in range(NT):
                tok = slice(P * t, P * t + P)
                if t:
                    pe.wait_ge(*at("x_done", 4 * t))
                    pe.wait_ge(*at("y_done", 2 * t))
                for i, x in enumerate((b, k, v)):
                    for c in range(KC):
                        mm = pe.transpose(bank[:, 2 * i + c // 4, (c % 4) * P:(c % 4 + 1) * P], x[:, c, tok],
                                          core.ident[:, :])
                    mm.then_inc(sg["tok_tr"].sem, 1)
                for h in range(NH):
                    j = slice(64 * (h % 2), 64 * (h % 2) + 64)
                    bk = h % 6
                    if h < 6:
                        pe.wait_ge(*at("tok_done", 5 * t + (2, 2, 4, 4, 5, 5)[h]))
                    else:
                        pe.wait_ge(*at("gram_done", NH * t + h - 5))
                    for i, (x, y) in enumerate(((b, kk), (b, r), (k, kk), (k, r))):
                        mm = pe.matmul(bank[:, bk, i * P:(i + 1) * P], x[j, h // 2, tok], y[j, h // 2, tok],
                                       start=True, stop=True)
                    mm.then_inc(sg["gram"].sem, 1)
                    if h >= 1:
                        pe_nv(pe, t, h - 1)
                pe_nv(pe, t, NH - 1)
                pe.wait_ge(*at("eye_done", 2 * t + 2))

                def level_m(n):
                    q = n % 4
                    i = NL * t + n
                    pe.wait_ge(*at("ltm", i + 1))
                    if n < 2:
                        pe.wait_ge(*at("gram_done", NH * t + NH))
                    else:
                        pe.wait_ge(*at("m_done", i - 1))
                    if n >= 4:
                        pe.wait_ge(*at("d_done", i - 3))
                    for e in range(4):
                        mm = pe.matmul(bank[:, n % 2, e * P:(e + 1) * P], Lm[n % 2][:, e, :], inv[:, 4 * q + e, :],
                                       start=True, stop=True)
                    mm.then_inc(sg["m"].sem, 1)

                level_m(0)
                for n in range(NL):
                    q = n % 4
                    i = NL * t + n
                    if n + 1 < NL:
                        level_m(n + 1)
                    pe.wait_ge(*at("m_done", i + 1))
                    if n >= 2:
                        pe.wait_ge(*at("d_done", i - 1))
                    for e in range(4):
                        h = 4 * q + e
                        if n // 4 < LEVELS - 1:
                            pe.matmul(bank[:, 2 + n % 2, e * P:(e + 1) * P], invT[:, h, :], Ms[n % 2][:, e, :],
                                      start=True, stop=True)
                        mm = pe.matmul(bank[:, 4 + n % 2, e * P:(e + 1) * P], Ms[n % 2][:, e, :], invT[:, h, :],
                                       start=True, stop=True)
                    mm.then_inc(sg["d"].sem, 1)
                pe.wait_ge(*at("d_done", NL * (t + 1)))
                pe.wait_ge(*at("nv_done", t + 1))
                for half in range(2):
                    c = 2 * t + half
                    Xc = X[c % 2]
                    if c:
                        pe.wait_ge(*at("x_done", 2 * c))
                    for p in range(HP):
                        mm = pe.matmul(bank[:, p // 4, (p % 4) * P:(p % 4 + 1) * P], kk[:, p, tok], Xc[:, p, :],
                                       start=True, stop=True)
                    mm.then_inc(sg["a"].sem, 1)
                    pe.wait_ge(*at("r1_done", c + 1))
                    for h in range(NH):
                        mm = pe.matmul(bank[:, 2 + h // 8, (h % 8) * HD:(h % 8 + 1) * HD], invT[:, h, :],
                                       R1[:, h * HD:(h + 1) * HD], start=True, stop=True)
                    mm.then_inc(sg["u"].sem, 1)
                    pe.wait_ge(*at("u_done", c + 1))
                    for p in range(HP):
                        o = bank[:, 4 + p // 4, (p % 4) * P:(p % 4 + 1) * P]
                        cols = slice(p * P, (p + 1) * P)
                        pe.matmul(o, Kz[:, half, cols], Vt[:, cols], start=True, stop=False)
                        mm = pe.matmul(o, Bz[:, half, cols], U[:, cols], start=False, stop=True)
                    mm.then_inc(sg["x"].sem, 1)
                    if c:
                        pe.wait_ge(*at("y_done", c))
                    ct = slice(CH * c, CH * c + CH)
                    lc = row_half(half)
                    for p in range(HP):
                        o = bank[:, 6, p * CH:(p + 1) * CH]
                        pe.matmul(o, Xc[:, p, :], r[:, p, ct], start=True, stop=False)
                        for e in range(2):
                            h = 2 * p + e
                            oh = bank[64 * e:64 * e + 64, 6, p * CH:(p + 1) * CH]
                            pe.matmul(oh, Vt[:, h * HD:(h + 1) * HD], MK[:, h, lc], start=False, stop=False)
                            mm = pe.matmul(oh, U[:, h * HD:(h + 1) * HD], MB[:, h, lc], start=False, stop=True)
                    mm.then_inc(sg["y"].sem, 1)
            pe.wait_ge(*at("x_done", 2 * NCH))
            for p in range(HP):
                mm = pe.transpose(bank[:, p // 4, (p % 4) * P:(p % 4 + 1) * P], X[NCH % 2][:, p, :], core.ident[:, :])
            mm.then_inc(sg["out_tr"].sem, 1)

        @block.scalar
        def _(act):
            act.wait_ge(*at("zero", 6))
            for t in range(NT):
                for i in range(2):
                    act.wait_ge(*at("tok_tr", 3 * t + i + 1))
                    for half in range(2):
                        rows = row_half(half)
                        act.activation((Bz, Kz)[i][rows, half, :].rearrange("p (a n) -> p a n", a=2),
                                       bank[rows, 2 * i:2 * i + 2, :], ACT.Copy, scale=(-1.0, 1.0)[i]
                                       ).then_inc(sg["tok_done"].sem, 1)
                act.wait_ge(*at("tok_tr", 3 * t + 3))
                act.activation(Vt[:, :].rearrange("p (a n) -> p a n", a=2), bank[:, 4:6, :], ACT.Copy
                               ).then_inc(sg["tok_done"].sem, 1)
                for i in range(2):
                    act.wait_ge(*at("nv", NH * t + 8 * (i + 1)))
                    act.activation(NV[:, 512 * i:512 * (i + 1)], bank[:, 7, :], ACT.Copy).then_inc(sg["nv_done"].sem, 1)
                for n in range(NL):
                    i = NL * t + n
                    act.wait_ge(*at("m", i + 1))
                    if i >= 2:
                        act.wait_ge(*at("d", i - 1))
                    act.activation(Ms[n % 2][:], bank[:, n % 2, :].rearrange("p (e n) -> p e n", e=4), ACT.Copy
                                   ).then_inc(sg["m_done"].sem, 1)
                for half in range(2):
                    c = 2 * t + half
                    rows = row_half(half)
                    act.wait_ge(*at("u", c + 1))
                    if c:
                        act.wait_ge(*at("y", c))
                    act.activation(U[rows, :].rearrange("p (a n) -> p a n", a=2), bank[rows, 2:4, :], ACT.Copy
                                   ).then_inc(sg["u_done"].sem, 1)
                    act.wait_ge(*at("y", c + 1))
                    act.activation(r[:, :, CH * c:CH * c + CH], bank[:, 6, :].rearrange("p (h t) -> p h t", t=CH), ACT.Copy
                                   ).then_inc(sg["y_done"].sem, 1)

        @block.vector
        def _(dve):
            chain = Chain(core, dve, "dve_chain")
            dve.wait_ge(const_in.sem, const_in.at(32))
            dve.wait_ge(*at("zero", 6))
            for t in range(NT):
                for x in (inv, invT):
                    if t:
                        dve.wait_ge(*at("y", 2 * t))
                    dve.tensor_copy(x[:], core.ident[:, :].rearrange("p (o n) -> p o n", o=1).broadcast_to([P, NH, P])
                                    ).then_inc(sg["eye_done"].sem, 1)
                for h in range(NH):
                    bk = h % 6
                    dve.wait_ge(*at("gram", NH * t + h + 1))
                    if h >= 2:
                        dve.wait_ge(*at("nv", NH * t + h - 1))
                    elif t:
                        dve.wait_ge(*at("nv", NH * t))
                    for i, o in enumerate((LT[:, h, :], MB[:, h, :], NTr[h % 2][:, :], MK[:, h, :])):
                        ins = dve.tensor_tensor(o, bank[:, bk, i * P:(i + 1) * P], mask[:, i, :], ALU.mult)
                    ins.then_inc(sg["gram_done"].sem, 1)
                dve.wait_ge(*at("eye_done", 2 * t + 2))
                for n in range(NL):
                    q = n % 4
                    i = NL * t + n
                    dve.wait_ge(*at("d", i + 1))
                    if n >= 4:
                        dve.wait_ge(*at("d_done", i - 3))
                    hs = slice(4 * q, 4 * q + 4)
                    if n // 4 < LEVELS - 1:
                        dve.tensor_tensor(inv[:, hs, :], inv[:, hs, :],
                                          bank[:, 2 + n % 2, :].rearrange("p (e n) -> p e n", e=4), ALU.subtract)
                    dve.tensor_tensor(invT[:, hs, :], invT[:, hs, :],
                                      bank[:, 4 + n % 2, :].rearrange("p (e n) -> p e n", e=4), ALU.subtract
                                      ).then_inc(sg["d_done"].sem, 1)
                for half in range(2):
                    c = 2 * t + half
                    rows = row_half(half)
                    dve.wait_ge(*at("a", c + 1))
                    dve.wait_ge(*at("nv_done", 2 * t + 2))
                    dve.tensor_tensor(R1[rows, :].rearrange("p (a n) -> p a n", a=2), bank[rows, 0:2, :],
                                      NV[rows, :].rearrange("p (a n) -> p a n", a=2), ALU.add).then_inc(sg["r1_done"].sem, 1)
                    dve.wait_ge(*at("x", c + 1))
                    if c:
                        dve.wait_ge(*at("y", c))
                    for e in range(2):
                        d = slice(64 * e, 64 * e + 64)
                        new = X[(c + 1) % 2][d, :, d]
                        chain.link(dve.tensor_tensor(new, bank[d, 4:6, :].rearrange("p a (h i) -> p (a h) i", i=P)[:, :, d],
                                                     X[c % 2][d, :, d], ALU.add))
                        dve.tensor_tensor(new, new, wc[d, :, c:c + 1].broadcast_to([64, HP, 64]), ALU.mult
                                          ).then_inc(sg["x_done"].sem, 1)
                    dve.wait_ge(*at("x_done", 2 * c + 2))
            dve.wait_ge(*at("out_tr", 1))
            for e in range(2):
                d = slice(64 * e, 64 * e + 64)
                dve.tensor_copy(R1[d, 0:HP * HD].rearrange("p (h i) -> p h i", i=HD),
                                bank[d, 0:2, :].rearrange("p a (h i) -> p (a h) i", i=P)[:, :, d]
                                ).then_inc(sg["out_done"].sem, 1)
            chain.close()

    total = {"tok_tr": 3 * NT, "tok_done": 5 * NT, "gram": NH * NT, "gram_done": NH * NT, "nv": NH * NT,
             "nv_done": 2 * NT, "ltm": NL * NT, "m": NL * NT, "m_done": NL * NT, "d": NL * NT, "d_done": NL * NT,
             "eye_done": 2 * NT, "a": NCH, "r1_done": NCH, "u": NCH, "u_done": NCH, "x": NCH, "x_done": 2 * NCH,
             "y": NCH, "y_done": NCH, "zero": 6, "out_tr": 1, "out_done": 2}
    for n, c in total.items():
        sg[n].close(c)
    const_in.close(32)
    stored.close(16)
    core.end_stage()


def rwkv_finish(core, stage, y, par):
    nc, io = core.nc, core.io
    names = ("mean_ready", "yc_ready", "sq_ready", "var_ready", "std_ready", "inv_ready", "bc_ready", "n_ready",
             "ln_ready", "z_ready")
    sg = {n: core.sig("rwf_" + n) for n in names}
    in_, lin_ready, lin_used = core.sig("rwf_in"), core.sig("lin_ready"), core.sig("lin_used")
    with ExitStack() as inner:
        sb, ps = tiles(core, inner)
        sel = sb("sel", [P, KC, NH])
        selT = sb("selT", [NH, KC, P])
        blk = sb("blk", [P, P])
        g, bonus = sb("g", [P, KC, T]), sb("bonus", [P, KC, T])
        sq = [sb(f"sq{u}", [P, T]) for u in range(2)]
        inv = sb("inv", [NH, T])
        slots = [sb(f"w{u}", [P, KC, P]) for u in range(2)]
        nsum = ps("nsum", [NH, 2, 512])
        acc = [ps(f"acc{u}", [P, 2, 512]) for u in range(2)]
        block = inner.enter_context(nc.Block())

        @block.sync
        def _(sync):
            for d, n in ((sel, "c_sel"), (selT, "c_selT"), (blk, "c_blk"), (g, "s_gate"), (bonus, "s_bonus")):
                sync.dma_start(d[:], io[n]).then_inc(in_.sem, 16)
            linear_sync(core, sync, slots, io["rwkv_wo"], KC, 0)

        def var(pe, c):
            pe.wait_ge(sg["sq_ready"].sem, sg["sq_ready"].at(c + 1))
            for half in range(2):
                mm = pe.matmul(nsum[:, half, 0:HALF], sel[:, c, :], sq[c % 2][:, half * HALF:(half + 1) * HALF],
                               start=(c == 0), stop=(c == KC - 1))
            mm.then_inc(sg["var_ready"].sem, 1)

        @block.tensor
        def _(pe):
            pe.wait_ge(in_.sem, in_.at(80))
            for c in range(KC):
                if c >= 2:
                    pe.wait_ge(sg["yc_ready"].sem, sg["yc_ready"].at(c - 1))
                for half in range(2):
                    mm = pe.matmul(acc[c % 2][:, half, 0:HALF], blk[:, :], y[:, c, half * HALF:(half + 1) * HALF],
                                   start=True, stop=True)
                mm.then_inc(sg["mean_ready"].sem, 1)
                if c:
                    var(pe, c - 1)
            var(pe, KC - 1)
            pe.wait_ge(sg["inv_ready"].sem, sg["inv_ready"].at(1))
            for c in range(KC):
                if c >= 2:
                    pe.wait_ge(sg["n_ready"].sem, sg["n_ready"].at(c - 1))
                for half in range(2):
                    mm = pe.matmul(acc[c % 2][:, half, 0:HALF], selT[:, c, :], inv[:, half * HALF:(half + 1) * HALF],
                                   start=True, stop=True)
                mm.then_inc(sg["bc_ready"].sem, 1)
            pe.wait_ge(sg["z_ready"].sem, sg["z_ready"].at(KC))
            linear_pe(core, pe, slots, y, acc, KC, 0)

        @block.scalar
        def _(act):
            for c in range(KC):
                act.wait_ge(sg["yc_ready"].sem, sg["yc_ready"].at(c + 1))
                if c >= 2:
                    act.wait_ge(sg["var_ready"].sem, sg["var_ready"].at(c - 1))
                act.activation(sq[c % 2][:, :], y[:, c, :], ACT.Square).then_inc(sg["sq_ready"].sem, 1)
            act.wait_ge(sg["var_ready"].sem, sg["var_ready"].at(KC))
            act.activation(halves(inv[:, :]), nsum[:, :, 0:HALF], ACT.Sqrt, bias=core.col("eps_gn")[0:NH],
                           scale=1.0 / HD).then_inc(sg["std_ready"].sem, 1)
            for c in range(KC):
                act.wait_ge(sg["n_ready"].sem, sg["n_ready"].at(c + 1))
                act.activation(y[:, c, :], y[:, c, :], ACT.Identity, bias=par[:, MIX.index("ln_b"), c:c + 1],
                               scale=par[:, MIX.index("ln_w"), c:c + 1]).then_inc(sg["ln_ready"].sem, 1)

        @block.vector
        def _(dve):
            chain = Chain(core, dve, "dve_chain")
            dve.sem_inc(lin_used.sem, 2)
            for c in range(KC):
                dve.wait_ge(sg["mean_ready"].sem, sg["mean_ready"].at(c + 1))
                dve.scalar_tensor_tensor(out=halves(y[:, c, :]), in0=acc[c % 2][:, :, 0:HALF], scalar=-1.0 / HD,
                                         in1=halves(y[:, c, :]), op0=ALU.mult, op1=ALU.add
                                         ).then_inc(sg["yc_ready"].sem, 1)
            dve.wait_ge(sg["std_ready"].sem, sg["std_ready"].at(1))
            dve.reciprocal(inv[:, :], inv[:, :]).then_inc(sg["inv_ready"].sem, 1)
            for c in range(KC):
                dve.wait_ge(sg["bc_ready"].sem, sg["bc_ready"].at(c + 1))
                dve.wait_ge(sg["sq_ready"].sem, sg["sq_ready"].at(c + 1))
                dve.tensor_tensor(halves(y[:, c, :]), halves(y[:, c, :]), acc[c % 2][:, :, 0:HALF], ALU.mult
                                  ).then_inc(sg["n_ready"].sem, 1)
            dve.wait_ge(in_.sem, in_.at(80))
            for c in range(KC):
                dve.wait_ge(sg["ln_ready"].sem, sg["ln_ready"].at(c + 1))
                chain.link(dve.tensor_tensor(y[:, c, :], y[:, c, :], bonus[:, c, :], ALU.add))
                dve.tensor_tensor(y[:, c, :], y[:, c, :], g[:, c, :], ALU.mult).then_inc(sg["z_ready"].sem, 1)
            for c in range(KC):
                dve.wait_ge(lin_ready.sem, lin_ready.at(c + 1))
                xk = halves(core.xT[:, c, :])
                dve.tensor_tensor(xk, xk, acc[c % 2][:, 0:2, 0:HALF], ALU.add).then_inc(lin_used.sem, 1)
            chain.close()

    linear_close(core, KC)
    in_.close(80)
    for n in names:
        sg[n].close({"std_ready": 1, "inv_ready": 1}.get(n, KC))
    core.end_stage()


def rwkv_stage(core, _):
    with ExitStack() as stage:
        sb, _ps = tiles(core, stage)
        par = sb("rwkv_par", [P, len(MIX), KC])
        wc = sb("wc", [P, KC, NCH])
        r, k, v, a = (sb(n, [P, KC, T]) for n in "rkva")
        with ExitStack() as early:
            s = tiles(core, early)[0]("s", [P, KC, T])
            rwkv_project(core, early, r, k, v, s, a, par)
            rwkv_prepare(core, early, r, k, v, s, a, wc, par)
            rwkv_sample(core, early, r, k, v, s, a)
        rwkv_chunks(core, stage, r, k, v, a, wc)
        rwkv_finish(core, stage, r, par)



HG = NH // NG
CMP_LP = 16
SEG = 16
NSEG_P = SEQ // SEG
NC_P = NSEG_P - 1
NSEG_S = PAST // SEG
NC_S = NSEG_S - 1
NSLC = PAST // HD + 1
NSEL = 16
Q_COL, KV_COL, GATE_COL = 0, D, D + 6 * KVW
NWT = 4
NK = NPAGE + NWT
PGC = 2 * NG * 8 * 8
PROJ_W = [512] * 5 + [PROJ - 5 * 512]


def nsa_project(core, j, layer, proj):
    nc, io = core.nc, core.io
    h_ready = core.sig("norm_h_ready")
    w_in = [core.sig(f"nsa_w_in{u}") for u in range(2)]
    ready, done = core.sig("nsa_proj_ready"), core.sig("nsa_proj_done")
    gain = core.gains[:, 2 * layer, :]
    n_out = len(PROJ_W) * (NT + 1)
    with ExitStack() as inner:
        sb, ps = tiles(core, inner)
        sq = sb("sq", [P, KC, T])
        std = sb("std", [P, T])
        slots = [sb(f"w{u}", [P, KC, 512]) for u in range(2)]
        bank = ps("bank", [P, 8, 512])
        block = inner.enter_context(nc.Block())

        @block.sync
        def _(sync):
            for c, w in enumerate(PROJ_W):
                if c >= 2:
                    sync.wait_ge(ready.sem, ready.at((NT + 1) * (c - 1)))
                sync.dma_start(slots[c % 2][:, :, 0:w], io["nsa_w_in"][j, :, :, 512 * c:512 * c + w]
                               ).then_inc(w_in[c % 2].sem, 16)

        @block.tensor
        def _(pe):
            norm_pe(core, pe, sq, bank)
            pe.wait_ge(h_ready.sem, h_ready.at(KC))
            for c, w in enumerate(PROJ_W):
                pe.wait_ge(w_in[c % 2].sem, w_in[c % 2].at(16 * (c // 2 + 1)))
                for t in range(NT + 1):
                    n = (NT + 1) * c + t
                    rows = min(P, T - P * t)
                    if n >= 8:
                        pe.wait_ge(done.sem, done.at(n - 7))
                    for k in range(KC):
                        mm = pe.matmul(bank[0:rows, n % 8, 0:w], core.hT[:, k, P * t:P * t + rows],
                                       slots[c % 2][:, k, 0:w], start=(k == 0), stop=(k == KC - 1))
                    mm.then_inc(ready.sem, 1)

        @block.scalar
        def _(act):
            norm_act(core, act, sq, std, bank)
            for n in range(n_out):
                c, t = n // (NT + 1), n % (NT + 1)
                rows, w = min(P, T - P * t), PROJ_W[c]
                act.wait_ge(ready.sem, ready.at(n + 1))
                func = ACT.Copy if c < 5 else ACT.Sigmoid
                act.activation(proj[0:rows, t, 512 * c:512 * c + w], bank[0:rows, n % 8, 0:w], func).then_inc(done.sem, 1)

        @block.vector
        def _(dve):
            norm_dve(core, dve, std, gain)

    norm_close(core)
    for u in range(2):
        w_in[u].close(16 * len(PROJ_W) // 2)
    ready.close(n_out)
    done.close(n_out)
    core.end_stage()


def nsa_heads(core, j, proj, qnT, qrT, kT, qblk):
    nc, io = core.nc, core.io
    names = ("gain", "sq", "ss", "rt", "kd", "rope", "tr", "tr_done")
    sg = {n: core.sig("nsh_" + n) for n in names}
    in_, stored = core.sig("nsh_in"), core.sig("nsh_stored")
    NTT = NT + 1
    with ExitStack() as inner:
        sb, ps = tiles(core, inner)
        cos, sin = sb("cos", [P, NTT, HD]), sb("sin", [P, NTT, HD])
        gq, gk = sb("gq", [P, HD]), sb("gk", [P, 2, HD])
        sq = [core.hT[:].rearrange("p k t -> p (k t)")[:, 24 * HD * u:24 * HD * (u + 1)].rearrange("p (h d) -> p h d", d=HD)
              for u in range(2)]
        ss = [sb(f"ss{u}", [P, 24]) for u in range(2)]
        qr = [sb(f"qr{u}", [P, NH, HD]) for u in range(2)]
        tmp = sb("tmp", [P, NH, HD])
        tmpk = sb("tmpk", [P, 2, NG, HD])
        kd = [sb(f"kd{u}", [P, 2 * NG, 2, HD]) for u in range(2)]
        qs = sb("qs", [NB, 2, 2, HG, 2, HD])
        bank = ps("bank", [P, 8, 512])
        block = inner.enter_context(nc.Block())

        def rows_of(t):
            return min(P, T - P * t)

        def q_of(t):
            return proj[0:rows_of(t), t, 0:D].rearrange("p (h d) -> p h d", d=HD)

        def k_of(t):
            return proj[0:rows_of(t), t, KV_COL + 2 * KVW:KV_COL + 6 * KVW].rearrange(
                "p (a x) -> p a x", a=2)[:, :, 0:KVW].rearrange("p a (g d) -> p a g d", d=HD)

        @block.sync
        def _(sync):
            sync.dma_start(cos[:], io["c_cos"]).then_inc(in_.sem, 16)
            sync.dma_start(sin[:], io["c_sin"]).then_inc(in_.sem, 16)
            sync.dma_start(gq[:], io["nsa_gq"][j]).then_inc(in_.sem, 16)
            sync.dma_start(gk[:], io["nsa_gk"][j]).then_inc(in_.sem, 16)
            for t in range(NTT):
                n = rows_of(t)
                sync.wait_ge(sg["rope"].sem, sg["rope"].at(2 * t + 2))
                rows, win = ("rows_prompt", "win_prompt") if t < NT else ("rows_sample", "s_wnew")
                at = slice(P * t, P * t + P) if t < NT else slice(0, NB)
                dst = io[rows][j] if t < NT else io[rows][j]
                sync.dma_start(dst[at], proj[0:n, t, KV_COL:KV_COL + 4 * KVW]).then_inc(stored.sem, 16)
                dst = io[win][j] if t < NT else io[win]
                sync.dma_start(dst[at], proj[0:n, t, KV_COL + 4 * KVW:KV_COL + 6 * KVW]).then_inc(stored.sem, 16)
            sync.dma_start(io["win_sample"][j, :, SEQ - 1], proj[0:NB, NT, KV_COL + 4 * KVW:KV_COL + 6 * KVW]
                           ).then_inc(stored.sem, 16)
            sync.dma_start(io["win_sample"][j, :, 0:SEQ - 1], io["cache_win"][j, :, 1:SEQ]).then_inc(stored.sem, 16)
            sync.dma_start(io["s_q"].rearrange("b (h d) -> b h d", d=HD), qr[NT % 2][0:NB]).then_inc(stored.sem, 16)
            sync.dma_start(io["s_g3"], proj[0:NB, NT, GATE_COL:PROJ]).then_inc(stored.sem, 16)
            sync.wait_ge(stored.sem, stored.at(16 * (2 * NTT + 4)))

        @block.tensor
        def _(pe):
            for t in range(NT):
                pe.wait_ge(sg["rope"].sem, sg["rope"].at(2 * t + 2))
                for i in range(3):
                    n = 3 * t + i
                    if n >= 4:
                        pe.wait_ge(sg["tr_done"].sem, sg["tr_done"].at(n - 3))
                    for c in range(8):
                        if i == 0:
                            src = proj[:, t, c * P:(c + 1) * P]
                        elif i == 1:
                            src = qr[t % 2][:, 2 * c:2 * c + 2, :]
                        else:
                            pe.wait_ge(sg["kd"].sem, sg["kd"].at(2 * t + 2))
                            src = kd[t % 2][:, c]
                        mm = pe.transpose(bank[:, 2 * (n % 4) + c // 4, (c % 4) * P:(c % 4 + 1) * P], src,
                                          core.ident[:, :])
                    mm.then_inc(sg["tr"].sem, 1)
            pe.wait_ge(sg["kd"].sem, sg["kd"].at(2 * NT + 4))
            pe.wait_ge(sg["tr_done"].sem, sg["tr_done"].at(3 * NT))
            for i in range(2):
                for c in range(8):
                    gp, n = c // HG, c % HG
                    mm = pe.transpose(bank[:, i, c * NB:(c + 1) * NB], qs[:, i, gp, n], core.ident[0:NB, 0:NB])
                mm.then_inc(sg["tr"].sem, 1)

        def copies(act, t):
            tok = slice(P * t, P * t + P)
            for i, dst in enumerate((qnT[:, :, tok], qrT[:, :, tok], kT[:, :, tok])):
                n = 3 * t + i
                b = 2 * (n % 4)
                act.wait_ge(sg["tr"].sem, sg["tr"].at(n + 1))
                act.activation(dst, bank[:, b:b + 2, :].rearrange("p a (h t) -> p (a h) t", t=P), ACT.Copy
                               ).then_inc(sg["tr_done"].sem, 1)

        @block.scalar
        def _(act):
            def squares(t):
                n = rows_of(t)
                if t >= 2:
                    act.wait_ge(sg["ss"].sem, sg["ss"].at(t - 1))
                act.activation(sq[t % 2][0:n, 0:NH], q_of(t), ACT.Square)
                act.activation(sq[t % 2][0:n, NH:24].rearrange("p (a g) d -> p a g d", a=2), k_of(t), ACT.Square
                               ).then_inc(sg["sq"].sem, 1)

            squares(0)
            for t in range(NTT):
                n = rows_of(t)
                if t + 1 < NTT:
                    squares(t + 1)
                act.wait_ge(sg["ss"].sem, sg["ss"].at(t + 1))
                act.activation(ss[t % 2][0:n, :], ss[t % 2][0:n, :], ACT.Sqrt, bias=core.col("eps_rms")[0:n],
                               scale=1.0 / HD).then_inc(sg["rt"].sem, 1)
                if t >= 1:
                    copies(act, t - 1)
            for i in range(2):
                act.wait_ge(sg["tr"].sem, sg["tr"].at(3 * NT + i + 1))
                for e in range(2):
                    d = slice(64 * e, 64 * e + 64)
                    act.activation(qblk[i][d, :, :, 4 * e:4 * e + 4],
                                   bank[d, i, 0:64].rearrange("p (gp n b) -> p gp b n", gp=2, n=HG), ACT.Copy
                                   ).then_inc(sg["tr_done"].sem, 1)

        @block.gpsimd
        def _(pool):
            for i in range(2):
                pool.memset(qblk[i][:], 0.0).then_inc(sg["gain"].sem, 1)
            for t in range(NT):
                pool.wait_ge(sg["rope"].sem, sg["rope"].at(2 * t + 2))
                if t >= 2:
                    pool.wait_ge(sg["tr"].sem, sg["tr"].at(3 * (t - 1)))
                for a in range(2):
                    pool.tensor_copy(kd[t % 2][:, NG * a:NG * (a + 1)], k_of(t)[:, a].rearrange(
                        "p g (o d) -> p g o d", o=1).broadcast_to([P, NG, 2, HD])).then_inc(sg["kd"].sem, 1)
            pool.wait_ge(sg["rope"].sem, sg["rope"].at(2 * NTT))
            for i, x in enumerate((q_of(NT), qr[NT % 2][0:NB])):
                for gp in range(2):
                    pool.tensor_copy(qs[:, i, gp], x.rearrange("p (gp g n) d -> p gp n g d", gp=2, g=2)[:, gp]
                                     ).then_inc(sg["kd"].sem, 1)

        @block.vector
        def _(dve):
            chain = Chain(core, dve, "dve_chain")
            dve.wait_ge(in_.sem, in_.at(64))
            chain.link(dve.tensor_scalar(gq[:, :], gq[:, :], SCALE, None, ALU.mult))
            dve.wait_ge(sg["gain"].sem, sg["gain"].at(2))
            for t in range(NTT):
                n = rows_of(t)
                q, k = q_of(t), k_of(t)
                s = ss[t % 2][0:n, :]
                dve.wait_ge(sg["sq"].sem, sg["sq"].at(t + 1))
                dve.tensor_reduce(s, sq[t % 2][0:n], AXX, ALU.add).then_inc(sg["ss"].sem, 1)
                dve.wait_ge(sg["rt"].sem, sg["rt"].at(t + 1))
                chain.link(dve.reciprocal(s, s))
                dve.tensor_tensor(q, q, s[:, 0:NH].rearrange("p (h o) -> p h o", o=1).broadcast_to([n, NH, HD]), ALU.mult)
                chain.link(dve.tensor_tensor(k, k, s[:, NH:24].rearrange("p (a g o) -> p a g o", a=2, o=1)
                                             .broadcast_to([n, 2, NG, HD]), ALU.mult))
                dve.tensor_tensor(q, q, gq[0:n, :].rearrange("p (o d) -> p o d", o=1).broadcast_to([n, NH, HD]), ALU.mult)
                chain.link(dve.tensor_tensor(k, k, gk[0:n].rearrange("p a (o d) -> p a o d", o=1)
                                             .broadcast_to([n, 2, NG, HD]), ALU.mult))
                half = HD // 2
                if t >= 2:
                    dve.wait_ge(sg["tr"].sem, sg["tr"].at(3 * (t - 2) + 2))
                out = qr[t % 2][0:n]

                def table(x, lo, hi, heads):
                    return x[0:n, t, lo:hi].rearrange("p (o d) -> p o d", o=1).broadcast_to([n, heads, hi - lo])

                chain.link(dve.tensor_tensor(tmp[0:n, :, 0:half], q[:, :, half:HD], table(sin, 0, half, NH), ALU.mult))
                chain.link(dve.tensor_tensor(tmp[0:n, :, half:HD], q[:, :, 0:half], table(sin, half, HD, NH), ALU.mult))
                chain.link(dve.tensor_tensor(out, q, table(cos, 0, HD, NH), ALU.mult))
                dve.tensor_tensor(out, out, tmp[0:n], ALU.add).then_inc(sg["rope"].sem, 1)
                for a in range(2):
                    ka, ta = k[:, a], tmpk[0:n, a]
                    dve.tensor_tensor(ta[:, :, 0:half], ka[:, :, half:HD], table(sin, 0, half, NG), ALU.mult)
                    chain.link(dve.tensor_tensor(ta[:, :, half:HD], ka[:, :, 0:half], table(sin, half, HD, NG), ALU.mult))
                    chain.link(dve.tensor_tensor(ka, ka, table(cos, 0, HD, NG), ALU.mult))
                chain.link(dve.tensor_tensor(k, k, tmpk[0:n], ALU.add))
                dve.engine_nop().then_inc(sg["rope"].sem, 1)
            chain.close()

    for n, c in zip(names, (2, NTT, NTT, NTT, 2 * NT + 4, 2 * NTT, 3 * NT + 2, 3 * NT + 4)):
        sg[n].close(c)
    in_.close(64)
    stored.close(16 * (2 * NTT + 4))
    core.end_stage()


def nsa_compress_prompt(core, j, w1, w2, bias, g0, kcT, vc):
    nc, io = core.nc, core.io
    names = ("b", "b_done", "tr", "tr_done", "h", "h_done", "o", "v_done", "sq", "ss", "rt", "kn", "t", "t_done")
    sg = {n: core.sig("ncp_" + n) for n in names}
    in_ = core.sig("ncp_in")
    with ExitStack() as inner:
        sb, ps = tiles(core, inner)
        pe_emb = sb("pe_emb", [P, 2, CMP_LP])
        seg = sb("seg", [NSEG_P, 2 * NG, SEG, HD])
        segT = core.hT[:].rearrange("p k t -> p (k t)")[:, 0:16 * NG * NSEG_P].rearrange(
            "p (s g l n) -> p s g l n", s=2, g=NG, l=8)
        hid = sb("hid", [P, 2, NG, NC_P])
        kn, sq = sb("kn", [NC_P, NG, HD]), sb("sq", [NC_P, NG, HD])
        kd = core.hT[:].rearrange("p k t -> p (k t)")[0:NC_P, 2048:2048 + 2 * KVW].rearrange(
            "p (g e d) -> p g e d", g=NG, e=2)
        ss = sb("ss", [NC_P, NG])
        bank = ps("bank", [P, 8, 512])
        block = inner.enter_context(nc.Block())

        def at(n, c):
            return sg[n].sem, sg[n].at(c)

        @block.sync
        def _(sync):
            sync.dma_start(pe_emb[:], io["nsa_pe"][j]).then_inc(in_.sem, 16)
            sync.dma_start(w1[:], io["nsa_w1"][j]).then_inc(in_.sem, 16)
            sync.dma_start(w2[:], io["nsa_w2"][j]).then_inc(in_.sem, 16)
            sync.dma_start(g0[:], io["nsa_g0"][j]).then_inc(in_.sem, 16)
            for g in range(2 * NG):
                sync.dma_start(seg[:, g], io["rows_prompt"][j].rearrange("(n l) c -> n l c", l=SEG)
                               [:, :, g * HD:(g + 1) * HD]).then_inc(in_.sem, 16)

        @block.tensor
        def _(pe):
            pe.wait_ge(in_.sem, in_.at(16 * (4 + 2 * NG)))
            for s in range(2):
                for i in range(CMP_LP):
                    mm = pe.matmul(bank[:, 4, s:s + 1], w1[:, s, i, :], pe_emb[:, s, i:i + 1],
                                   start=(i == 0), stop=(i == CMP_LP - 1))
            mm.then_inc(sg["b"].sem, 1)
            for n in range(64):
                s, g, lp = n // 32, n // 8 % NG, n % 8
                mm = pe.transpose(bank[:, n // 16, (n % 16) * NSEG_P:(n % 16 + 1) * NSEG_P],
                                  seg[:, s * NG + g, 2 * lp:2 * lp + 2, :],
                                  core.ident[0:NSEG_P, 0:NSEG_P])
                if n % 16 == 15:
                    mm.then_inc(sg["tr"].sem, 1)
            pe.wait_ge(*at("tr_done", 4))
            for s in range(2):
                for i in range(CMP_LP):
                    r, lp = i // 8, i % 8
                    mm = pe.matmul(bank[:, 5 + s, 0:NG * NC_P], w1[:, s, i, :], segT[:, s, :, lp, r:r + NC_P],
                                   start=(i == 0), stop=(i == CMP_LP - 1))
                mm.then_inc(sg["h"].sem, 1)
            pe.wait_ge(*at("h_done", 2))
            for s in range(2):
                for g in range(NG):
                    mm = pe.matmul(bank[0:NC_P, 7, (s * NG + g) * HD:(s * NG + g + 1) * HD], hid[:, s, g, :], w2[:, s, :],
                                   start=True, stop=True)
            mm.then_inc(sg["o"].sem, 1)
            pe.wait_ge(*at("kn", 1))
            for g in range(NG):
                mm = pe.transpose(bank[:, 0, g * NC_P:(g + 1) * NC_P],
                                  kd[:, g],
                                  core.ident[0:NC_P, 0:NC_P])
            mm.then_inc(sg["t"].sem, 1)

        @block.scalar
        def _(act):
            act.wait_ge(*at("b", 1))
            act.activation(bias[:, :], bank[:, 4, 0:2], ACT.Copy).then_inc(sg["b_done"].sem, 1)
            for i in range(4):
                act.wait_ge(*at("tr", i + 1))
                act.activation(segT[:, i // 2, 2 * (i % 2):2 * (i % 2) + 2].rearrange("p g l n -> p (g l n)"),
                               bank[:, i, :], ACT.Copy).then_inc(sg["tr_done"].sem, 1)
            act.wait_ge(*at("b_done", 1))
            for s in range(2):
                act.wait_ge(*at("h", s + 1))
                act.activation(hid[:, s].rearrange("p g n -> p (g n)"), bank[:, 5 + s, 0:NG * NC_P], ACT.Silu,
                               bias=bias[:, s:s + 1]).then_inc(sg["h_done"].sem, 1)
            act.wait_ge(*at("o", 1))
            act.activation(vc[:], bank[0:NC_P, 7, 256:512].rearrange("p (g d) -> p g d", d=HD), ACT.Copy
                           ).then_inc(sg["v_done"].sem, 1)
            act.activation(sq[:], bank[0:NC_P, 7, 0:256].rearrange("p (g d) -> p g d", d=HD), ACT.Square
                           ).then_inc(sg["sq"].sem, 1)
            act.wait_ge(*at("ss", 1))
            act.activation(ss[:], ss[:], ACT.Sqrt, bias=core.col("eps_rms")[0:NC_P], scale=1.0 / HD
                           ).then_inc(sg["rt"].sem, 1)
            act.wait_ge(*at("t", 1))
            act.activation(kcT[:].rearrange("p g n -> p (g n)"), bank[:, 0, 0:NG * NC_P], ACT.Copy
                           ).then_inc(sg["t_done"].sem, 1)

        @block.vector
        def _(dve):
            chain = Chain(core, dve, "dve_chain")
            dve.wait_ge(*at("sq", 1))
            dve.tensor_reduce(ss[:], sq[:], AXX, ALU.add).then_inc(sg["ss"].sem, 1)
            dve.wait_ge(*at("rt", 1))
            chain.link(dve.reciprocal(ss[:], ss[:]))
            chain.link(dve.tensor_tensor(kn[:], bank[0:NC_P, 7, 0:256].rearrange("p (g d) -> p g d", d=HD),
                                         ss[:].rearrange("p (g o) -> p g o", o=1).broadcast_to([NC_P, NG, HD]), ALU.mult))
            for e in range(2):
                ins = dve.tensor_tensor(kd[:, :, e, :], kn[:], g0[0:NC_P, :].rearrange("p (o d) -> p o d", o=1)
                                        .broadcast_to([NC_P, NG, HD]), ALU.mult)
            ins.then_inc(sg["kn"].sem, 1)
            chain.close()

    for n, c in {"tr": 4, "tr_done": 4, "h": 2, "h_done": 2}.items():
        sg[n].close(c)
    for n in names:
        if n not in ("tr", "tr_done", "h", "h_done"):
            sg[n].close(1)
    in_.close(16 * (4 + 2 * NG))
    core.end_stage()


def nsa_attend_compressed(core, proj, qnT, kcT, vc, o):
    nc, io = core.nc, core.io
    names = ("s", "smax", "exp", "p", "tr", "tr_done", "o", "o_done")
    sg = {n: core.sig("nac_" + n) for n in names}
    in_ = core.sig("nac_in")
    with ExitStack() as inner:
        sb, ps = tiles(core, inner)
        madd, mone = sb("madd", [P, NT, NC_P]), sb("mone", [P, NT, NC_P])
        S = [sb(f"S{u}", [P, 2, HP, NC_P]) for u in range(2)]
        mx, den = sb("mx", [P, 2, HP]), sb("den", [P, 2, HP])
        pT = sb("pT", [NC_P, NH, P])
        bank = ps("bank", [P, 8, 512])
        block = inner.enter_context(nc.Block())

        def at(n, c):
            return sg[n].sem, sg[n].at(c)

        @block.sync
        def _(sync):
            sync.dma_start(madd[:], io["c_cmp_add"]).then_inc(in_.sem, 16)
            sync.dma_start(mone[:], io["c_cmp_one"]).then_inc(in_.sem, 16)

        @block.tensor
        def _(pe):
            def scores(t):
                if t:
                    pe.wait_ge(*at("smax", t))
                for h in range(NH):
                    d = slice(64 * (h % 2), 64 * (h % 2) + 64)
                    mm = pe.matmul(bank[:, h % 2, (h // 2) * 32:(h // 2) * 32 + NC_P], qnT[d, h // 2, P * t:P * t + P],
                                   kcT[d, h // HG, :], start=True, stop=True)
                mm.then_inc(sg["s"].sem, 1)

            scores(0)
            for t in range(NT):
                if t + 1 < NT:
                    scores(t + 1)
                pe.wait_ge(*at("p", t + 1))
                if t:
                    pe.wait_ge(*at("tr_done", 2 * t))
                for h in range(NH):
                    mm = pe.transpose(bank[0:NC_P, 2 + h // 4, (h % 4) * P:(h % 4 + 1) * P], S[t % 2][:, h % 2, h // 2, :],
                                      core.ident[:, :])
                mm.then_inc(sg["tr"].sem, 1)
                pe.wait_ge(*at("tr_done", 2 * t + 2))
                if t:
                    pe.wait_ge(*at("o_done", t))
                for h in range(NH):
                    mm = pe.matmul(bank[:, 6 + h // 8, (h % 8) * HD:(h % 8 + 1) * HD], pT[:, h, :], vc[:, h // HG, :],
                                   start=True, stop=True)
                mm.then_inc(sg["o"].sem, 1)

        @block.scalar
        def _(act):
            for t in range(NT):
                act.wait_ge(*at("smax", t + 1))
                act.activation(S[t % 2][:], S[t % 2][:], ACT.Exp).then_inc(sg["exp"].sem, 1)
                act.wait_ge(*at("tr", t + 1))
                if t:
                    act.wait_ge(*at("o", t))
                for i in range(2):
                    act.activation(pT[:, 8 * i:8 * i + 8, :], bank[0:NC_P, 2 + 2 * i:4 + 2 * i, :].rearrange(
                        "p a (h t) -> p (a h) t", t=P), ACT.Copy).then_inc(sg["tr_done"].sem, 1)

        @block.vector
        def _(dve):
            chain = Chain(core, dve, "dve_chain")
            dve.wait_ge(in_.sem, in_.at(32))
            for t in range(NT):
                Sf = S[t % 2][:].rearrange("p e h c -> p (e h) c")
                mxf, denf = mx[:].rearrange("p e h -> p (e h)"), den[:].rearrange("p e h -> p (e h)")
                dve.wait_ge(*at("s", t + 1))
                if t >= 2:
                    dve.wait_ge(*at("tr", t - 1))
                for e in range(2):
                    chain.link(dve.tensor_tensor(S[t % 2][:, e], bank[:, e, 0:256].rearrange("p (h c) -> p h c", c=32)
                                                 [:, :, 0:NC_P], madd[:, t:t + 1, :].broadcast_to([P, HP, NC_P]), ALU.add))
                chain.link(dve.tensor_reduce(mxf, Sf, AXX, ALU.max))
                dve.tensor_tensor(Sf, Sf, mxf.rearrange("p (h o) -> p h o", o=1).broadcast_to([P, NH, NC_P]), ALU.subtract
                                  ).then_inc(sg["smax"].sem, 1)
                dve.wait_ge(*at("exp", t + 1))
                chain.link(dve.tensor_tensor(Sf, Sf, mone[:, t:t + 1, :].broadcast_to([P, NH, NC_P]), ALU.mult))
                chain.link(dve.tensor_reduce(denf, Sf, AXX, ALU.add))
                chain.link(dve.tensor_scalar(denf, denf, 0.5, None, ALU.max))
                chain.link(dve.reciprocal(denf, denf))
                dve.tensor_tensor(Sf, Sf, denf.rearrange("p (h o) -> p h o", o=1).broadcast_to([P, NH, NC_P]), ALU.mult
                                  ).then_inc(sg["p"].sem, 1)
                dve.wait_ge(*at("o", t + 1))
                gate = proj[:, t, GATE_COL:PROJ].rearrange("p (h j) -> p h j", j=3)[:, :, 0:1].broadcast_to([P, NH, HD])
                dve.tensor_tensor(o[:, t, :].rearrange("p (h d) -> p h d", d=HD),
                                  bank[:, 6:8, :].rearrange("p a (h d) -> p (a h) d", d=HD), gate, ALU.mult
                                  ).then_inc(sg["o_done"].sem, 1)
            chain.close()

    in_.close(32)
    for n in names:
        sg[n].close(2 * NT if n == "tr_done" else NT)
    core.end_stage()


def nsa_attend_causal(core, proj, qrT, kT, o):
    nc, io = core.nc, core.io
    names = ("s", "mask", "max", "exp", "tr", "pd", "pa", "o", "o_done")
    sg = {n: core.sig("nat_" + n) for n in names}
    in_ = core.sig("nat_in")
    units = [(br, t, h) for br in range(2) for t in range(NT) for h in range(NH)]
    NU = len(units)
    with ExitStack() as inner:
        sb, ps = tiles(core, inner)
        diag = sb("diag", [P, P])
        pr = [sb(f"pr{u}", [P, SEQ]) for u in range(2)]
        prT = [sb(f"prT{u}", [P, NT, P]) for u in range(2)]
        nm = sb("nm", [P, 4])
        den = [sb(f"den{u}", [P, NH]) for u in range(2)]
        coef = sb("coef", [P, NH])
        part = sb("part", [P, NH, HD])
        bs = ps("bs", [P, 2, 512])
        bt = ps("bt", [P, 2, 512])
        bo = ps("bo", [P, 2, 2, 512])
        block = inner.enter_context(nc.Block())

        def at(n, c):
            return sg[n].sem, sg[n].at(c)

        @block.sync
        def _(sync):
            sync.dma_start(diag[:], io["c_causal"]).then_inc(in_.sem, 16)

        @block.tensor
        def _(pe):
            def scores(u):
                br, t, h = units[u]
                if u >= 2:
                    pe.wait_ge(*at("exp", u - 1))
                d = slice(64 * (h % 2), 64 * (h % 2) + 64)
                pe.matmul(bs[:, u % 2, 0:P * (t + 1)], qrT[d, h // 2, P * t:P * t + P],
                          kT[d, br * NG + h // HG, 0:P * (t + 1)], start=True, stop=True).then_inc(sg["s"].sem, 1)

            def values(u):
                br, t, h = units[u]
                pe.wait_ge(*at("pd" if u % 2 == 0 else "pa", u // 2 + 1))
                if h == 0 and u >= 2 * NH:
                    pe.wait_ge(*at("o_done", u // NH - 1))
                at_v = KV_COL + (3 + 2 * br) * KVW + (h // HG) * HD
                for b in range(t + 1):
                    mm = pe.matmul(bo[:, u // NH % 2, h // 8, (h % 8) * HD:(h % 8 + 1) * HD], prT[u % 2][:, b, :],
                                   proj[:, b, at_v:at_v + HD], start=(b == 0), stop=(b == t))
                mm.then_inc(sg["o"].sem, 1)

            scores(0)
            for u in range(NU):
                br, t, h = units[u]
                if u + 1 < NU:
                    scores(u + 1)
                pe.wait_ge(*at("exp", u + 1))
                if u >= 2:
                    pe.wait_ge(*at("pd" if u % 2 == 0 else "pa", u // 2))
                for b in range(t + 1):
                    mm = pe.transpose(bt[:, u % 2, b * P:(b + 1) * P], pr[u % 2][:, b * P:(b + 1) * P], core.ident[:, :])
                mm.then_inc(sg["tr"].sem, 1)
                if u:
                    values(u - 1)
            values(NU - 1)

        @block.scalar
        def _(act):
            def copy_back(u):
                t = units[u][1]
                act.wait_ge(*at("tr", u + 1))
                if u >= 2:
                    act.wait_ge(*at("o", u - 1))
                act.activation(prT[u % 2][:, 0:t + 1, :], bt[:, u % 2, 0:P * (t + 1)].rearrange("p (b q) -> p b q", q=P),
                               ACT.Copy).then_inc(sg["pa"].sem, 1)

            for u in range(NU):
                br, t, h = units[u]
                act.wait_ge(*at("max", u + 1))
                if u >= 2:
                    act.wait_ge(*at("tr", u - 1))
                if h == 0 and u >= 2 * NH:
                    act.wait_ge(*at("o_done", u // NH - 1))
                act.activation(pr[u % 2][:, 0:P * (t + 1)], bs[:, u % 2, 0:P * (t + 1)], ACT.Exp, bias=nm[:, u % 4:u % 4 + 1],
                               accum_out=den[u // NH % 2][:, h:h + 1]).then_inc(sg["exp"].sem, 1)
                if u % 2 == 0 and u:
                    copy_back(u - 1)
            copy_back(NU - 1)

        @block.vector
        def _(dve):
            chain = Chain(core, dve, "dve_chain")
            dve.wait_ge(in_.sem, in_.at(16))

            def finish(n):
                br, t = n // NT, n % NT
                dve.wait_ge(*at("o", NH * (n + 1)))
                chain.link(dve.reciprocal(coef[:, :], den[n % 2][:, :]))
                gate = proj[:, t, GATE_COL:PROJ].rearrange("p (h j) -> p h j", j=3)[:, :, 1 + br:2 + br]
                chain.link(dve.tensor_tensor(coef[:, :].rearrange("p (h o) -> p h o", o=1),
                                             coef[:, :].rearrange("p (h o) -> p h o", o=1), gate, ALU.mult))
                chain.link(dve.tensor_tensor(part[:], bo[:, n % 2].rearrange("p a (h d) -> p (a h) d", d=HD),
                                             coef[:, :].rearrange("p (h o) -> p h o", o=1).broadcast_to([P, NH, HD]),
                                             ALU.mult))
                ot = o[:, t, :].rearrange("p (h d) -> p h d", d=HD)
                dve.tensor_tensor(ot, ot, part[:], ALU.add).then_inc(sg["o_done"].sem, 1)

            def copy_back(u):
                t = units[u][1]
                dve.wait_ge(*at("tr", u + 1))
                if u >= 2:
                    dve.wait_ge(*at("o", u - 1))
                dve.tensor_copy(prT[u % 2][:, 0:t + 1, :], bt[:, u % 2, 0:P * (t + 1)].rearrange("p (b q) -> p b q", q=P)
                                ).then_inc(sg["pd"].sem, 1)

            for u in range(NU):
                br, t, h = units[u]
                dve.wait_ge(*at("s", u + 1))
                block_ = bs[:, u % 2, P * t:P * t + P]
                dve.tensor_tensor(block_, block_, diag[:, :], ALU.add).then_inc(sg["mask"].sem, 1)
                dve.wait_ge(*at("mask", u + 1))
                if u >= 4:
                    dve.wait_ge(*at("exp", u - 3))
                dve.tensor_reduce(nm[:, u % 4:u % 4 + 1], bs[:, u % 2, 0:P * (t + 1)], AXX, ALU.max, negate=True
                                  ).then_inc(sg["max"].sem, 1)
                if u % 2 == 1:
                    copy_back(u - 1)
                if h == 2 and u > NH:
                    finish(u // NH - 1)
            finish(NU // NH - 1)
            chain.close()

    in_.close(16)
    for n in names:
        sg[n].close({"pd": NU // 2, "pa": NU // 2, "o_done": NU // NH}.get(n, NU))
    core.end_stage()


def nsa_sample_scores(core, j, w1, w2, bias, g0, qblk, Sc, vcs, Ssb):
    nc, io = core.nc, core.io
    names = ("h", "h_done", "sc", "sc_done", "o", "v_done", "sq", "ss", "rt", "kn", "t", "t_done", "c", "c_done")
    sg = {n: core.sig("nss_" + n) for n in names}
    pt_in = core.sig("nss_pt_in")
    pg_in = [core.sig(f"nss_pg_in{u}") for u in range(2)]
    kw_in = [core.sig(f"nss_kw_in{u}") for u in range(2)]
    with ExitStack() as inner:
        sb, ps = tiles(core, inner)
        pt = sb("pt", [1, NB * NPAGE], I32)
        pages = [sb(f"pages{u}", [P, NPAGE, PGC + 2 * P]) for u in range(2)]
        kw = [sb(f"kw{u}", [P, 2, NWT, P]) for u in range(2)]
        hid = [sb(f"hid{u}", [P, 2, NG, NC_S]) for u in range(2)]
        kn, sq = sb("kn", [NC_S, NG, HD]), sb("sq", [NC_S, NG, HD])
        ss = sb("ss", [NC_S, NG])
        kcT = sb("kcT", [P, 2, NC_S])
        bh = [ps(f"bh{u}", [P, 512]) for u in range(2)]
        bs, bo, bt, bc = (ps(n, [P, 512]) for n in ("bs", "bo", "bt", "bc"))
        block = inner.enter_context(nc.Block())

        def at(n, c):
            return sg[n].sem, sg[n].at(c)

        @block.sync
        def _(sync):
            sync.dma_start(pt[:], io["page_table"]).then_inc(pt_in.sem, 16)
            sync.wait_ge(pt_in.sem, pt_in.at(16))
            for b in range(NB):
                if b >= 2:
                    sync.wait_ge(*at("h", 4 * (b - 1)))
                    sync.wait_ge(*at("sc", b - 1))
                sync.dma_start(kw[b % 2][:], io["cache_wkT"][j, b]).then_inc(kw_in[b % 2].sem, 16)
                with sync.Fori(0, NPAGE) as p:
                    page = sync.value_load(pt[0:1, bass.ds(p + NPAGE * b, 1)], min_val=0, max_val=io["cache_kT"].shape[1] - 1)
                    sync.dma_start(pages[b % 2][:, bass.ds(p, 1), :],
                                   io["cache_kT"][j, bass.ds(page, 1)].rearrange("o p n -> p o n")
                                   ).then_inc(pg_in[b % 2].sem, 16)

        @block.tensor
        def _(pe):
            def tail(b):
                pe.wait_ge(*at("h_done", 4 * b + 4))
                if b:
                    pe.wait_ge(*at("v_done", b))
                    pe.wait_ge(*at("kn", b))
                for s in range(2):
                    for g in range(NG):
                        mm = pe.matmul(bo[0:NC_S, (s * NG + g) * HD:(s * NG + g + 1) * HD], hid[b % 2][:, s, g, :], w2[:, s, :],
                                       start=True, stop=True)
                mm.then_inc(sg["o"].sem, 1)
                pe.wait_ge(*at("kn", b + 1))
                if b:
                    pe.wait_ge(*at("t_done", b))
                for gp in range(2):
                    mm = pe.transpose(bt[:, gp * NC_S:(gp + 1) * NC_S], kn[:, 2 * gp:2 * gp + 2, :],
                                      core.ident[0:NC_S, 0:NC_S])
                mm.then_inc(sg["t"].sem, 1)
                pe.wait_ge(*at("t_done", b + 1))
                if b:
                    pe.wait_ge(*at("c_done", b))
                for gp in range(2):
                    mm = pe.matmul(bc[0:NC_S, gp * 8:gp * 8 + 8], kcT[:, gp, :], qblk[0][:, gp, b, :], start=True, stop=True)
                mm.then_inc(sg["c"].sem, 1)

            for b in range(NB):
                u = b % 2
                pe.wait_ge(pg_in[u].sem, pg_in[u].at(16 * NPAGE * (b // 2 + 1)))
                for q in range(4):
                    s, gp = q // 2, q % 2
                    n = 4 * b + q
                    if n >= 2:
                        pe.wait_ge(*at("h_done", n - 1))
                    o = bh[n % 2][:, 0:2 * (NSEG_S + 1)].rearrange("p (g c) -> p g c", g=2)
                    x = pages[u][:, :, 0:PGC].rearrange("p pg (s g l n) -> p s g l pg n", s=2, g=NG, l=8)
                    for i in range(CMP_LP):
                        r, lp = i // 8, i % 8
                        mm = pe.matmul(o[:, :, 1 - r:1 - r + NSEG_S].rearrange("p g (pg n) -> p g pg n", n=8),
                                       w1[:, s, i, :], x[:, s, 2 * gp:2 * gp + 2, lp], start=(i == 0),
                                       stop=(i == CMP_LP - 1), skip_group_check=True)
                    mm.then_inc(sg["h"].sem, 1)
                    if q == 2 and b:
                        tail(b - 1)
                pe.wait_ge(kw_in[u].sem, kw_in[u].at(16 * (b // 2 + 1)))
                if b:
                    pe.wait_ge(*at("sc_done", b))
                for p in range(NK):
                    for gp in range(2):
                        k = pages[u][:, p, PGC + gp * P:PGC + (gp + 1) * P] if p < NPAGE else kw[u][:, gp, p - NPAGE, :]
                        mm = pe.matmul(bs[:, p * NH + gp * 8:p * NH + gp * 8 + 8], k, qblk[1][:, gp, b, :],
                                       start=True, stop=True)
                mm.then_inc(sg["sc"].sem, 1)
            tail(NB - 1)

        @block.scalar
        def _(act):
            def tail(b):
                act.wait_ge(*at("o", b + 1))
                if b:
                    act.wait_ge(*at("ss", b))
                act.activation(sq[:], bo[0:NC_S, 0:256].rearrange("p (g d) -> p g d", d=HD), ACT.Square
                               ).then_inc(sg["sq"].sem, 1)
                act.activation(vcs[:, b, :], bo[0:NC_S, 256:512], ACT.Copy).then_inc(sg["v_done"].sem, 1)
                act.wait_ge(*at("ss", b + 1))
                act.activation(ss[:], ss[:], ACT.Sqrt, bias=core.col("eps_rms")[0:NC_S], scale=1.0 / HD
                               ).then_inc(sg["rt"].sem, 1)
                act.wait_ge(*at("t", b + 1))
                act.activation(kcT[:], bt[:, 0:2 * NC_S].rearrange("p (g c) -> p g c", g=2), ACT.Copy
                               ).then_inc(sg["t_done"].sem, 1)
                act.wait_ge(*at("c", b + 1))
                act.activation(Sc[:, b * NH:(b + 1) * NH], bc[0:NC_S, 0:NH], ACT.Copy).then_inc(sg["c_done"].sem, 1)

            for b in range(NB):
                for q in range(4):
                    s, gp = q // 2, q % 2
                    n = 4 * b + q
                    act.wait_ge(*at("h", n + 1))
                    if q == 0 and b >= 2:
                        act.wait_ge(*at("o", b - 1))
                    act.activation(hid[b % 2][:, s, 2 * gp:2 * gp + 2, :],
                                   bh[n % 2][:, 0:2 * (NSEG_S + 1)].rearrange("p (g c) -> p g c", g=2)[:, :, 1:NSEG_S],
                                   ACT.Silu, bias=bias[:, s:s + 1]).then_inc(sg["h_done"].sem, 1)
                    if q == 2 and b:
                        tail(b - 1)
                act.wait_ge(*at("sc", b + 1))
                act.activation(Ssb[:, :, b * NH:(b + 1) * NH], bs[:, 0:NK * NH].rearrange("p (k h) -> p k h", h=NH), ACT.Copy
                               ).then_inc(sg["sc_done"].sem, 1)
            tail(NB - 1)

        @block.vector
        def _(dve):
            chain = Chain(core, dve, "dve_chain")
            for b in range(NB):
                dve.wait_ge(*at("sq", b + 1))
                dve.tensor_reduce(ss[:], sq[:], AXX, ALU.add).then_inc(sg["ss"].sem, 1)
                dve.wait_ge(*at("rt", b + 1))
                chain.link(dve.reciprocal(ss[:], ss[:]))
                if b:
                    dve.wait_ge(*at("t", b))
                chain.link(dve.tensor_tensor(kn[:], bo[0:NC_S, 0:256].rearrange("p (g d) -> p g d", d=HD),
                                             ss[:].rearrange("p (g o) -> p g o", o=1).broadcast_to([NC_S, NG, HD]),
                                             ALU.mult))
                dve.tensor_tensor(kn[:], kn[:], g0[0:NC_S, :].rearrange("p (o d) -> p o d", o=1)
                                  .broadcast_to([NC_S, NG, HD]), ALU.mult).then_inc(sg["kn"].sem, 1)
            chain.close()

    pt_in.close(16)
    for u in range(2):
        pg_in[u].close(16 * NPAGE * NB // 2)
        kw_in[u].close(16 * NB // 2)
    for n in names:
        sg[n].close(4 * NB if n in ("h", "h_done") else NB)
    core.end_stage()


def nsa_sample_attend(core, j, Sc, vcs, Ssb, o):
    nc, io = core.nc, core.io
    names = ("scT", "nmx", "ecmp", "p", "pT", "pT_done", "blk", "blk_done", "grp", "madd", "maddT", "maddT_done", "exp_",
             "masked", "mxT", "diag", "mb", "mb_done", "sub", "e", "enew_in", "enew", "esum", "den", "pv", "pv_done", "oT",
             "out")
    sg = {n: core.sig("nsv_" + n) for n in names}
    in_, loc_in, spilled, back = (core.sig("nsv_" + n + "_dma") for n in ("in", "loc", "spilled", "back"))
    new_in = core.sig("nsv_new_in", pool_dma=True)
    pt_in = core.sig("nsv_pt_in")
    NVS = 3
    v_in = [core.sig(f"nsv_v_in{u}") for u in range(NVS)]
    with ExitStack() as inner:
        sb, ps = tiles(core, inner)
        pt = sb("pt", [1, NB * NPAGE], I32)
        V = [sb(f"V{u}", [P, NK, KVW]) for u in range(NVS)]
        c2s, grp = sb("c2s", [NC_S, NSLC]), sb("grp", [P, P])
        keep, force = sb("keep", [P, NSLC]), sb("force", [P, NSLC])
        before = sb("before", [P, NSLC, NSLC])
        spread = sb("spread", [NSLC, NPAGE, P])
        wmask = sb("wmask", [P, NWT])
        parity = sb("parity", [P, 2])
        q, kn, vn = sb("q", [P, HD]), sb("kn", [P, 2, HD]), sb("vn", [P, 2, HD])
        gate = sb("gate", [P, 3])
        pc, pT = sb("pc", [P, NC_S]), sb("pT", [NC_S, P])
        small = sb("small", [P, 16])
        blk, score = sb("blk", [P, NSLC]), sb("score", [P, NSLC])
        gt, eq = sb("gt", [P, NSLC, NSLC]), sb("eq", [P, NSLC, NSLC])
        madd, maddT = sb("madd", [P, NSLC]), sb("maddT", [NSLC, P])
        mxs, dg, mb, es = sb("mxs", [P, 2, P]), sb("dg", [P, 2, P]), sb("mb", [P, 2, P]), sb("es", [P, 2, P])
        prod = sb("prod", [P, 2, HD])
        osb, ob = sb("osb", [P, 3, P]), sb("ob", [P, 3, HD])
        fin = sb("fin", [P, HD])
        bank = ps("bank", [P, 8, 512])
        block = inner.enter_context(nc.Block())
        NMX, DEN_C, R_C, SN, M, EN, DEN, RD = slice(0, 1), slice(1, 2), slice(2, 3), slice(3, 5), slice(5, 7), slice(7, 9), \
            slice(9, 11), slice(11, 13)

        def at(n, c=1):
            return sg[n].sem, sg[n].at(c)

        consts = ((c2s, "c_c2s"), (grp, "c_grp"), (keep, "c_keep"), (force, "c_force"), (before, "c_before"),
                  (spread, "c_spread"), (wmask, "c_wmask"), (parity, "c_parity"))

        @block.sync
        def _(sync):
            sync.dma_start(pt[:], io["page_table"]).then_inc(pt_in.sem, 16)
            sync.wait_ge(pt_in.sem, pt_in.at(16))
            for b in range(NB):
                u = b % NVS
                if b >= NVS:
                    sync.wait_ge(*at("pv", b - NVS + 1))
                sync.dma_start(V[u][:, NPAGE:NK, :], io["cache_wv"][j, b]).then_inc(v_in[u].sem, 16)
                with sync.Fori(0, NPAGE) as p:
                    page = sync.value_load(pt[0:1, bass.ds(p + NPAGE * b, 1)], min_val=0, max_val=io["cache_v"].shape[1] - 1)
                    sync.dma_start(V[u][:, bass.ds(p, 1), :], io["cache_v"][j, bass.ds(page, 1)].rearrange("o p n -> p o n")
                                   ).then_inc(v_in[u].sem, 16)
            sync.wait_ge(*at("out"))
            sync.dma_start(io["s_o"].rearrange("b (h d) -> (b h) d", d=HD), fin[:, :]).then_inc(spilled.sem, 16)
            sync.wait_ge(spilled.sem, spilled.at(16))
            sync.dma_start(o[0:NB, NT, :], io["s_o"]).then_inc(back.sem, 16)
            sync.wait_ge(back.sem, back.at(16))

        @block.scalar
        def _(act):
            for d, n in consts:
                act.dma_start(d[:], io[n]).then_inc(in_.sem, 16)
            act.dma_start(q[:, :], io["s_q"].rearrange("b (h d) -> (b h) d", d=HD)).then_inc(loc_in.sem, 16)
            act.dma_start(gate[:, :], io["s_g3"].rearrange("b (h g) -> (b h) g", g=3)).then_inc(loc_in.sem, 16)
            act.wait_ge(*at("nmx"))
            act.activation(pc[:, :], bank[:, 0, 0:NC_S], ACT.Exp, bias=small[:, NMX], accum_out=small[:, DEN_C]
                           ).then_inc(sg["ecmp"].sem, 1)
            act.wait_ge(*at("pT"))
            act.activation(pT[:, :], bank[0:NC_S, 1, 0:P], ACT.Copy).then_inc(sg["pT_done"].sem, 1)
            act.wait_ge(*at("blk"))
            act.activation(blk[:, :], bank[:, 2, 0:NSLC], ACT.Copy).then_inc(sg["blk_done"].sem, 1)
            act.wait_ge(*at("maddT"))
            act.activation(maddT[:, :], bank[0:NSLC, 0, 0:P], ACT.Copy).then_inc(sg["maddT_done"].sem, 1)
            act.wait_ge(*at("mb"))
            act.activation(mb[:], bank[:, 1, 0:2 * P].rearrange("p (a n) -> p a n", a=2), ACT.Copy
                           ).then_inc(sg["mb_done"].sem, 1)
            act.wait_ge(*at("enew_in"))
            act.activation(small[:, EN], small[:, EN], ACT.Exp).then_inc(sg["enew"].sem, 1)
            act.wait_ge(*at("sub", 2))
            act.activation(Ssb[:], Ssb[:], ACT.Exp).then_inc(sg["e"].sem, 1)
            act.wait_ge(*at("pv", NB + 1))
            act.activation(osb[:], bank[:, 3, 0:3 * P].rearrange("p (a n) -> p a n", a=3), ACT.Copy
                           ).then_inc(sg["pv_done"].sem, 1)

        @block.gpsimd
        def _(pool):
            new = io["rows_sample"][j].rearrange("b (s g d) -> b s g d", s=4, g=NG)
            wnew = io["s_wnew"].rearrange("b (s g d) -> b s g d", s=2, g=NG)
            for b in range(NB):
                rows = slice(NH * b, NH * b + NH)
                for dst, a, src in ((kn, 0, new[b, 2]), (vn, 0, new[b, 3]), (kn, 1, wnew[b, 0]), (vn, 1, wnew[b, 1])):
                    pool.dma_start(dst[rows, a, :], src.rearrange("g (o d) -> g o d", o=1).broadcast_to([NG, HG, HD])
                                   ).then_inc(new_in.sem, 16)

        @block.tensor
        def _(pe):
            pe.transpose(bank[:, 0, 0:NC_S], Sc[:, :], core.ident[0:NC_S, 0:NC_S]).then_inc(sg["scT"].sem, 1)
            pe.wait_ge(*at("p"))
            pe.transpose(bank[0:NC_S, 1, 0:P], pc[:, :], core.ident[:, :]).then_inc(sg["pT"].sem, 1)
            pe.wait_ge(*at("pT_done"))
            pe.wait_ge(in_.sem, in_.at(16 * len(consts)))
            pe.matmul(bank[:, 2, 0:NSLC], pT[:, :], c2s[:, :], start=True, stop=True).then_inc(sg["blk"].sem, 1)
            pe.wait_ge(*at("blk_done"))
            pe.matmul(bank[:, 2, 64:64 + NSLC], grp[:, :], blk[:, :], start=True, stop=True).then_inc(sg["grp"].sem, 1)
            pe.wait_ge(*at("madd"))
            pe.transpose(bank[0:NSLC, 0, 0:P], madd[:, :], core.ident[:, :]).then_inc(sg["maddT"].sem, 1)
            pe.wait_ge(*at("maddT_done"))
            for p in range(NPAGE):
                mm = pe.matmul(bank[:, 4 + p // 4, (p % 4) * P:(p % 4 + 1) * P], spread[:, p, :], maddT[:, :],
                               start=True, stop=True)
            mm.then_inc(sg["exp_"].sem, 1)
            pe.wait_ge(*at("masked"))
            for a in range(2):
                mm = pe.transpose(bank[:, 0, a * P:(a + 1) * P], mxs[:, a, :], core.ident[:, :])
            mm.then_inc(sg["mxT"].sem, 1)
            pe.wait_ge(*at("diag"))
            pe.matmul(bank[:, 1, 0:2 * P], core.ones[:, :], dg[:].rearrange("p a n -> p (a n)"), start=True, stop=True
                      ).then_inc(sg["mb"].sem, 1)
            pe.wait_ge(*at("esum"))
            for a in range(2):
                mm = pe.matmul(bank[:, 2, 128 + a:129 + a], es[:, a, :], core.ones[:, 0:1], start=True, stop=True)
            mm.then_inc(sg["den"].sem, 1)
            for b in range(NB):
                u = b % NVS
                pe.wait_ge(v_in[u].sem, v_in[u].at(16 * (NPAGE + 1) * (b // NVS + 1)))
                for a, ks in enumerate((range(NPAGE), range(NPAGE, NK))):
                    for gp in range(2):
                        at_ = b * NH + gp * 8
                        for k in ks:
                            mm = pe.matmul(bank[:, 3, a * P + at_:a * P + at_ + 8], V[u][:, k, gp * P:(gp + 1) * P],
                                           Ssb[:, k, at_:at_ + 8], start=(k == ks[0]), stop=(k == ks[-1]))
                mm.then_inc(sg["pv"].sem, 1)
            for b in range(NB):
                for gp in range(2):
                    at_ = b * NH + gp * 8
                    mm = pe.matmul(bank[:, 3, 2 * P + at_:2 * P + at_ + 8], vcs[:, b, gp * P:(gp + 1) * P],
                                   pT[:, at_:at_ + 8], start=True, stop=True)
            mm.then_inc(sg["pv"].sem, 1)
            pe.wait_ge(*at("pv_done"))
            for a in range(3):
                mm = pe.transpose(bank[:, 4, a * P:(a + 1) * P], osb[:, a, :], core.ident[:, :])
            mm.then_inc(sg["oT"].sem, 1)

        @block.vector
        def _(dve):
            chain = Chain(core, dve, "dve_chain")
            link = chain.link
            dve.wait_ge(*at("scT"))
            dve.tensor_reduce(small[:, NMX], bank[:, 0, 0:NC_S], AXX, ALU.max, negate=True).then_inc(sg["nmx"].sem, 1)
            dve.wait_ge(*at("ecmp"))
            link(dve.reciprocal(small[:, R_C], small[:, DEN_C]))
            dve.tensor_scalar(pc[:, :], pc[:, :], small[:, R_C], None, ALU.mult).then_inc(sg["p"].sem, 1)
            dve.wait_ge(in_.sem, in_.at(16 * len(consts)))
            dve.wait_ge(*at("grp"))
            link(dve.tensor_tensor(score[:, :], bank[:, 2, 64:64 + NSLC], keep[:, :], ALU.mult))
            link(dve.tensor_tensor(score[:, :], score[:, :], force[:, :], ALU.add))
            other = score[:, :].rearrange("p (o i) -> p o i", o=1).broadcast_to([P, NSLC, NSLC])
            own = score[:, :].rearrange("p (j o) -> p j o", o=1).broadcast_to([P, NSLC, NSLC])
            dve.tensor_tensor(gt[:], other, own, ALU.is_gt)
            link(dve.tensor_tensor(eq[:], other, own, ALU.is_equal))
            link(dve.tensor_tensor(eq[:], eq[:], before[:], ALU.mult))
            link(dve.tensor_tensor(gt[:], gt[:], eq[:], ALU.add))
            link(dve.tensor_reduce(madd[:, :], gt[:], AXX, ALU.add))
            link(dve.tensor_scalar(madd[:, :], madd[:, :], NSEL - 0.5, None, ALU.is_gt))
            dve.tensor_scalar(madd[:, :], madd[:, :], NEG, None, ALU.mult).then_inc(sg["madd"].sem, 1)
            win = Ssb[:, NPAGE:NK, :]
            link(dve.tensor_tensor(win, win, wmask[:, :].rearrange("p (k o) -> p k o", o=1).broadcast_to([P, NWT, P]),
                                   ALU.add))
            dve.wait_ge(loc_in.sem, loc_in.at(32))
            dve.wait_ge(new_in.sem, new_in.at(16 * 4 * NB))
            link(dve.tensor_tensor(prod[:], kn[:], q[:, :].rearrange("p (o d) -> p o d", o=1).broadcast_to([P, 2, HD]),
                                   ALU.mult))
            link(dve.tensor_reduce(small[:, SN], prod[:], AXX, ALU.add))
            dve.wait_ge(*at("exp_"))
            past = Ssb[:, 0:NPAGE, :]
            link(dve.tensor_tensor(past, past, bank[:, 4:8, :].rearrange("p a (k c) -> p (a k) c", c=P), ALU.add))
            dve.tensor_reduce(mxs[:, 1, :], win.rearrange("p k c -> p c k"), AXX, ALU.max)
            dve.tensor_reduce(mxs[:, 0, :], past.rearrange("p k c -> p c k"), AXX, ALU.max).then_inc(sg["masked"].sem, 1)
            dve.wait_ge(*at("mxT"))
            link(dve.tensor_reduce(small[:, M], bank[:, 0, 0:2 * P].rearrange("p (a n) -> p a n", a=2), AXX, ALU.max))
            link(dve.tensor_tensor(small[:, M], small[:, M], small[:, SN], ALU.max))
            dve.tensor_scalar(dg[:, 0, :], core.ident[:, :], small[:, 5:6], None, ALU.mult)
            link(dve.tensor_scalar(dg[:, 1, :], core.ident[:, :], small[:, 6:7], None, ALU.mult))
            dve.tensor_tensor(small[:, EN], small[:, SN], small[:, M], ALU.subtract).then_inc(sg["enew_in"].sem, 1)
            dve.engine_nop().then_inc(sg["diag"].sem, 1)
            dve.wait_ge(*at("mb_done"))
            for a, (x, nk) in enumerate(((past, NPAGE), (win, NWT))):
                dve.tensor_tensor(x, x, mb[:, a:a + 1, :].broadcast_to([P, nk, P]), ALU.subtract).then_inc(sg["sub"].sem, 1)
            dve.wait_ge(*at("e"))
            for a, x in enumerate((past, win)):
                ins = dve.tensor_reduce(es[:, a, :], x.rearrange("p k c -> p c k"), AXX, ALU.add)
            link(ins)
            dve.engine_nop().then_inc(sg["esum"].sem, 1)
            dve.wait_ge(*at("den"))
            dve.wait_ge(*at("enew"))
            link(dve.tensor_tensor(small[:, DEN], bank[:, 2, 128:130], small[:, EN], ALU.add))
            link(dve.reciprocal(small[:, RD], small[:, DEN]))
            link(dve.tensor_tensor(small[:, RD], small[:, RD], gate[:, 1:3], ALU.mult))
            dve.wait_ge(*at("oT"))
            y = bank[:, 4, 0:3 * P].rearrange("p (a x d) -> p a x d", a=3, x=2)
            link(dve.tensor_scalar(ob[:], y[:, :, 0, :], parity[:, 0:1], None, ALU.mult))
            link(dve.scalar_tensor_tensor(out=ob[:], in0=y[:, :, 1, :], scalar=parity[:, 1:2], in1=ob[:],
                                          op0=ALU.mult, op1=ALU.add))
            for a in range(2):
                link(dve.scalar_tensor_tensor(out=ob[:, a, :], in0=vn[:, a, :], scalar=small[:, 7 + a:8 + a],
                                              in1=ob[:, a, :], op0=ALU.mult, op1=ALU.add))
            link(dve.tensor_scalar(fin[:, :], ob[:, 2, :], gate[:, 0:1], None, ALU.mult))
            link(dve.scalar_tensor_tensor(out=fin[:, :], in0=ob[:, 0, :], scalar=small[:, 11:12], in1=fin[:, :],
                                          op0=ALU.mult, op1=ALU.add))
            dve.scalar_tensor_tensor(out=fin[:, :], in0=ob[:, 1, :], scalar=small[:, 12:13], in1=fin[:, :],
                                     op0=ALU.mult, op1=ALU.add).then_inc(sg["out"].sem, 1)
            chain.close()

    pt_in.close(16)
    in_.close(16 * len(consts))
    loc_in.close(32)
    new_in.close(16 * 4 * NB)
    spilled.close(16)
    back.close(16)
    for u in range(NVS):
        v_in[u].close(16 * (NPAGE + 1) * len(range(u, NB, NVS)))
    for n in names:
        sg[n].close({"sub": 2, "pv": NB + 1}.get(n, 1))
    core.end_stage()


def nsa_out(core, j, o):
    nc, io = core.nc, core.io
    tr, tr_done = core.sig("nso_tr"), core.sig("nso_tr_done")
    lin_ready, lin_used = core.sig("lin_ready"), core.sig("lin_used")
    oT = core.hT
    with ExitStack() as inner:
        sb, ps = tiles(core, inner)
        slots = [sb(f"w{u}", [P, KC, P]) for u in range(2)]
        acc = [ps(f"acc{u}", [P, 4, 512]) for u in range(2)]
        block = inner.enter_context(nc.Block())

        @block.sync
        def _(sync):
            linear_sync(core, sync, slots, io["nsa_wo"][j], KC, 0)

        @block.tensor
        def _(pe):
            for t in range(NT + 1):
                rows = min(P, T - P * t)
                if t >= 4:
                    pe.wait_ge(tr_done.sem, tr_done.at(t - 3))
                for c in range(KC):
                    mm = pe.transpose(acc[t // 2 % 2][:, 2 * (t % 2) + c // 4, (c % 4) * P:(c % 4) * P + rows],
                                      o[0:rows, t, c * P:(c + 1) * P], core.ident[0:rows, 0:rows])
                mm.then_inc(tr.sem, 1)
            pe.wait_ge(tr_done.sem, tr_done.at(NT + 1))
            linear_pe(core, pe, slots, oT, acc, KC, 0)

        @block.scalar
        def _(act):
            for t in range(NT + 1):
                rows = min(P, T - P * t)
                act.wait_ge(tr.sem, tr.at(t + 1))
                src = acc[t // 2 % 2][:, 2 * (t % 2):2 * (t % 2) + 2, :].rearrange("p a (c t) -> p (a c) t", t=P)
                act.activation(oT[:, :, P * t:P * t + rows], src[:, :, 0:rows], ACT.Copy).then_inc(tr_done.sem, 1)

        @block.vector
        def _(dve):
            dve.sem_inc(lin_used.sem, 2)
            for c in range(KC):
                dve.wait_ge(lin_ready.sem, lin_ready.at(c + 1))
                xk = halves(core.xT[:, c, :])
                dve.tensor_tensor(xk, xk, acc[c % 2][:, 0:2, 0:HALF], ALU.add).then_inc(lin_used.sem, 1)

    linear_close(core, KC)
    tr.close(NT + 1)
    tr_done.close(NT + 1)
    core.end_stage()


def nsa_stage(core, layer):
    j = layer // 3
    with ExitStack() as stage:
        sb, _ps = tiles(core, stage)
        o = sb("o", [P, NT + 1, D])
        w1, w2 = sb("cmp_w1", [P, 2, CMP_LP, P]), sb("cmp_w2", [P, 2, HD])
        bias, g0 = sb("cmp_bias", [P, 2]), sb("cmp_gain", [P, HD])
        qblk = [sb(f"qblk{i}", [P, 2, NB, 8]) for i in range(2)]
        with ExitStack() as prompt:
            sbp, _ps = tiles(core, prompt)
            proj = sbp("proj", [P, NT + 1, PROJ])
            nsa_project(core, j, layer, proj)
            qnT, qrT = sbp("qnT", [P, HP, SEQ]), sbp("qrT", [P, HP, SEQ])
            kT = sbp("kT", [P, 2 * NG, SEQ])
            kcT, vc = sbp("kcT", [P, NG, NC_P]), sbp("vc", [NC_P, NG, HD])
            nsa_heads(core, j, proj, qnT, qrT, kT, qblk)
            nsa_compress_prompt(core, j, w1, w2, bias, g0, kcT, vc)
            nsa_attend_compressed(core, proj, qnT, kcT, vc, o)
            nsa_attend_causal(core, proj, qrT, kT, o)
        Sc, vcs = sb("Sc", [NC_S, P]), sb("vcs", [NC_S, NB, KVW])
        Ssb = sb("Ssb", [P, NK, P])
        nsa_sample_scores(core, j, w1, w2, bias, g0, qblk, Sc, vcs, Ssb)
        nsa_sample_attend(core, j, Sc, vcs, Ssb, o)
        nsa_out(core, j, o)


CONST_COLS = ["eps_rms", "eps_ln", "eps_gn", "neg_half_exp", "one", "tiny"]


def begin_stage(core):
    nc, io = core.nc, core.io
    ctx = core.ctx

    def sb(name, shape, dt=F32):
        return ctx.enter_context(nc.sbuf_tensor(name, shape, dt))

    core.xT = sb("xT", [P, KC, T])
    core.hT = sb("hT", [P, KC, T])
    core.gains = sb("gains", [P, 2 * DEPTH, KC])
    core.ones = sb("ones", [P, P])
    core.ident = sb("ident", [P, P])
    core.cols = sb("cols", [P, len(CONST_COLS)])
    core.col = lambda name: core.cols[:, CONST_COLS.index(name):CONST_COLS.index(name) + 1]
    loaded = core.sig("begin_loaded")
    with ExitStack() as stage:
        block = stage.enter_context(nc.Block())

        @block.sync
        def _(sync):
            sync.dma_start(core.xT[:], io["xT"]).then_inc(loaded.sem, 16)
            sync.dma_start(core.gains[:], io["gains"]).then_inc(loaded.sem, 16)
            sync.dma_start(core.ones[:], io["c_ones"]).then_inc(loaded.sem, 16)
            sync.dma_start(core.ident[:], io["c_ident"]).then_inc(loaded.sem, 16)
            sync.dma_start(core.cols[:], io["c_cols"]).then_inc(loaded.sem, 16)
            sync.wait_ge(loaded.sem, loaded.at(80))
    loaded.close(80)
    core.end_stage()


def end_stage(core):
    nc, io = core.nc, core.io
    stored = core.sig("end_stored")
    with ExitStack() as stage:
        block = stage.enter_context(nc.Block())

        @block.sync
        def _(sync):
            sync.dma_start(io["yT"], core.xT[:]).then_inc(stored.sem, 16)
            sync.wait_ge(stored.sem, stored.at(16))
    stored.close(16)
    core.end_stage()


def program(nc, io, plan):
    with ExitStack() as ctx:
        core = Core(nc, ctx, io)
        begin_stage(core)
        for name, arg in plan:
            STAGES[name](core, arg)
        end_stage(core)


STAGES = {"ffn": ffn_stage, "conv": conv_stage, "rwkv": rwkv_stage, "nsa": nsa_stage}
PLAN = [("nsa", 0), ("ffn", 0), ("rwkv", 1), ("ffn", 1), ("conv", 2), ("ffn", 2), ("nsa", 3), ("ffn", 3)]



def chunked(w, k, n):
    K, N = w.shape[-2:]
    lead = w.shape[:-2]
    w = w.reshape(*lead, K // k, k, N // n, n)
    m = len(lead)
    return np.ascontiguousarray(w.transpose(*range(m), m + 2, m + 1, m, m + 3))


def by_lane(v):
    v = v.reshape(*v.shape[:-1], KC, P)
    return np.moveaxis(v, -1, 0)


def layouts(x_prompt, x_sample, norms, ffn_w_gu, ffn_w_down, **rest):
    a = {}
    nsa_layouts(a, **rest)
    conv_layouts(a, **rest)
    rwkv_layouts(a, **rest)
    x = np.concatenate([x_prompt[0], x_sample[:, 0]], 0)
    a["xT"] = x.T.reshape(KC, P, T).transpose(1, 0, 2)
    a["gains"] = norms.reshape(2 * DEPTH, KC, P).transpose(2, 0, 1)
    gu = chunked(ffn_w_gu, P, P)
    a["w_gu"] = np.stack([gu[:, :FC], gu[:, FC:]], 3)
    a["w_down"] = chunked(ffn_w_down, P, P)
    a["c_ones"] = np.ones((P, P), np.float32)
    a["c_ident"] = np.eye(P, dtype=np.float32)
    col = dict(eps_rms=RMS_EPS, eps_ln=LN_EPS, eps_gn=GN_EPS, neg_half_exp=-np.exp(-0.5), one=1.0, tiny=1e-12)
    a["c_cols"] = np.tile(np.array([col[c] for c in CONST_COLS], np.float32), (P, 1))
    return {k: np.ascontiguousarray(v) for k, v in a.items()}


def conv_layouts(a, state_conv, conv_w_pw1, conv_b_pw1, conv_w_dw, conv_b_dw, conv_ln_w, conv_ln_b, conv_w_pw2,
                 conv_b_pw2, **rest):
    w = chunked(conv_w_pw1[0], P, P)
    a["conv_w1"] = np.stack([w[:KC], w[KC:]], 2)
    a["conv_w2"] = chunked(conv_w_pw2[0], P, P)
    a["conv_par"] = by_lane(np.stack([conv_b_pw1[0, :D], conv_b_pw1[0, D:], conv_b_dw[0], conv_ln_w[0], conv_ln_b[0],
                                      conv_b_pw2[0]]))
    a["conv_taps"] = by_lane(conv_w_dw[0]).transpose(0, 2, 1)
    a["conv_hist"] = by_lane(state_conv[0]).transpose(0, 3, 1, 2)


def rwkv_layouts(a, state_rwkv_wkv, state_rwkv_shift, rwkv_mix, rwkv_w_rkv, rwkv_w0, rwkv_w1, rwkv_w2, rwkv_a0, rwkv_a1,
                 rwkv_a2, rwkv_g1, rwkv_g2, rwkv_k_k, rwkv_k_a, rwkv_r_k, rwkv_ln_w, rwkv_ln_b, rwkv_w_out, **rest):
    vectors = dict(k_k=rwkv_k_k[0], k_a=rwkv_k_a[0], r_k=rwkv_r_k[0].reshape(D), ln_w=rwkv_ln_w[0], ln_b=rwkv_ln_b[0],
                   w0=rwkv_w0[0], a0=rwkv_a0[0], **{f"mix{m}": rwkv_mix[0, m] for m in range(6)})
    a["rwkv_par"] = by_lane(np.stack([vectors[n] for n in MIX]))
    a["rwkv_shift"] = by_lane(state_rwkv_shift[0]).transpose(0, 2, 1)
    a["rwkv_rkv"] = chunked(rwkv_w_rkv[0], P, P).reshape(3 * KC, P, KC, P)
    a["rwkv_wo"] = chunked(rwkv_w_out[0], P, P)
    for m, (down, up) in enumerate(((rwkv_w1, rwkv_w2), (rwkv_a1, rwkv_a2), (rwkv_g1, rwkv_g2))):
        a[f"rwkv_down{m}"] = down[0].reshape(KC, P, -1).transpose(1, 0, 2)
        a[f"rwkv_up{m}"] = up[0]
    a["rwkv_state"] = state_rwkv_wkv[0].reshape(NB * NH, HD, HD)
    head = np.arange(P) // HD
    sel = (2 * np.arange(KC)[None, :, None] + head[:, None, None] == np.arange(NH)).astype(np.float32)
    a["c_sel"], a["c_selT"] = sel, sel.transpose(2, 1, 0)
    a["c_blk"] = (head[:, None] == head).astype(np.float32)
    a["c_reset"] = np.tile((np.arange(SEQ) % CH != 0).astype(np.float32), (P, 1))
    s, t = np.arange(P)[:, None], np.arange(P)[None, :]
    same = s // CH == t // CH
    a["c_mask4"] = np.stack([same & (s < t), -1.0 * (same & (s <= t)), same & (s < t), same & (s <= t)],
                            1).astype(np.float32)
    a["c_level"] = np.stack([(s >> l + 1 == t >> l + 1) & ((t >> l) % 2 == 1) & ((s >> l) % 2 == 0)
                             for l in range(LEVELS)], 1).astype(np.float32)


def nsa_layouts(a, cache_nsa, cache_nsa_win, page_table, nsa_w_in, nsa_q_norm, nsa_k_norm, nsa_cmp_pe, nsa_cmp_w1,
                nsa_cmp_w2, nsa_w_out, **rest):
    n, pool = cache_nsa.shape[:2]
    a["page_table"] = page_table.reshape(1, NB * NPAGE)
    c = cache_nsa[:, :, :, 0:2].reshape(n, pool, 8, 8, 2, 2, NG, HD)
    cmp_ = c.transpose(0, 1, 4, 7, 5, 6, 3, 2).reshape(n, pool, P, PGC)
    ks = cache_nsa[:, :, :, 2].reshape(n, pool, P, 2, 2, HD).transpose(0, 1, 4, 5, 3, 2).reshape(n, pool, P, 2 * P)
    a["cache_kT"] = np.concatenate([cmp_, ks], 3)
    a["cache_v"] = cache_nsa[:, :, :, 3].reshape(n, pool, P, KVW)
    w = cache_nsa_win.reshape(n, NB, NWT, P, 2, KVW)
    a["cache_win"] = cache_nsa_win.reshape(n, NB, NWT * P, 2 * KVW)
    a["cache_wkT"] = w[:, :, :, :, 0].reshape(n, NB, NWT, P, 2, P).transpose(0, 1, 5, 4, 2, 3)
    a["cache_wv"] = w[:, :, :, :, 1].transpose(0, 1, 3, 2, 4)
    a["nsa_w_in"] = nsa_w_in.reshape(n, KC, P, PROJ).transpose(0, 2, 1, 3)
    a["nsa_wo"] = chunked(nsa_w_out, P, P)
    a["nsa_gq"] = np.broadcast_to(nsa_q_norm[:, None], (n, P, HD))
    a["nsa_g0"] = np.broadcast_to(nsa_k_norm[:, None, 0], (n, P, HD))
    a["nsa_gk"] = np.broadcast_to(nsa_k_norm[:, None, 1:3], (n, P, 2, HD))
    a["nsa_pe"] = nsa_cmp_pe.reshape(n, 2, CMP_LP, P).transpose(0, 3, 1, 2)
    a["nsa_w1"] = nsa_cmp_w1.reshape(n, 2, CMP_LP, P, P).transpose(0, 3, 1, 2, 4)
    a["nsa_w2"] = nsa_cmp_w2.transpose(0, 2, 1, 3)
    f = np.float32
    half = HD // 2
    inv = f(10000.0) ** (-np.arange(half, dtype=f) / f(half))
    pos = np.concatenate([np.arange(SEQ), np.full(P, PAST)]).astype(f)
    ang = (pos[:, None] * inv).astype(f)
    cos, sin = np.cos(ang).astype(f), np.sin(ang).astype(f)
    a["c_cos"] = np.concatenate([cos, cos], 1).reshape(NT + 1, P, HD).transpose(1, 0, 2)
    a["c_sin"] = np.concatenate([-sin, sin], 1).reshape(NT + 1, P, HD).transpose(1, 0, 2)
    ok = (np.arange(NC_P) * SEG + 2 * SEG - 1)[None, :] <= np.arange(SEQ)[:, None]
    a["c_cmp_one"] = ok.astype(f).reshape(NT, P, NC_P).transpose(1, 0, 2)
    a["c_cmp_add"] = np.where(ok, 0, NEG).astype(f).reshape(NT, P, NC_P).transpose(1, 0, 2)
    i = np.arange(P)
    a["c_causal"] = np.where(i[None, :] <= i[:, None], 0, NEG).astype(f)
    c0, j0 = np.arange(NC_S)[:, None] * SEG, np.arange(NSLC)[None, :] * HD
    a["c_c2s"] = ((c0 < j0 + HD) & (c0 + 2 * SEG > j0)).astype(f)
    a["c_grp"] = (i[:, None] // HG == i[None, :] // HG).astype(f)
    b = np.arange(NSLC)
    forced = (b == 0) | (b == NSLC - 1) | (b == NSLC - 2)
    a["c_keep"] = np.tile(1 - forced.astype(f), (P, 1))
    a["c_force"] = np.tile(np.where(forced, -NEG, 0).astype(f), (P, 1))
    a["c_before"] = np.tile((b[None, :] < b[:, None]).astype(f)[None], (P, 1, 1))
    a["c_spread"] = (b[:, None, None] == 2 * np.arange(NPAGE)[None, :, None] + i[None, None, :] // HD).astype(f)
    wm = np.zeros((P, NWT), f)
    wm[0, 0] = NEG
    a["c_wmask"] = wm
    par = i // HG % 2
    a["c_parity"] = np.stack([par == 0, par == 1], 1).astype(f)


OUTPUTS = {"yT": (P, KC, T), "conv_prompt": (P, KC, HIST), "conv_sample": (P, KC, NB, HIST), "shift_out": (P, KC, NB + 1),
           "wkv_prompt": (P, HP, HD), "wkv_sample": (NB * NH, HD, HD),
           "rows_prompt": (2, SEQ, 4 * KVW), "rows_sample": (2, NB, 4 * KVW), "win_prompt": (2, SEQ, 2 * KVW),
           "win_sample": (2, NB, SEQ, 2 * KVW)}
SCRATCH = {"s_gate": (P, KC, T), "s_bonus": (P, KC, T), "s_vec": (NB, 6, D), "s_y": (NB, D),
           "s_wnew": (NB, 2 * KVW), "s_q": (NB, D), "s_g3": (NB, 3 * NH), "s_o": (NB, D)}


def results(o):

    def tokens(v):
        return v.transpose(2, 1, 0).reshape(v.shape[2], D)

    y, shift = tokens(o["yT"]), tokens(o["shift_out"])
    wkv = o["wkv_prompt"].reshape(2, HD, HP, HD).transpose(2, 0, 1, 3).reshape(1, 1, NH, HD, HD)
    return tuple(np.ascontiguousarray(v) for v in (
        y[None, 0:SEQ], y[SEQ:T, None],
        o["rows_prompt"].reshape(2, 1, SEQ, 4, NG, HD), o["rows_sample"].reshape(2, NB, 1, 4, NG, HD),
        o["win_prompt"].reshape(2, 1, SEQ, 2, NG, HD), o["win_sample"].reshape(2, NB, SEQ, 2, NG, HD),
        wkv, o["wkv_sample"].reshape(1, NB, NH, HD, HD),
        shift[None, 0:1], shift[None, 1:],
        tokens(o["conv_prompt"])[None, None], o["conv_sample"].transpose(2, 3, 1, 0).reshape(1, NB, HIST, D)))


def kernel(**inputs):
    import concourse.bacc as _bacc
    from concourse import mybir as _mybir
    from concourse.bass_utils import run_bass_kernel_spmd as _run

    nc = _bacc.Bacc("TRN2", target_bir_lowering=False, num_devices=1)
    arrays = layouts(**{name: np.asarray(a) for name, a in inputs.items()})
    io = {}
    for name, a in arrays.items():
        io[name] = nc.dram_tensor(f"in_{name}", a.shape, _mybir.dt.from_np(a.dtype), kind="ExternalInput").ap()
    for name, shape in OUTPUTS.items():
        io[name] = nc.dram_tensor(f"out_{name}", shape, F32, kind="ExternalOutput").ap()
    for name, shape in SCRATCH.items():
        io[name] = nc.dram_tensor(name, shape, F32, kind="Internal").ap()
    program(nc, io, PLAN)
    r = _run(nc, [{f"in_{name}": a for name, a in arrays.items()}], core_ids=[0])
    return results({name: r.results[0][f"out_{name}"] for name in OUTPUTS})
```

```python
from contextlib import ExitStack

import concourse.bass as bass
from concourse import mybir
import numpy as np

F32 = mybir.dt.float32
F32R = mybir.dt.float32r
I32 = mybir.dt.int32
ALU = mybir.AluOpType
ACT = mybir.ActivationFunctionType
AXX = mybir.AxisListType.X

P = 128
D = 1024
KC = D // P
SEQ = 512
NB = 8
T = SEQ + NB
HALF = T // 2
DEPTH = 4
D_FF = 2816
FC = D_FF // P
HD = 64
NH = 16
NG = 4
KVW = NG * HD
PROJ = D + 6 * KVW + 3 * NH
PAST = 2048
PAGE = 128
NPAGE = PAST // PAGE
SCALE = HD ** -0.5
RMS_EPS = 1e-6
LN_EPS = 1e-5
GN_EPS = HD * 1e-5
NEG = -1e30


class Signal:

    def __init__(self, sem):
        self.sem = sem
        self.base = 0

    def at(self, n):
        return self.base + n

    def close(self, n):
        self.base += n


class Core:

    def __init__(self, nc, ctx, io):
        self.nc, self.ctx, self.io = nc, ctx, io
        self.signals, self.kept, self.idle = {}, {}, []
        self.uid = 0

    def sig(self, name, pool_dma=False):
        found = self.kept if pool_dma else self.signals
        if name not in found:
            if self.idle and not pool_dma:
                found[name] = self.idle.pop()
            else:
                self.uid += 1
                found[name] = Signal(self.ctx.enter_context(self.nc.semaphore(f"{name}_{self.uid}")))
        return found[name]

    def end_stage(self):
        self.idle += self.signals.values()
        self.signals = {}


class Chain:

    def __init__(self, core, eng, name):
        self.eng, self.done, self.n = eng, core.sig(name), 0

    def link(self, ins):
        self.n += 1
        ins.then_inc(self.done.sem, 1)
        self.eng.wait_ge(self.done.sem, self.done.at(self.n))

    def close(self):
        self.done.close(self.n)


def tiles(core, stage):
    nc = core.nc

    def sb(name, shape, dt=F32):
        core.uid += 1
        return stage.enter_context(nc.sbuf_tensor(f"{name}_{core.uid}", shape, dt))

    def ps(name, shape, dt=F32):
        core.uid += 1
        return stage.enter_context(nc.psum_tensor(f"{name}_{core.uid}", shape, dt))

    return sb, ps



def norm_act(core, act, sq, std, ps, meanwhile=lambda: None):
    sq_ready, sum_ready, std_ready = core.sig("norm_sq_ready"), core.sig("norm_sum_ready"), core.sig("norm_std_ready")
    for k in range(KC):
        act.activation(sq[:, k, :], core.xT[:, k, :], ACT.Square).then_inc(sq_ready.sem, 1)
    meanwhile()
    act.wait_ge(sum_ready.sem, sum_ready.at(1))
    act.activation(std[:, :].rearrange("p (a t) -> p a t", a=2), ps[:, 0:2, 0:HALF], ACT.Sqrt, bias=core.col("eps_rms"),
                   scale=1.0 / D).then_inc(std_ready.sem, 1)


def norm_sum_dve(core, dve, sq):
    sq_ready, add_ready = core.sig("norm_sq_ready"), core.sig("norm_add_ready")
    for k in range(1, KC):
        dve.wait_ge(sq_ready.sem, sq_ready.at(k + 1))
        if k > 1:
            dve.wait_ge(add_ready.sem, add_ready.at(k - 1))
        dve.tensor_tensor(sq[:, 0, :], sq[:, 0, :], sq[:, k, :], ALU.add).then_inc(add_ready.sem, 1)


def norm_pe(core, pe, sq, ps):
    add_ready, sum_ready = core.sig("norm_add_ready"), core.sig("norm_sum_ready")
    pe.wait_ge(add_ready.sem, add_ready.at(KC - 1))
    for a in range(2):
        mm = pe.matmul(ps[:, a, 0:HALF], core.ones[:, :], sq[:, 0, a * HALF:(a + 1) * HALF], start=True, stop=True)
    mm.then_inc(sum_ready.sem, 1)


def norm_dve(core, dve, std, gain):
    std_ready, h_ready = core.sig("norm_std_ready"), core.sig("norm_h_ready")
    dve.wait_ge(std_ready.sem, std_ready.at(1))
    inv_ready = core.sig("norm_inv_ready")
    dve.reciprocal(std[:, :], std[:, :]).then_inc(inv_ready.sem, 1)
    dve.wait_ge(inv_ready.sem, inv_ready.at(1))
    for k in range(KC):
        dve.scalar_tensor_tensor(out=core.hT[:, k, :], in0=core.xT[:, k, :], scalar=gain[:, k:k + 1],
                                 in1=std[:, :], op0=ALU.mult, op1=ALU.mult).then_inc(h_ready.sem, 1)


def norm_close(core):
    for name, n in (("norm_sq_ready", KC), ("norm_add_ready", KC - 1), ("norm_sum_ready", 1), ("norm_std_ready", 1),
                    ("norm_inv_ready", 1), ("norm_h_ready", KC)):
        core.sig(name).close(n)


def norm_split_dve(core, dve, std, gain, tmp, hi, lo):
    std_ready, inv_ready = core.sig("norm_std_ready"), core.sig("norm_inv_ready")
    full_ready, hi_ready, h_ready = core.sig("norm_full_ready"), core.sig("norm_hi_ready"), core.sig("norm_h_ready")
    dve.wait_ge(std_ready.sem, std_ready.at(1))
    dve.reciprocal(std[:, :], std[:, :]).then_inc(inv_ready.sem, 1)
    dve.wait_ge(inv_ready.sem, inv_ready.at(1))
    for k in range(KC + 1):
        if k < KC:
            if k >= 2:
                dve.wait_ge(h_ready.sem, h_ready.at(k - 1))
            dve.scalar_tensor_tensor(out=tmp[k % 2][:, :], in0=core.xT[:, k, :], scalar=gain[:, k:k + 1],
                                     in1=std[:, :], op0=ALU.mult, op1=ALU.mult).then_inc(full_ready.sem, 1)
        if k:
            c = k - 1
            dve.wait_ge(hi_ready.sem, hi_ready.at(c + 1))
            dve.tensor_tensor(lo[:, c, :], tmp[c % 2][:, :], hi[:, c, :].bitcast(F32), ALU.subtract
                              ).then_inc(h_ready.sem, 1)


def norm_split_act(core, act, tmp, hi):
    full_ready, hi_ready = core.sig("norm_full_ready"), core.sig("norm_hi_ready")
    for k in range(KC):
        act.wait_ge(full_ready.sem, full_ready.at(k + 1))
        act.activation(hi[:, k, :], tmp[k % 2][:, :], ACT.Copy).then_inc(hi_ready.sem, 1)


def norm_split_close(core):
    norm_close(core)
    core.sig("norm_full_ready").close(KC)
    core.sig("norm_hi_ready").close(KC)



class SplitWeights:

    def __init__(self, core, sb, name, kn, width=P, raw=None, used=None, per=1):
        self.raw = raw or [sb(f"{name}_raw{u}", [P, kn, width]) for u in range(2)]
        self.hi = [sb(f"{name}_hi{u}", [P, kn, width], F32R) for u in range(2)]
        self.lo = [sb(f"{name}_lo{u}", [P, kn, width], F32R) for u in range(2)]
        self.raw_in = [core.sig(f"{name}_raw_in{u}") for u in range(2)]
        self.hi_ready, self.lo_ready = core.sig(f"{name}_hi_ready"), core.sig(f"{name}_lo_ready")
        self.used, self.per = used or core.sig(f"{name}_used"), per

    def load(self, sync, src, n0, j=0, step=0):
        if n0 >= 2:
            sync.wait_ge(self.lo_ready.sem, self.lo_ready.at(n0 - 1) + j * step)
        sync.dma_start(self.raw[n0 % 2][:, 0:src.shape[1], 0:src.shape[2]], src).then_inc(self.raw_in[n0 % 2].sem, 16)

    def cut_hi(self, act, kn, n0, j=0, step=0, width=P):
        u = n0 % 2
        act.wait_ge(self.raw_in[u].sem, self.raw_in[u].at(16 * (n0 // 2 + 1)) + j * (8 * step))
        if n0 >= 2:
            act.wait_ge(self.used.sem, self.used.at((n0 - 1) * self.per) + j * (step * self.per))
        act.activation(self.hi[u][:, 0:kn, 0:width], self.raw[u][:, 0:kn, 0:width], ACT.Copy).then_inc(self.hi_ready.sem, 1)

    def cut_lo(self, eng, kn, n0, j=0, step=0, width=P):
        u = n0 % 2
        eng.wait_ge(self.hi_ready.sem, self.hi_ready.at(n0 + 1) + j * step)
        eng.tensor_tensor(self.lo[u][:, 0:kn, 0:width], self.raw[u][:, 0:kn, 0:width],
                          self.hi[u][:, 0:kn, 0:width].bitcast(F32), ALU.subtract).then_inc(self.lo_ready.sem, 1)

    def products(self, pe, out, src_hi, src_lo, k0, kn, first, last, n0, j=0, step=0,
                 ready=None):
        u = n0 % 2
        pe.wait_ge(self.lo_ready.sem, self.lo_ready.at(n0 + 1) + j * step)
        for a in range(2):
            cols = slice(a * HALF, (a + 1) * HALF)
            for k in range(kn):
                if ready and a == 0:
                    pe.wait_ge(ready.sem, ready.at(k + 1))
                for i, (w, h) in enumerate(((self.lo, src_hi), (self.hi, src_lo), (self.hi, src_hi))):
                    mm = pe.matmul(out[:, a, 0:HALF], w[u][:, k, :], h[:, k0 + k, cols],
                                   start=(first and k == 0 and i == 0), stop=(last and k == kn - 1 and i == 2))
        mm.then_inc(self.used.sem, 1)
        return mm

    def close(self, n):
        for u in range(2):
            self.raw_in[u].close(16 * ((n + 1 - u) // 2))
        for s in (self.hi_ready, self.lo_ready) + ((self.used,) if self.per == 1 else ()):
            s.close(n)



def ffn_stage(core, layer):
    nc = core.nc
    w_gu, w_down = core.io["w_gu"], core.io["w_down"]
    gain = core.gains[:, 2 * layer + 1, :]
    h_ready = core.sig("norm_h_ready")
    silu_ready, gu_full, gu_hi, gu_done = (core.sig("ffn_" + n) for n in ("silu_ready", "gu_full", "gu_hi", "gu_done"))
    add_done = core.sig("ffn_add_done")
    HC = FC // 2
    UNITS = 2 * FC
    with ExitStack() as stage:
        sb, ps = tiles(core, stage)
        sq = core.hT
        h_hi, h_lo = sb("h_hi", [P, KC, T], F32R), sb("h_lo", [P, KC, T], F32R)
        std = sb("std", [P, T])
        w = SplitWeights(core, sb, "ffn_w", HC)
        gu_r = [sb("gu_hi", [P, FC, T], F32R), sb("gu_lo", [P, FC, T], F32R)]
        silu = [sb(f"silu{u}", [P, T]) for u in range(2)]
        full = [sb(f"full{u}", [P, T]) for u in range(2)]
        acc = [ps(f"acc{u}", [P, 4, 512]) for u in range(2)]
        block = stage.enter_context(nc.Block())

        @block.sync
        def _(sync):
            for m in range(2):
                w.load(sync, w_gu[layer, 0, :, m], m)
            with sync.Fori(0, FC - 1) as j:
                for m in range(2):
                    w.load(sync, w_gu[layer, bass.ds(j + 1, 1), :, m].rearrange("o p k n -> (o p) k n"), 2 + m, j, 2)
            for m in range(2):
                w.load(sync, w_down[layer, 0, :, m * HC:(m + 1) * HC], UNITS + m)
            with sync.Fori(0, KC - 1) as j:
                for m in range(2):
                    w.load(sync, w_down[layer, bass.ds(j + 1, 1), :, m * HC:(m + 1) * HC]
                           .rearrange("o p k n -> (o p) k n"), UNITS + 2 + m, j, 2)

        @block.tensor
        def _(pe):
            norm_pe(core, pe, sq, acc[0])
            with pe.Fori(0, FC // 2) as j:
                for u in range(2):
                    pe.wait_ge(gu_full.sem, gu_full.at(1 + u) + j * 2)
                    for m in range(2):
                        w.products(pe, acc[u][:, 2 * m:2 * m + 2, :], h_hi, h_lo, 0, KC, True, True, 2 * u + m, j, 4,
                                   h_ready if u == m == 0 else None)
            with pe.Fori(0, KC // 2) as j:
                for u in range(2):
                    pe.wait_ge(add_done.sem, add_done.at(1 + u) + j * 2)
                    for m in range(2):
                        pe.wait_ge(gu_done.sem, gu_done.at((m + 1) * HC + 2))
                        w.products(pe, acc[u][:, 0:2, :], gu_r[0], gu_r[1], m * HC, HC, m == 0, m == 1,
                                   UNITS + 2 * u + m, j, 4)

        @block.scalar
        def _(act):
            norm_act(core, act, sq, std, acc[0], lambda: [w.cut_hi(act, KC, m) for m in range(2)])
            norm_split_act(core, act, full, h_hi)

            def silu_step(u, next_kn, n0, j, step):
                w.cut_hi(act, next_kn, n0 + 2, j, step)
                act.wait_ge(gu_full.sem, gu_full.at(n0 // 2 + 1) + j * (step // 2))
                act.activation(halves(silu[u][:, :]), acc[u][:, 0:2, 0:HALF], ACT.Silu).then_inc(silu_ready.sem, 1)
                w.cut_hi(act, next_kn, n0 + 3, j, step)

            with act.Fori(0, FC // 2 - 1) as j:
                for u in range(2):
                    silu_step(u, KC, 2 * u, j, 4)
            for c in (FC - 2, FC - 1):
                silu_step(c % 2, KC if c == FC - 2 else HC, 2 * c, 0, 0)
            with act.Fori(0, KC - 1) as j:
                for m in range(2):
                    w.cut_hi(act, HC, UNITS + 2 + m, j, 2)

        @block.vector
        def _(dve):
            dve.sem_inc(gu_full.sem, 2)
            dve.sem_inc(add_done.sem, 2)
            norm_sum_dve(core, dve, sq)
            for m in range(2):
                w.cut_lo(dve, KC, m)
            norm_split_dve(core, dve, std, gain, full, h_hi, h_lo)

            def gu_step(u, next_kn, n0, j, step):
                c0, sj = n0 // 2, step // 2
                w.cut_lo(dve, next_kn, n0 + 2, j, step)
                dve.wait_ge(silu_ready.sem, silu_ready.at(c0 + 1) + j * sj)
                dve.wait_ge(w.used.sem, w.used.at(n0 + 2) + j * step)
                dve.wait_ge(gu_done.sem, gu_done.at(c0 + 1) + j * sj)
                dve.tensor_tensor(halves(full[u][:, :]), halves(silu[u][:, :]), acc[u][:, 2:4, 0:HALF], ALU.mult
                                  ).then_inc(gu_full.sem, 1)
                w.cut_lo(dve, next_kn, n0 + 3, j, step)

            with dve.Fori(0, FC // 2 - 1) as j:
                for u in range(2):
                    gu_step(u, KC, 2 * u, j, 4)
            for c in (FC - 2, FC - 1):
                gu_step(c % 2, KC if c == FC - 2 else HC, 2 * c, 0, 0)

            def add_step(c0, j, step):
                dve.wait_ge(w.used.sem, w.used.at(UNITS + 2 * c0 + 2) + j * (2 * step))
                xk = core.xT[:, bass.ds(j * step + c0, 1), :].rearrange("p o (a t) -> p (o a) t", a=2) \
                    if step else halves(core.xT[:, c0, :])
                dve.tensor_tensor(xk, xk, acc[c0 % 2][:, 0:2, 0:HALF], ALU.add).then_inc(add_done.sem, 1)

            with dve.Fori(0, KC // 2 - 1) as j:
                for u in range(2):
                    for m in range(2):
                        w.cut_lo(dve, HC, UNITS + 2 + 2 * u + m, j, 4)
                    add_step(u, j, 2)
            for m in range(2):
                w.cut_lo(dve, HC, UNITS + 2 * KC - 2 + m)
            add_step(KC - 2, 0, 0)
            add_step(KC - 1, 0, 0)

        @block.gpsimd
        def _(pool):
            pool.sem_inc(gu_done.sem, 2)
            with pool.Fori(0, FC // 2) as j:
                for u in range(2):
                    pool.wait_ge(gu_full.sem, gu_full.at(3 + u) + j * 2)
                    hi, lo = (g[:, bass.ds(j * 2 + u, 1), :].rearrange("p o t -> p (o t)") for g in gu_r)
                    pool.tensor_copy(hi, full[u][:, :]).then_inc(gu_hi.sem, 1)
                    pool.wait_ge(gu_hi.sem, gu_hi.at(1 + u) + j * 2)
                    pool.tensor_tensor(lo, full[u][:, :], hi.bitcast(F32), ALU.subtract).then_inc(gu_done.sem, 1)

    norm_split_close(core)
    w.close(UNITS + 2 * KC)
    silu_ready.close(FC)
    gu_full.close(FC + 2)
    gu_hi.close(FC)
    gu_done.close(FC + 2)
    add_done.close(KC + 2)
    core.end_stage()



def linear_sync(core, sync, slots, w, n, first):
    ready = core.sig("lin_ready")
    for u in range(2):
        if first:
            sync.wait_ge(ready.sem, ready.at(first - 1 + u))
        sync.dma_start(slots[u][:], w[u]).then_inc(core.sig(f"lin_in{u}").sem, 16)
    if n > 2:
        with sync.Fori(1, n // 2) as j:
            for u in range(2):
                sync.wait_ge(ready.sem, ready.at(first - 1 + u) + j * 2)
                sync.dma_start(slots[u][:], w[bass.ds(j * 2 + u, 1)].rearrange("o p k n -> (o p) k n")
                               ).then_inc(core.sig(f"lin_in{u}").sem, 16)


def linear_pe(core, pe, slots, src, acc, n, first, K=KC):
    ready, used = core.sig("lin_ready"), core.sig("lin_used")
    with pe.Fori(0, n // 2) as j:
        for u in range(2):
            w_in = core.sig(f"lin_in{u}")
            pe.wait_ge(w_in.sem, w_in.at(16 * (first // 2 + 1)) + j * 16)
            pe.wait_ge(used.sem, used.at(first + 1 + u) + j * 2)
            for a in range(2):
                for k in range(K):
                    mm = pe.matmul(acc[u][:, a, 0:HALF], slots[u][:, k, :], src[:, k, a * HALF:(a + 1) * HALF],
                                   start=(k == 0), stop=(k == K - 1))
            mm.then_inc(ready.sem, 1)


def linear_close(core, n):
    for u in range(2):
        core.sig(f"lin_in{u}").close(16 * n // 2)
    core.sig("lin_ready").close(n)
    core.sig("lin_used").close(n + 2)


def split_linear_sync(sync, w, src, n, n0=0):
    for m in range(2):
        w.load(sync, src[m], n0 + m)
    with sync.Fori(0, n // 2 - 1) as j:
        for m in range(2):
            w.load(sync, src[bass.ds(j * 2 + m + 2, 1)].rearrange("o p k n -> (o p) k n"), n0 + m + 2, j, 2)


def split_linear_pe(core, pe, w, hi, lo, acc, n, n0=0):
    used = core.sig("lin_used")
    with pe.Fori(0, n // 2) as j:
        for u in range(2):
            pe.wait_ge(used.sem, used.at(1 + u) + j * 2)
            w.products(pe, acc[u], hi, lo, 0, KC, True, True, n0 + u, j, 2)


def split_linear_dve(core, dve, w, acc, n, n0=0, bias=None):
    used = core.sig("lin_used")
    for c in range(n):
        if c + 2 < n:
            w.cut_lo(dve, KC, n0 + c + 2)
        dve.wait_ge(w.used.sem, w.used.at(n0 + c + 1))
        xk, y = halves(core.xT[:, c, :]), acc[c % 2][:, 0:2, 0:HALF]
        if bias is None:
            ins = dve.tensor_tensor(xk, xk, y, ALU.add)
        else:
            ins = dve.scalar_tensor_tensor(out=xk, in0=y, scalar=bias[:, c:c + 1], in1=xk, op0=ALU.add, op1=ALU.add)
        ins.then_inc(used.sem, 1)


def halves(ap):
    return ap.rearrange("p (a t) -> p a t", a=2)



TAPS = 31
HIST = TAPS - 1
PE_TAP_CHUNKS = 3


def conv_stage(core, _):
    nc, io = core.nc, core.io
    gain = core.gains[:, 4, :]
    h_ready, h_used = core.sig("norm_h_ready"), core.sig("conv_h_used")
    par_in = core.sig("conv_par_in")
    sig_ready, glu_ready = core.sig("conv_sig_ready"), core.sig("conv_glu_ready")
    zero_ready, diag_ready, diag_used = core.sig("conv_zero_ready"), core.sig("conv_diag_ready"), core.sig("conv_diag_used")
    tap_ready = core.sig("conv_tap_ready")
    y_ready, mean_ready, yc_ready, sq_ready = (core.sig("conv_" + n) for n in ("y_ready", "mean_ready", "yc_ready", "sq_ready"))
    var_ready, std_ready, n_ready, z_ready = (core.sig("conv_" + n) for n in ("var_ready", "std_ready", "n_ready", "z_ready"))
    z_full, z_hi = core.sig("conv_z_full"), core.sig("conv_z_hi")
    lin_used = core.sig("lin_used")
    stored, hist_ready = core.sig("conv_stored"), core.sig("conv_hist_ready")
    dve_taps = KC - PE_TAP_CHUNKS
    with ExitStack() as stage:
        sb, ps = tiles(core, stage)
        sq = sb("sq", [P, KC, T])
        std = sb("std", [P, T])
        w = SplitWeights(core, sb, "conv_w", KC)
        h_hi, h_lo = sb("h_hi", [P, KC, T], F32R), sb("h_lo", [P, KC, T], F32R)
        gate = [sb(f"gate{u}", [P, T]) for u in range(2)]
        ext = sb("ext", [P, KC, HIST + T])
        hist = sb("hist", [P, KC, NB, TAPS])
        prod = sb("prod", [P, NB, TAPS])
        newhist = sb("newhist", [P, KC, NB, HIST])
        taps = sb("taps", [P, KC, TAPS])
        par = sb("par", [P, 6, KC])
        diag = [sb(f"diag{u}", [P, P]) for u in range(4)]
        acc = [ps(f"acc{u}", [P, 4, 512]) for u in range(2)]
        y = core.hT
        B_VAL, B_GATE, B_DW, LN_W, LN_B, B_PW2 = range(6)
        block = stage.enter_context(nc.Block())

        @block.sync
        def _(sync):
            sync.dma_start(par[:], io["conv_par"]).then_inc(par_in.sem, 16)
            sync.dma_start(taps[:], io["conv_taps"]).then_inc(par_in.sem, 16)
            sync.dma_start(hist[:, :, :, 0:HIST], io["conv_hist"]).then_inc(par_in.sem, 16)
            for c in range(KC):
                for i in range(2):
                    w.load(sync, io["conv_w1"][c][:, 1 - i], 2 * c + i)
            split_linear_sync(sync, w, io["conv_w2"], KC, 2 * KC)
            sync.wait_ge(glu_ready.sem, glu_ready.at(KC))
            sync.dma_start(io["conv_prompt"], ext[:, :, SEQ:SEQ + HIST]).then_inc(stored.sem, 16)
            sync.wait_ge(hist_ready.sem, hist_ready.at(1))
            sync.dma_start(io["conv_sample"], newhist[:]).then_inc(stored.sem, 16)
            sync.wait_ge(stored.sem, stored.at(32))

        @block.tensor
        def _(pe):
            norm_pe(core, pe, sq, acc[0])
            for c in range(KC):
                if c >= 2:
                    pe.wait_ge(glu_ready.sem, glu_ready.at(c - 1))
                for i in range(2):
                    w.products(pe, acc[c % 2][:, 2 - 2 * i:4 - 2 * i, :], h_hi, h_lo, 0, KC, True, True, 2 * c + i,
                               ready=h_ready if c == i == 0 else None)
            pe.wait_ge(glu_ready.sem, glu_ready.at(KC))
            for n in range(PE_TAP_CHUNKS):
                for i in range(TAPS):
                    m = n * TAPS + i
                    pe.wait_ge(diag_ready.sem, diag_ready.at(m + 1))
                    mm = pe.matmul(acc[0][:, n, :], diag[m % 4][:, :], ext[:, dve_taps + n, i:i + SEQ],
                                   start=(i == 0), stop=(i == TAPS - 1))
                    mm.then_inc(diag_used.sem, 1)
            for k in range(KC):
                pe.wait_ge(y_ready.sem, y_ready.at(k + 1))
                for a in range(2):
                    mm = pe.matmul(acc[1][:, a, 0:HALF], core.ones[:, :], y[:, k, a * HALF:(a + 1) * HALF],
                                   start=(k == 0), stop=(k == KC - 1))
            mm.then_inc(mean_ready.sem, 1)
            for k in range(KC):
                pe.wait_ge(sq_ready.sem, sq_ready.at(k + 1))
                for a in range(2):
                    mm = pe.matmul(acc[1][:, 2 + a, 0:HALF], core.ones[:, :], sq[:, k, a * HALF:(a + 1) * HALF],
                                   start=(k == 0), stop=(k == KC - 1))
            mm.then_inc(var_ready.sem, 1)
            pe.wait_ge(z_ready.sem, z_ready.at(KC))
            split_linear_pe(core, pe, w, h_hi, h_lo, acc, KC, 2 * KC)

        @block.scalar
        def _(act):
            norm_act(core, act, sq, std, acc[0], lambda: [w.cut_hi(act, KC, n) for n in range(2)])
            norm_split_act(core, act, gate, h_hi)
            act.wait_ge(par_in.sem, par_in.at(48))
            for c in range(KC):
                w.cut_hi(act, KC, 2 * c + 2)
                if c >= 2:
                    act.wait_ge(glu_ready.sem, glu_ready.at(c - 1))
                act.activation(halves(gate[c % 2][:, :]), acc[c % 2][:, 2:4, 0:HALF], ACT.Sigmoid,
                               bias=par[:, B_GATE, c:c + 1]).then_inc(sig_ready.sem, 1)
                w.cut_hi(act, KC, 2 * c + 3)
            for m in range(PE_TAP_CHUNKS * TAPS):
                if m >= 4:
                    act.wait_ge(diag_used.sem, diag_used.at(m - 3))
                act.activation(diag[m % 4][:, :], core.ident[:, :], ACT.Copy,
                               scale=taps[:, dve_taps + m // TAPS, m % TAPS:m % TAPS + 1]).then_inc(diag_ready.sem, 1)
            for k in range(KC):
                act.wait_ge(yc_ready.sem, yc_ready.at(k + 1))
                act.activation(sq[:, k, :], y[:, k, :], ACT.Square).then_inc(sq_ready.sem, 1)
            act.wait_ge(var_ready.sem, var_ready.at(1))
            act.activation(halves(std[:, :]), acc[1][:, 2:4, 0:HALF], ACT.Sqrt, bias=core.col("eps_ln"),
                           scale=1.0 / D).then_inc(std_ready.sem, 1)
            for k in range(KC + 1):
                if k < KC:
                    act.wait_ge(n_ready.sem, n_ready.at(k + 1))
                    act.activation(y[:, k, :], y[:, k, :], ACT.Silu, bias=par[:, LN_B, k:k + 1],
                                   scale=par[:, LN_W, k:k + 1]).then_inc(z_full.sem, 1)
                if k:
                    act.wait_ge(z_full.sem, z_full.at(k))
                    act.activation(h_hi[:, k - 1, :], y[:, k - 1, :], ACT.Copy).then_inc(z_hi.sem, 1)
            for c in range(2, KC):
                w.cut_hi(act, KC, 2 * KC + c)

        @block.vector
        def _(dve):
            chain = Chain(core, dve, "dve_chain")
            dve.sem_inc(lin_used.sem, 2)
            norm_sum_dve(core, dve, sq)
            for n in range(2):
                w.cut_lo(dve, KC, n)
            norm_split_dve(core, dve, std, gain, gate, h_hi, h_lo)
            chain.link(dve.memset(ext[:, :, 0:HIST], 0.0))
            dve.wait_ge(par_in.sem, par_in.at(48))
            for c in range(KC):
                w.cut_lo(dve, KC, 2 * c + 2)
                dve.wait_ge(sig_ready.sem, sig_ready.at(c + 1))
                dve.wait_ge(w.used.sem, w.used.at(2 * c + 2))
                dve.scalar_tensor_tensor(out=halves(ext[:, c, HIST:]), in0=acc[c % 2][:, 0:2, 0:HALF],
                                         scalar=par[:, B_VAL, c:c + 1], in1=halves(gate[c % 2][:, :]),
                                         op0=ALU.add, op1=ALU.mult).then_inc(glu_ready.sem, 1)
                w.cut_lo(dve, KC, 2 * c + 3)
            dve.wait_ge(glu_ready.sem, glu_ready.at(KC))
            chain.link(dve.tensor_copy(hist[:, :, :, HIST:TAPS].rearrange("p k b o -> p k (b o)"), ext[:, :, HIST + SEQ:]))
            dve.tensor_copy(newhist[:], hist[:, :, :, 1:TAPS]).then_inc(hist_ready.sem, 1)
            for k in range(KC):
                chain.link(dve.tensor_tensor(prod[:], hist[:, k], taps[:, k, :].rearrange("p (o i) -> p o i", o=1)
                                             .broadcast_to([P, NB, TAPS]), ALU.mult))
                chain.link(dve.tensor_reduce(y[:, k, SEQ:T], prod[:], AXX, ALU.add))
                if k < dve_taps:
                    for i in range(TAPS):
                        e = ext[:, k, i:i + SEQ]
                        if i == 0:
                            ins = dve.tensor_scalar(y[:, k, 0:SEQ], e, taps[:, k, 0:1], None, ALU.mult)
                        else:
                            ins = dve.scalar_tensor_tensor(out=y[:, k, 0:SEQ], in0=e, scalar=taps[:, k, i:i + 1],
                                                           in1=y[:, k, 0:SEQ], op0=ALU.mult, op1=ALU.add)
                        chain.link(ins)
                else:
                    n = k - dve_taps
                    dve.wait_ge(diag_used.sem, diag_used.at((n + 1) * TAPS))
                    chain.link(dve.tensor_copy(y[:, k, 0:SEQ], acc[0][:, n, :]))
                dve.tensor_scalar(y[:, k, :], y[:, k, :], par[:, B_DW, k:k + 1], None, ALU.add).then_inc(y_ready.sem, 1)
            dve.wait_ge(mean_ready.sem, mean_ready.at(1))
            dve.wait_ge(y_ready.sem, y_ready.at(KC))
            for k in range(KC):
                dve.scalar_tensor_tensor(out=halves(y[:, k, :]), in0=acc[1][:, 0:2, 0:HALF], scalar=-1.0 / D,
                                         in1=halves(y[:, k, :]), op0=ALU.mult, op1=ALU.add).then_inc(yc_ready.sem, 1)
            dve.wait_ge(std_ready.sem, std_ready.at(1))
            chain.link(dve.reciprocal(std[:, :], std[:, :]))
            dve.wait_ge(sq_ready.sem, sq_ready.at(KC))
            for k in range(KC):
                dve.tensor_tensor(y[:, k, :], y[:, k, :], std[:, :], ALU.mult).then_inc(n_ready.sem, 1)
            for k in range(KC):
                dve.wait_ge(z_hi.sem, z_hi.at(k + 1))
                dve.tensor_tensor(h_lo[:, k, :], y[:, k, :], h_hi[:, k, :].bitcast(F32), ALU.subtract
                                  ).then_inc(z_ready.sem, 1)
            split_linear_dve(core, dve, w, acc, KC, 2 * KC, par[:, B_PW2, :])
            chain.close()

    norm_split_close(core)
    w.close(3 * KC)
    lin_used.close(KC + 2)
    par_in.close(48)
    for s in (z_full, z_hi, sig_ready, glu_ready, y_ready, yc_ready, sq_ready, n_ready, z_ready):
        s.close(KC)
    for s in (diag_ready, diag_used):
        s.close(PE_TAP_CHUNKS * TAPS)
    for s in (mean_ready, var_ready, std_ready, hist_ready):
        s.close(1)
    stored.close(32)
    core.end_stage()




CH = 64
NCH = SEQ // CH
NT = SEQ // P
HP = NH // 2
DECAY = float(np.exp(-0.5))
LEVELS = 6
MIX = ["k_k", "k_a", "r_k", "ln_w", "ln_b", "w0", "a0", "mix0", "mix1", "mix2", "mix3", "mix4", "mix5"]


def rwkv_project(core, stage, r, k, v, s, a, par):
    nc, io = core.nc, core.io
    h_ready, par_in, lora_in = core.sig("norm_h_ready"), core.sig("rwkv_par_in"), core.sig("rwkv_lora_in", pool_dma=True)
    mix_ready, lin_ready, lin_used = core.sig("rwkv_mix_ready"), core.sig("lin_ready"), core.sig("lin_used")
    low_ready, act_ready = core.sig("rwkv_low_ready"), core.sig("rwkv_act_ready")
    lora_ready, lora_used = core.sig("rwkv_lora_ready"), core.sig("rwkv_lora_used")
    stored = core.sig("rwkv_proj_stored")
    gain = core.gains[:, 2, :]
    with ExitStack() as inner:
        sb, ps = tiles(core, inner)
        diff = sb("diff", [P, KC, T])
        g = diff
        std = sb("std", [P, T])
        mixed = [sb(f"mixed{u}", [P, KC, T]) for u in range(2)]
        shift = sb("shift", [P, KC, NB])
        slots = [sb(f"w{u}", [P, KC, P]) for u in range(2)]
        down = [sb("down_w", [P, KC, 64]), sb("down_a", [P, KC, 64]), sb("down_g", [P, KC, P])]
        up = [sb("up_w", [64, D]), sb("up_a", [64, D]), sb("up_g", [P, D])]
        low = [sb("low_w", [64, T]), sb("low_a", [64, T]), sb("low_g", [P, T])]
        acc = [ps(f"acc{u}", [P, 4, 512]) for u in range(2)]
        sq = mixed[1]
        low_acc = [acc[0][0:64, 0:2, 0:HALF], acc[0][0:64, 2:4, 0:HALF], acc[1][:, 0:2, 0:HALF]]
        block = inner.enter_context(nc.Block())

        @block.sync
        def _(sync):
            sync.dma_start(par[:], io["rwkv_par"]).then_inc(par_in.sem, 16)
            sync.dma_start(shift[:], io["rwkv_shift"]).then_inc(par_in.sem, 16)
            linear_sync(core, sync, slots, io["rwkv_rkv"], 3 * KC, 0)
            sync.wait_ge(h_ready.sem, h_ready.at(KC))
            sync.dma_start(io["shift_out"], core.hT[:, :, SEQ - 1:T]).then_inc(stored.sem, 16)
            for c in range(0, KC, 2):
                sync.wait_ge(lora_used.sem, lora_used.at(2 * KC + c + 2))
                sync.dma_start(io["s_gate"][:, c:c + 2], g[:, c:c + 2]).then_inc(stored.sem, 16)
            sync.wait_ge(stored.sem, stored.at(16 + 16 * KC // 2))

        @block.gpsimd
        def _(pool):
            for m in range(3):
                pool.dma_start(down[m][:], io[f"rwkv_down{m}"]).then_inc(lora_in.sem, 16)
                pool.dma_start(up[m][:], io[f"rwkv_up{m}"]).then_inc(lora_in.sem, 16)

        @block.tensor
        def _(pe):
            norm_pe(core, pe, sq, acc[0])
            for m in range(3):
                pe.wait_ge(mix_ready.sem, mix_ready.at(KC * (m + 1)))
                linear_pe(core, pe, slots, mixed[m % 2], acc, KC, KC * m)
            pe.wait_ge(lin_used.sem, lin_used.at(3 * KC + 2))
            pe.wait_ge(lora_in.sem, lora_in.at(96))
            for m in range(3):
                pe.wait_ge(mix_ready.sem, mix_ready.at(KC * (m + 4)))
                for half in range(2):
                    for i in range(KC):
                        mm = pe.matmul(low_acc[m][:, half, :], down[m][:, i, :],
                                       mixed[(m + 3) % 2][:, i, half * HALF:(half + 1) * HALF],
                                       start=(i == 0), stop=(i == KC - 1))
                mm.then_inc(low_ready.sem, 1)
            pe.wait_ge(act_ready.sem, act_ready.at(3))
            for n in range(3 * KC):
                m, c, q = n // KC, n % KC, n % 4
                if n >= 4:
                    pe.wait_ge(lora_used.sem, lora_used.at(n - 3))
                for half in range(2):
                    mm = pe.matmul(acc[q // 2][:, 2 * (q % 2) + half, 0:HALF], up[m][:, c * P:(c + 1) * P],
                                   low[m][:, half * HALF:(half + 1) * HALF], start=True, stop=True)
                mm.then_inc(lora_ready.sem, 1)

        @block.scalar
        def _(act):
            norm_act(core, act, sq, std, acc[0])
            for n in range(3 * KC):
                act.wait_ge(lin_ready.sem, lin_ready.at(n + 1))
                act.activation(halves((r, k, v)[n // KC][:, n % KC, :]), acc[n % 2][:, 0:2, 0:HALF], ACT.Copy
                               ).then_inc(lin_used.sem, 1)
            for m, func in enumerate((ACT.Tanh, ACT.Copy, ACT.Sigmoid)):
                act.wait_ge(low_ready.sem, low_ready.at(m + 1))
                act.activation(halves(low[m][:, :]), low_acc[m], func).then_inc(act_ready.sem, 1)
            act.wait_ge(par_in.sem, par_in.at(32))
            for n in range(3 * KC):
                m, c, q = n // KC, n % KC, n % 4
                act.wait_ge(lora_ready.sem, lora_ready.at(n + 1))
                src = acc[q // 2][:, 2 * (q % 2):2 * (q % 2) + 2, 0:HALF]
                if m < 2:
                    bias = par[:, MIX.index(("w0", "a0")[m]), c:c + 1]
                    ins = act.activation(halves((s, a)[m][:, c, :]), src, ACT.Sigmoid, bias=bias)
                else:
                    ins = act.activation(halves(g[:, c, :]), src, ACT.Copy)
                ins.then_inc(lora_used.sem, 1)

        @block.vector
        def _(dve):
            chain = Chain(core, dve, "dve_chain")
            dve.sem_inc(lin_used.sem, 2)
            norm_sum_dve(core, dve, sq)
            norm_dve(core, dve, std, gain)
            dve.wait_ge(h_ready.sem, h_ready.at(KC))
            dve.wait_ge(par_in.sem, par_in.at(32))
            h = core.hT
            dve.tensor_scalar(diff[:, :, 0:1], h[:, :, 0:1], -1.0, None, ALU.mult)
            dve.tensor_tensor(diff[:, :, 1:SEQ], h[:, :, 0:SEQ - 1], h[:, :, 1:SEQ], ALU.subtract)
            chain.link(dve.tensor_tensor(diff[:, :, SEQ:T], shift[:], h[:, :, SEQ:T], ALU.subtract))
            chain.link(dve.engine_nop())
            for m in range(6):
                if 2 <= m <= 4:
                    dve.wait_ge(lin_ready.sem, lin_ready.at(KC * (m - 1)))
                if m == 5:
                    dve.wait_ge(low_ready.sem, low_ready.at(1))
                for c in range(KC):
                    dve.scalar_tensor_tensor(out=mixed[m % 2][:, c, :], in0=diff[:, c, :],
                                             scalar=par[:, MIX.index(f"mix{m}"), c:c + 1], in1=h[:, c, :],
                                             op0=ALU.mult, op1=ALU.add).then_inc(mix_ready.sem, 1)
            chain.close()

    norm_close(core)
    linear_close(core, 3 * KC)
    par_in.close(32)
    lora_in.close(96)
    mix_ready.close(6 * KC)
    low_ready.close(3)
    act_ready.close(3)
    lora_ready.close(3 * KC)
    lora_used.close(3 * KC)
    stored.close(16 + 16 * KC // 2)
    core.end_stage()


def rwkv_prepare(core, stage, r, k, v, s, a, wc, par):
    nc, io = core.nc, core.io
    kk = core.hT
    names = ("kk_ready", "kksq_ready", "nsum_ready", "norm_ready", "inv_ready", "bc_ready", "kkn_ready", "cs_ready",
             "dcs_ready", "exp_ready", "exp_used", "rk_ready", "dot_ready", "bonus_ready")
    sg = {n: core.sig("rwkv_" + n) for n in names}
    const_in, stored = core.sig("rwkv_const_in"), core.sig("rwkv_bonus_stored")
    with ExitStack() as inner:
        sb, ps = tiles(core, inner)
        sel = sb("sel", [P, KC, NH])
        selT = sb("selT", [NH, KC, P])
        blk = sb("blk", [P, P])
        reset = sb("reset", [P, SEQ])
        bonus = sb("bonus", [P, KC, T])
        sq = [sb(f"sq{u}", [P, T]) for u in range(2)]
        cs = [sb(f"cs{u}", [P, SEQ]) for u in range(2)]
        dcs = [sb(f"dcs{u}", [P, SEQ]) for u in range(2)]
        W, Wp, iW = ([sb(f"{n}{u}", [P, SEQ]) for u in range(2)] for n in ("W", "Wp", "iW"))
        tmp = [sb(f"tmp{u}", [P, T]) for u in range(2)]
        rk = [sb(f"rk{u}", [P, T]) for u in range(2)]
        inv = sb("inv", [NH, T])
        nsum = ps("nsum", [NH, 2, 512])
        dot = [ps(f"dot{u}", [P, 2, 512]) for u in range(2)]
        bc = dot
        block = inner.enter_context(nc.Block())

        @block.sync
        def _(sync):
            sync.dma_start(sel[:], io["c_sel"]).then_inc(const_in.sem, 16)
            sync.dma_start(selT[:], io["c_selT"]).then_inc(const_in.sem, 16)
            sync.dma_start(blk[:], io["c_blk"]).then_inc(const_in.sem, 16)
            sync.dma_start(reset[:], io["c_reset"]).then_inc(const_in.sem, 16)
            for c in range(0, KC, 2):
                sync.wait_ge(sg["bonus_ready"].sem, sg["bonus_ready"].at(c + 2))
                sync.dma_start(io["s_bonus"][:, c:c + 2], bonus[:, c:c + 2]).then_inc(stored.sem, 16)
            sync.wait_ge(stored.sem, stored.at(16 * KC // 2))

        @block.tensor
        def _(pe):
            pe.wait_ge(const_in.sem, const_in.at(64))
            for c in range(KC):
                pe.wait_ge(sg["kksq_ready"].sem, sg["kksq_ready"].at(c + 1))
                for half in range(2):
                    mm = pe.matmul(nsum[:, half, 0:HALF], sel[:, c, :], sq[c % 2][:, half * HALF:(half + 1) * HALF],
                                   start=(c == 0), stop=(c == KC - 1))
                mm.then_inc(sg["nsum_ready"].sem, 1)
            pe.wait_ge(sg["inv_ready"].sem, sg["inv_ready"].at(1))
            for c in range(KC):
                if c >= 2:
                    pe.wait_ge(sg["kkn_ready"].sem, sg["kkn_ready"].at(c - 1))
                for half in range(2):
                    mm = pe.matmul(bc[c % 2][:, half, 0:HALF], selT[:, c, :], inv[:, half * HALF:(half + 1) * HALF],
                                   start=True, stop=True)
                mm.then_inc(sg["bc_ready"].sem, 1)
            pe.wait_ge(sg["kkn_ready"].sem, sg["kkn_ready"].at(KC))
            for c in range(KC):
                pe.wait_ge(sg["rk_ready"].sem, sg["rk_ready"].at(c + 1))
                if c >= 2:
                    pe.wait_ge(sg["bonus_ready"].sem, sg["bonus_ready"].at(c - 1))
                for half in range(2):
                    mm = pe.matmul(dot[c % 2][:, half, 0:HALF], blk[:, :], rk[c % 2][:, half * HALF:(half + 1) * HALF],
                                   start=True, stop=True)
                mm.then_inc(sg["dot_ready"].sem, 1)

        @block.scalar
        def _(act):
            for c in range(KC):
                act.wait_ge(sg["kk_ready"].sem, sg["kk_ready"].at(c + 1))
                if c >= 2:
                    act.wait_ge(sg["nsum_ready"].sem, sg["nsum_ready"].at(c - 1))
                act.activation(sq[c % 2][:, :], kk[:, c, :], ACT.Square).then_inc(sg["kksq_ready"].sem, 1)
            act.wait_ge(sg["nsum_ready"].sem, sg["nsum_ready"].at(KC))
            act.activation(halves(inv[:, :]), nsum[:, :, 0:HALF], ACT.Sqrt).then_inc(sg["norm_ready"].sem, 1)
            for c in range(KC):
                u = c % 2
                act.wait_ge(sg["cs_ready"].sem, sg["cs_ready"].at(c + 1))
                act.wait_ge(sg["dcs_ready"].sem, sg["dcs_ready"].at(c + 1))
                if c >= 2:
                    act.wait_ge(sg["exp_used"].sem, sg["exp_used"].at(c - 1))
                act.activation(W[u][:, :], cs[u][:, :], ACT.Exp, scale=-DECAY)
                act.activation(iW[u][:, :], cs[u][:, :], ACT.Exp, scale=DECAY)
                act.activation(Wp[u][:, :], dcs[u][:, :], ACT.Exp, scale=-DECAY)
                act.activation(s[:, c, SEQ:T], s[:, c, SEQ:T], ACT.Exp, scale=-DECAY).then_inc(sg["exp_ready"].sem, 1)

        @block.vector
        def _(dve):
            chain = Chain(core, dve, "dve_chain")
            for c in range(KC):
                dve.tensor_scalar(kk[:, c, :], k[:, c, :], par[:, MIX.index("k_k"), c:c + 1], None, ALU.mult
                                  ).then_inc(sg["kk_ready"].sem, 1)
            dve.wait_ge(sg["kk_ready"].sem, sg["kk_ready"].at(KC))
            for c in range(KC):
                t_ = tmp[c % 2]
                chain.link(dve.tensor_scalar(t_[:, :], a[:, c, :], 1.0, par[:, MIX.index("k_a"), c:c + 1],
                                             ALU.subtract, ALU.mult))
                ins = dve.scalar_tensor_tensor(out=k[:, c, :], in0=t_[:, :], scalar=1.0, in1=k[:, c, :],
                                               op0=ALU.add, op1=ALU.mult)
            chain.link(ins)
            dve.wait_ge(sg["norm_ready"].sem, sg["norm_ready"].at(1))
            chain.link(dve.tensor_scalar(inv[:, :], inv[:, :], 1e-12, None, ALU.max))
            dve.reciprocal(inv[:, :], inv[:, :]).then_inc(sg["inv_ready"].sem, 1)
            for c in range(KC):
                dve.wait_ge(sg["bc_ready"].sem, sg["bc_ready"].at(c + 1))
                dve.wait_ge(sg["kksq_ready"].sem, sg["kksq_ready"].at(c + 1))
                dve.tensor_tensor(halves(kk[:, c, :]), halves(kk[:, c, :]), bc[c % 2][:, :, 0:HALF], ALU.mult
                                  ).then_inc(sg["kkn_ready"].sem, 1)
            dve.wait_ge(sg["kkn_ready"].sem, sg["kkn_ready"].at(KC))
            dve.wait_ge(const_in.sem, const_in.at(64))

            def sums(c):
                if c >= 2:
                    dve.wait_ge(sg["exp_ready"].sem, sg["exp_ready"].at(c - 1))
                dve.tensor_tensor_scan(out=cs[c % 2][:, :], data0=reset[:, :], data1=s[:, c, 0:SEQ], initial=0.0,
                                       op0=ALU.mult, op1=ALU.add).then_inc(sg["cs_ready"].sem, 1)
                dve.wait_ge(sg["cs_ready"].sem, sg["cs_ready"].at(c + 1))
                dve.tensor_tensor(dcs[c % 2][:, :], cs[c % 2][:, :], s[:, c, 0:SEQ], ALU.subtract
                                  ).then_inc(sg["dcs_ready"].sem, 1)

            def bonuses(c):
                dve.wait_ge(sg["dot_ready"].sem, sg["dot_ready"].at(c + 1))
                dve.tensor_tensor(halves(bonus[:, c, :]), dot[c % 2][:, :, 0:HALF], halves(v[:, c, :]), ALU.mult
                                  ).then_inc(sg["bonus_ready"].sem, 1)

            sums(0)
            for c in range(KC):
                u = c % 2
                if c + 1 < KC:
                    sums(c + 1)
                if c >= 2:
                    dve.wait_ge(sg["dot_ready"].sem, sg["dot_ready"].at(c - 1))
                dve.scalar_tensor_tensor(out=rk[u][:, :], in0=r[:, c, :], scalar=par[:, MIX.index("r_k"), c:c + 1],
                                         in1=k[:, c, :], op0=ALU.mult, op1=ALU.mult).then_inc(sg["rk_ready"].sem, 1)
                chain.link(dve.tensor_tensor(a[:, c, :], a[:, c, :], kk[:, c, :], ALU.mult))
                if c:
                    bonuses(c - 1)
                dve.wait_ge(sg["exp_ready"].sem, sg["exp_ready"].at(c + 1))
                dve.wait_ge(sg["rk_ready"].sem, sg["rk_ready"].at(c + 1))
                chain.link(dve.tensor_copy(wc[:, c, :].rearrange("p (n o) -> p n o", o=1),
                                           W[u][:, :].rearrange("p (n i) -> p n i", i=CH)[:, :, CH - 1:CH]))
                for x, f in ((kk, Wp), (r, W), (a, iW), (k, iW)):
                    ins = dve.tensor_tensor(x[:, c, 0:SEQ], x[:, c, 0:SEQ], f[u][:, :], ALU.mult)
                ins.then_inc(sg["exp_used"].sem, 1)
            bonuses(KC - 1)
            chain.close()

    for n in names:
        sg[n].close({"norm_ready": 1, "inv_ready": 1}.get(n, KC))
    const_in.close(64)
    stored.close(16 * KC // 2)
    core.end_stage()


def rwkv_sample(core, stage, r, k, v, s, a):
    nc, io = core.nc, core.io
    tr_ready, tok_ready = core.sig("rws_tr_ready"), core.sig("rws_tok_ready")
    spilled, vec_in, state_in = core.sig("rws_spilled"), core.sig("rws_vec_in"), core.sig("rws_state_in")
    y_ready, y_out, y_in = core.sig("rws_y_ready"), core.sig("rws_y_out"), core.sig("rws_y_in")
    back_ready, s_ready, stored = core.sig("rws_back_ready"), core.sig("rws_s_ready"), core.sig("rws_stored")
    sw_ready, vk_ready = core.sig("rws_sw_ready"), core.sig("rws_vk_ready")
    with ExitStack() as inner:
        sb, ps = tiles(core, inner)
        tok = sb("tok", [NB, 6, D])
        vec = sb("vec", [P, 6, HD])
        S = sb("S", [P, HD, HD])
        tmp = sb("tmp", [P, HD, HD])
        SW, VK = sb("SW", [P, HD, HD]), sb("VK", [P, HD, HD])
        sa = sb("sa", [P, HD])
        y = sb("y", [P, HD])
        ytok = tok[:, 0, :]
        pt = [ps(f"pt{i}", [NB, D]) for i in range(3)]
        pb = ps("pb", [P, KC * NB])
        R, W, K, V, KK, B = range(6)
        block = inner.enter_context(nc.Block())

        @block.sync
        def _(sync):
            sync.dma_start(S[:], io["rwkv_state"]).then_inc(state_in.sem, 16)
            for i in range(6):
                sync.wait_ge(tok_ready.sem, tok_ready.at(i + 1))
            sync.dma_start(io["s_vec"], tok[:]).then_inc(spilled.sem, 16)
            sync.wait_ge(spilled.sem, spilled.at(16))
            for b in range(NB):
                sync.dma_start(vec[NH * b:NH * (b + 1)], io["s_vec"][b].rearrange("a (h d) -> h a d", d=HD)
                               ).then_inc(vec_in.sem, 16)
            sync.wait_ge(s_ready.sem, s_ready.at(1))
            sync.dma_start(io["wkv_sample"], SW[:]).then_inc(stored.sem, 16)
            sync.wait_ge(y_ready.sem, y_ready.at(1))
            sync.dma_start(io["s_y"].rearrange("b (h d) -> (b h) d", d=HD), y[:]).then_inc(y_out.sem, 16)
            sync.wait_ge(y_out.sem, y_out.at(16))
            sync.dma_start(ytok, io["s_y"]).then_inc(y_in.sem, 16)
            sync.wait_ge(stored.sem, stored.at(16))

        @block.tensor
        def _(pe):
            for i, x in enumerate((r, s, k, v, core.hT, a)):
                if i >= 3:
                    pe.wait_ge(tok_ready.sem, tok_ready.at(i - 2))
                for c in range(KC):
                    mm = pe.transpose(pt[i % 3][:, c * P:(c + 1) * P], x[:, c, SEQ:T], core.ident[:, :])
                mm.then_inc(tr_ready.sem, 1)
            pe.wait_ge(y_in.sem, y_in.at(16))
            for c in range(KC):
                mm = pe.transpose(pb[:, c * NB:(c + 1) * NB], tok[:, 0, c * P:(c + 1) * P], core.ident[0:NB, 0:NB])
            mm.then_inc(back_ready.sem, 1)

        @block.scalar
        def _(act):
            for i in range(6):
                act.wait_ge(tr_ready.sem, tr_ready.at(i + 1))
                act.activation(tok[:, i, :], pt[i % 3][:, :], ACT.Copy).then_inc(tok_ready.sem, 1)

        def row(i):
            return vec[:, i, :].rearrange("p (o j) -> p o j", o=1).broadcast_to([P, HD, HD])

        def column(ap):
            return ap.rearrange("p (i o) -> p i o", o=1).broadcast_to([P, HD, HD])

        @block.gpsimd
        def _(pool):
            pool.wait_ge(state_in.sem, state_in.at(16))
            pool.wait_ge(vec_in.sem, vec_in.at(16 * NB))
            pool.tensor_tensor(SW[:], S[:], row(W), ALU.mult).then_inc(sw_ready.sem, 1)
            pool.tensor_tensor(VK[:], column(vec[:, V, :]), row(K), ALU.mult).then_inc(vk_ready.sem, 1)

        @block.vector
        def _(dve):
            chain = Chain(core, dve, "dve_chain")
            dve.wait_ge(state_in.sem, state_in.at(16))
            dve.wait_ge(vec_in.sem, vec_in.at(16 * NB))
            chain.link(dve.tensor_tensor(tmp[:], S[:], row(KK), ALU.mult))
            chain.link(dve.tensor_reduce(sa[:, :], tmp[:], AXX, ALU.add))
            chain.link(dve.tensor_tensor(tmp[:], column(sa[:, :]), row(B), ALU.mult))
            dve.wait_ge(sw_ready.sem, sw_ready.at(1))
            chain.link(dve.tensor_tensor(SW[:], SW[:], tmp[:], ALU.subtract))
            dve.wait_ge(vk_ready.sem, vk_ready.at(1))
            dve.tensor_tensor(SW[:], SW[:], VK[:], ALU.add).then_inc(s_ready.sem, 1)
            dve.wait_ge(s_ready.sem, s_ready.at(1))
            chain.link(dve.tensor_tensor(tmp[:], SW[:], row(R), ALU.mult))
            dve.tensor_reduce(y[:, :], tmp[:], AXX, ALU.add).then_inc(y_ready.sem, 1)
            dve.wait_ge(back_ready.sem, back_ready.at(1))
            dve.tensor_copy(r[:, :, SEQ:T], pb[:, :].rearrange("p (k b) -> p k b", b=NB))
            chain.close()

    for s_, n in ((tr_ready, 6), (tok_ready, 6), (spilled, 16), (vec_in, 16 * NB), (state_in, 16), (y_ready, 1),
                  (y_out, 16), (y_in, 16), (back_ready, 1), (s_ready, 1), (stored, 16),
                  (sw_ready, 1), (vk_ready, 1)):
        s_.close(n)
    core.end_stage()


def rwkv_chunks(core, stage, r, k, v, b, wc):
    nc, io = core.nc, core.io
    kk = core.hT
    const_in = core.sig("rwc_const_in")
    names = ("tok_tr", "tok_done", "gram", "gram_done", "nv", "nv_done", "ltm", "m", "m_done", "d", "d_done",
             "eye_done", "a", "r1_done", "u", "u_done", "x", "x_done", "y", "y_done", "zero", "out_tr", "out_done")
    sg = {n: core.sig("rwc_" + n) for n in names}
    cnt = dict.fromkeys(names, 0)
    stored = core.sig("rwc_stored")
    NL = 4 * LEVELS
    ND = NL - 4
    NLM = 4

    def doubled(t, n):
        return ND * t + max(0, n - 3)

    with ExitStack() as inner:
        sb, ps = tiles(core, inner)
        mask = sb("mask", [P, 4, P])
        level = sb("level", [P, LEVELS, P])
        LT, MB, MK = (sb(n, [P, NH, P]) for n in ("LT", "MB", "MK"))
        NTr = [sb(f"NTr{u}", [P, P]) for u in range(2)]
        inv, invT = sb("inv", [P, NH, P]), sb("invT", [P, NH, P])
        Bz, Kz = sb("Bz", [P, 2, D]), sb("Kz", [P, 2, D])
        Vt, NV, R1, U = (sb(n, [P, D]) for n in ("Vt", "NV", "R1", "U"))
        X = [sb(f"X{u}", [P, HP, P]) for u in range(2)]
        Lm = [sb(f"Lm{u}", [P, 4, P]) for u in range(NLM)]
        Ms = [sb(f"Ms{u}", [P, 4, P]) for u in range(2)]
        bank = ps("bank", [P, 8, 512])
        block = inner.enter_context(nc.Block())

        def at(name, n):
            return sg[name].sem, sg[name].at(n)

        def row_half(q):
            return slice(64 * q, 64 * q + 64)

        @block.sync
        def _(sync):
            sync.dma_start(mask[:], io["c_mask4"]).then_inc(const_in.sem, 16)
            sync.dma_start(level[:], io["c_level"]).then_inc(const_in.sem, 16)
            sync.wait_ge(*at("out_done", 2))
            sync.dma_start(io["wkv_prompt"], R1[:, 0:HP * HD].rearrange("p (h j) -> p h j", j=HD)).then_inc(stored.sem, 16)
            sync.wait_ge(stored.sem, stored.at(16))

        @block.gpsimd
        def _(pool):
            for x in (Bz[:], Kz[:], X[0][:], X[1][:], R1[:], U[:]):
                pool.memset(x, 0.0).then_inc(sg["zero"].sem, 1)
            pool.wait_ge(const_in.sem, const_in.at(32))
            for t in range(NT):
                for n in range(NL):
                    lv, q = n // 4, n % 4
                    if n < 4:
                        pool.wait_ge(*at("gram_done", NH * t + 4 * q + 4))
                    i = NL * t + n
                    if i >= NLM:
                        pool.wait_ge(*at("m", i - NLM + 1))
                    if NLM <= n < NLM + 4:
                        pool.wait_ge(*at("d_done", i - NLM + 1))
                    pool.tensor_tensor(Lm[n % NLM][:], LT[:, 4 * q:4 * q + 4, :],
                                       level[:, lv:lv + 1, :].broadcast_to([P, 4, P]), ALU.mult
                                       ).then_inc(sg["ltm"].sem, 1)

        def pe_nv(pe, t, h):
            pe.wait_ge(*at("gram_done", NH * t + h + 1))
            if h == 0:
                pe.wait_ge(*at("tok_done", 5 * t + 5))
            if h == NH // 2:
                pe.wait_ge(*at("nv_done", 2 * t + 1))
            mm = pe.matmul(bank[:, 7, (h % 8) * HD:(h % 8 + 1) * HD], NTr[h % 2][:, :], Vt[:, h * HD:(h + 1) * HD],
                           start=True, stop=True)
            mm.then_inc(sg["nv"].sem, 1)

        @block.tensor
        def _(pe):
            pe.wait_ge(*at("zero", 6))
            for t in range(NT):
                tok = slice(P * t, P * t + P)
                if t:
                    pe.wait_ge(*at("x_done", 4 * t))
                    pe.wait_ge(*at("y_done", 2 * t))
                for i, x in enumerate((b, k, v)):
                    for c in range(KC):
                        mm = pe.transpose(bank[:, 2 * i + c // 4, (c % 4) * P:(c % 4 + 1) * P], x[:, c, tok],
                                          core.ident[:, :])
                    mm.then_inc(sg["tok_tr"].sem, 1)
                for h in range(NH):
                    j = slice(64 * (h % 2), 64 * (h % 2) + 64)
                    bk = h % 6
                    if h < 6:
                        pe.wait_ge(*at("tok_done", 5 * t + (2, 2, 4, 4, 5, 5)[h]))
                    else:
                        pe.wait_ge(*at("gram_done", NH * t + h - 5))
                    for i, (x, y) in enumerate(((b, kk), (b, r), (k, kk), (k, r))):
                        mm = pe.matmul(bank[:, bk, i * P:(i + 1) * P], x[j, h // 2, tok], y[j, h // 2, tok],
                                       start=True, stop=True)
                    mm.then_inc(sg["gram"].sem, 1)
                    if h >= 1:
                        pe_nv(pe, t, h - 1)
                pe_nv(pe, t, NH - 1)
                pe.wait_ge(*at("eye_done", 2 * t + 2))

                def level_m(n):
                    q = n % 4
                    i = NL * t + n
                    pe.wait_ge(*at("ltm", i + 1))
                    if n < 2:
                        pe.wait_ge(*at("gram_done", NH * t + NH))
                    elif n < 6:
                        pe.wait_ge(*at("d_done", i - 1))
                    else:
                        pe.wait_ge(*at("m_done", doubled(t, n - 2)))
                    if n >= 4:
                        pe.wait_ge(*at("d_done", i - 3))
                    for e in range(4):
                        mm = pe.matmul(bank[:, n % 2, e * P:(e + 1) * P], Lm[n % NLM][:, e, :], inv[:, 4 * q + e, :],
                                       start=True, stop=True)
                    mm.then_inc(sg["m"].sem, 1)

                for n in range(5):
                    level_m(n)
                for n in range(4, NL):
                    q = n % 4
                    i = NL * t + n
                    if n + 1 < NL:
                        level_m(n + 1)
                    pe.wait_ge(*at("m_done", doubled(t, n)))
                    pe.wait_ge(*at("d_done", i - 1))
                    for e in range(4):
                        h = 4 * q + e
                        if n // 4 < LEVELS - 1:
                            pe.matmul(bank[:, 2 + n % 2, e * P:(e + 1) * P], invT[:, h, :], Ms[n % 2][:, e, :],
                                      start=True, stop=True)
                        mm = pe.matmul(bank[:, 4 + n % 2, e * P:(e + 1) * P], Ms[n % 2][:, e, :], invT[:, h, :],
                                       start=True, stop=True)
                    mm.then_inc(sg["d"].sem, 1)
                pe.wait_ge(*at("d_done", NL * (t + 1)))
                pe.wait_ge(*at("nv_done", t + 1))
                for half in range(2):
                    c = 2 * t + half
                    Xc = X[c % 2]
                    if c:
                        pe.wait_ge(*at("x_done", 2 * c))
                    for p in range(HP):
                        mm = pe.matmul(bank[:, p // 4, (p % 4) * P:(p % 4 + 1) * P], kk[:, p, tok], Xc[:, p, :],
                                       start=True, stop=True)
                    mm.then_inc(sg["a"].sem, 1)
                    pe.wait_ge(*at("r1_done", c + 1))
                    for h in range(NH):
                        mm = pe.matmul(bank[row_half(half), 2 + h // 8, (h % 8) * HD:(h % 8 + 1) * HD],
                                       invT[:, h, row_half(half)], R1[:, h * HD:(h + 1) * HD], start=True, stop=True)
                    mm.then_inc(sg["u"].sem, 1)
                    pe.wait_ge(*at("u_done", c + 1))
                    for p in range(HP):
                        o = bank[:, 4 + p // 4, (p % 4) * P:(p % 4 + 1) * P]
                        cols = slice(p * P, (p + 1) * P)
                        pe.matmul(o, Kz[:, half, cols], Vt[:, cols], start=True, stop=False)
                        mm = pe.matmul(o, Bz[:, half, cols], U[:, cols], start=False, stop=True)
                    mm.then_inc(sg["x"].sem, 1)
                    if c:
                        pe.wait_ge(*at("y_done", c))
                    ct = slice(CH * c, CH * c + CH)
                    lc = row_half(half)
                    for p in range(HP):
                        o = bank[:, 6, p * CH:(p + 1) * CH]
                        pe.matmul(o, Xc[:, p, :], r[:, p, ct], start=True, stop=False)
                        for e in range(2):
                            h = 2 * p + e
                            oh = bank[64 * e:64 * e + 64, 6, p * CH:(p + 1) * CH]
                            pe.matmul(oh, Vt[:, h * HD:(h + 1) * HD], MK[:, h, lc], start=False, stop=False)
                            mm = pe.matmul(oh, U[:, h * HD:(h + 1) * HD], MB[:, h, lc], start=False, stop=True)
                    mm.then_inc(sg["y"].sem, 1)
            pe.wait_ge(*at("x_done", 2 * NCH))
            for p in range(HP):
                mm = pe.transpose(bank[:, p // 4, (p % 4) * P:(p % 4 + 1) * P], X[NCH % 2][:, p, :], core.ident[:, :])
            mm.then_inc(sg["out_tr"].sem, 1)

        @block.scalar
        def _(act):
            act.wait_ge(*at("zero", 6))
            for t in range(NT):
                for i in range(2):
                    act.wait_ge(*at("tok_tr", 3 * t + i + 1))
                    for half in range(2):
                        rows = row_half(half)
                        act.activation((Bz, Kz)[i][rows, half, :].rearrange("p (a n) -> p a n", a=2),
                                       bank[rows, 2 * i:2 * i + 2, :], ACT.Copy, scale=(-1.0, 1.0)[i]
                                       ).then_inc(sg["tok_done"].sem, 1)
                act.wait_ge(*at("tok_tr", 3 * t + 3))
                act.activation(Vt[:, :].rearrange("p (a n) -> p a n", a=2), bank[:, 4:6, :], ACT.Copy
                               ).then_inc(sg["tok_done"].sem, 1)
                for i in range(2):
                    act.wait_ge(*at("nv", NH * t + 8 * (i + 1)))
                    act.activation(NV[:, 512 * i:512 * (i + 1)], bank[:, 7, :], ACT.Copy).then_inc(sg["nv_done"].sem, 1)
                for n in range(4, NL):
                    act.wait_ge(*at("m", NL * t + n + 1))
                    if doubled(t, n) > 2:
                        act.wait_ge(*at("d", doubled(t, n) - 2))
                    act.activation(Ms[n % 2][:], bank[:, n % 2, :].rearrange("p (e n) -> p e n", e=4), ACT.Copy
                                   ).then_inc(sg["m_done"].sem, 1)
                for half in range(2):
                    c = 2 * t + half
                    rows = row_half(half)
                    act.wait_ge(*at("u", c + 1))
                    if c:
                        act.wait_ge(*at("y", c))
                    act.activation(U[rows, :].rearrange("p (a n) -> p a n", a=2), bank[rows, 2:4, :], ACT.Copy
                                   ).then_inc(sg["u_done"].sem, 1)
                    act.wait_ge(*at("y", c + 1))
                    act.activation(r[:, :, CH * c:CH * c + CH], bank[:, 6, :].rearrange("p (h t) -> p h t", t=CH), ACT.Copy
                                   ).then_inc(sg["y_done"].sem, 1)

        @block.vector
        def _(dve):
            chain = Chain(core, dve, "dve_chain")
            dve.wait_ge(const_in.sem, const_in.at(32))
            dve.wait_ge(*at("zero", 6))
            for t in range(NT):
                for x in (inv, invT):
                    if t:
                        dve.wait_ge(*at("y", 2 * t))
                    dve.tensor_copy(x[:], core.ident[:, :].rearrange("p (o n) -> p o n", o=1).broadcast_to([P, NH, P])
                                    ).then_inc(sg["eye_done"].sem, 1)
                for h in range(NH):
                    bk = h % 6
                    dve.wait_ge(*at("gram", NH * t + h + 1))
                    if h >= 2:
                        dve.wait_ge(*at("nv", NH * t + h - 1))
                    elif t:
                        dve.wait_ge(*at("nv", NH * t))
                    for i, o in enumerate((LT[:, h, :], MB[:, h, :], NTr[h % 2][:, :], MK[:, h, :])):
                        ins = dve.tensor_tensor(o, bank[:, bk, i * P:(i + 1) * P], mask[:, i, :], ALU.mult)
                    ins.then_inc(sg["gram_done"].sem, 1)
                dve.wait_ge(*at("eye_done", 2 * t + 2))
                for n in range(NL):
                    q = n % 4
                    i = NL * t + n
                    hs = slice(4 * q, 4 * q + 4)
                    if n < 4:
                        dve.wait_ge(*at("m", i + 1))
                        dve.tensor_tensor(invT[:, hs, :], invT[:, hs, :], Lm[n % NLM][:], ALU.subtract)
                        dve.tensor_tensor(inv[:, hs, :], inv[:, hs, :],
                                          bank[:, n % 2, :].rearrange("p (e n) -> p e n", e=4), ALU.subtract
                                          ).then_inc(sg["d_done"].sem, 1)
                        continue
                    dve.wait_ge(*at("d", doubled(t, n)))
                    dve.wait_ge(*at("d_done", i - 3))
                    if n // 4 < LEVELS - 1:
                        dve.tensor_tensor(inv[:, hs, :], inv[:, hs, :],
                                          bank[:, 2 + n % 2, :].rearrange("p (e n) -> p e n", e=4), ALU.subtract)
                    dve.tensor_tensor(invT[:, hs, :], invT[:, hs, :],
                                      bank[:, 4 + n % 2, :].rearrange("p (e n) -> p e n", e=4), ALU.subtract
                                      ).then_inc(sg["d_done"].sem, 1)
                for half in range(2):
                    c = 2 * t + half
                    rows = row_half(half)
                    dve.wait_ge(*at("a", c + 1))
                    dve.wait_ge(*at("nv_done", 2 * t + 2))
                    dve.tensor_tensor(R1[rows, :].rearrange("p (a n) -> p a n", a=2), bank[rows, 0:2, :],
                                      NV[rows, :].rearrange("p (a n) -> p a n", a=2), ALU.add).then_inc(sg["r1_done"].sem, 1)
                    dve.wait_ge(*at("x", c + 1))
                    if c:
                        dve.wait_ge(*at("y", c))
                    for e in range(2):
                        d = slice(64 * e, 64 * e + 64)
                        new = X[(c + 1) % 2][d, :, d]
                        chain.link(dve.tensor_tensor(new, bank[d, 4:6, :].rearrange("p a (h i) -> p (a h) i", i=P)[:, :, d],
                                                     X[c % 2][d, :, d], ALU.add))
                        dve.tensor_tensor(new, new, wc[d, :, c:c + 1].broadcast_to([64, HP, 64]), ALU.mult
                                          ).then_inc(sg["x_done"].sem, 1)
                    dve.wait_ge(*at("x_done", 2 * c + 2))
            dve.wait_ge(*at("out_tr", 1))
            for e in range(2):
                d = slice(64 * e, 64 * e + 64)
                dve.tensor_copy(R1[d, 0:HP * HD].rearrange("p (h i) -> p h i", i=HD),
                                bank[d, 0:2, :].rearrange("p a (h i) -> p (a h) i", i=P)[:, :, d]
                                ).then_inc(sg["out_done"].sem, 1)
            chain.close()

    total = {"tok_tr": 3 * NT, "tok_done": 5 * NT, "gram": NH * NT, "gram_done": NH * NT, "nv": NH * NT,
             "nv_done": 2 * NT, "ltm": NL * NT, "m": NL * NT, "m_done": ND * NT, "d": ND * NT, "d_done": NL * NT,
             "eye_done": 2 * NT, "a": NCH, "r1_done": NCH, "u": NCH, "u_done": NCH, "x": NCH, "x_done": 2 * NCH,
             "y": NCH, "y_done": NCH, "zero": 6, "out_tr": 1, "out_done": 2}
    for n, c in total.items():
        sg[n].close(c)
    const_in.close(32)
    stored.close(16)
    core.end_stage()


def rwkv_finish(core, stage, y, par):
    nc, io = core.nc, core.io
    names = ("mean_ready", "yc_ready", "sq_ready", "var_ready", "std_ready", "inv_ready", "bc_ready", "n_ready",
             "ln_ready", "bonus_done", "z_full", "z_hi", "z_ready")
    sg = {n: core.sig("rwf_" + n) for n in names}
    in_, bonus_in, lin_used = core.sig("rwf_in"), core.sig("rwf_bonus_in"), core.sig("lin_used")
    with ExitStack() as inner:
        sb, ps = tiles(core, inner)
        sel = sb("sel", [P, KC, NH])
        selT = sb("selT", [NH, KC, P])
        blk = sb("blk", [P, P])
        g, bonus = sb("g", [P, KC, T]), sb("bonus", [P, KC, T])
        sq = [sb(f"sq{u}", [P, T]) for u in range(2)]
        inv = sb("inv", [NH, T])
        w = SplitWeights(core, sb, "rwf_w", KC)
        z_hi, z_lo = sb("z_hi", [P, KC, T], F32R), sb("z_lo", [P, KC, T], F32R)
        nsum = ps("nsum", [NH, 2, 512])
        acc = [ps(f"acc{u}", [P, 2, 512]) for u in range(2)]
        block = inner.enter_context(nc.Block())

        @block.sync
        def _(sync):
            for d, n in ((sel, "c_sel"), (selT, "c_selT"), (blk, "c_blk")):
                sync.dma_start(d[:], io[n]).then_inc(in_.sem, 16)
            for d, n in ((g, "s_gate"), (bonus, "s_bonus")):
                sync.dma_start(d[:], io[n]).then_inc(bonus_in.sem, 16)
            split_linear_sync(sync, w, io["rwkv_wo"], KC)

        def var(pe, c):
            pe.wait_ge(sg["sq_ready"].sem, sg["sq_ready"].at(c + 1))
            for half in range(2):
                mm = pe.matmul(nsum[:, half, 0:HALF], sel[:, c, :], sq[c % 2][:, half * HALF:(half + 1) * HALF],
                               start=(c == 0), stop=(c == KC - 1))
            mm.then_inc(sg["var_ready"].sem, 1)

        @block.tensor
        def _(pe):
            pe.wait_ge(in_.sem, in_.at(48))
            for c in range(KC):
                if c >= 2:
                    pe.wait_ge(sg["yc_ready"].sem, sg["yc_ready"].at(c - 1))
                for half in range(2):
                    mm = pe.matmul(acc[c % 2][:, half, 0:HALF], blk[:, :], y[:, c, half * HALF:(half + 1) * HALF],
                                   start=True, stop=True)
                mm.then_inc(sg["mean_ready"].sem, 1)
                if c:
                    var(pe, c - 1)
            var(pe, KC - 1)
            pe.wait_ge(sg["inv_ready"].sem, sg["inv_ready"].at(1))
            for c in range(KC):
                if c >= 2:
                    pe.wait_ge(sg["n_ready"].sem, sg["n_ready"].at(c - 1))
                for half in range(2):
                    mm = pe.matmul(acc[c % 2][:, half, 0:HALF], selT[:, c, :], inv[:, half * HALF:(half + 1) * HALF],
                                   start=True, stop=True)
                mm.then_inc(sg["bc_ready"].sem, 1)
            pe.wait_ge(sg["z_ready"].sem, sg["z_ready"].at(KC))
            split_linear_pe(core, pe, w, z_hi, z_lo, acc, KC)

        @block.scalar
        def _(act):
            for c in range(KC):
                act.wait_ge(sg["yc_ready"].sem, sg["yc_ready"].at(c + 1))
                if c >= 2:
                    act.wait_ge(sg["var_ready"].sem, sg["var_ready"].at(c - 1))
                act.activation(sq[c % 2][:, :], y[:, c, :], ACT.Square).then_inc(sg["sq_ready"].sem, 1)
            for c in range(2):
                w.cut_hi(act, KC, c)
            act.wait_ge(sg["var_ready"].sem, sg["var_ready"].at(KC))
            act.activation(halves(inv[:, :]), nsum[:, :, 0:HALF], ACT.Sqrt, bias=core.col("eps_gn")[0:NH],
                           scale=1.0 / HD).then_inc(sg["std_ready"].sem, 1)
            for c in range(KC):
                act.wait_ge(sg["n_ready"].sem, sg["n_ready"].at(c + 1))
                act.activation(y[:, c, :], y[:, c, :], ACT.Identity, bias=par[:, MIX.index("ln_b"), c:c + 1],
                               scale=par[:, MIX.index("ln_w"), c:c + 1]).then_inc(sg["ln_ready"].sem, 1)
            for c in range(KC):
                act.wait_ge(sg["z_full"].sem, sg["z_full"].at(c + 1))
                act.activation(z_hi[:, c, :], y[:, c, :], ACT.Copy).then_inc(sg["z_hi"].sem, 1)
            for c in range(2, KC):
                w.cut_hi(act, KC, c)

        @block.gpsimd
        def _(pool):
            pool.wait_ge(bonus_in.sem, bonus_in.at(32))
            for c in range(KC):
                pool.wait_ge(sg["ln_ready"].sem, sg["ln_ready"].at(c + 1))
                pool.tensor_tensor(y[:, c, :], y[:, c, :], bonus[:, c, :], ALU.add).then_inc(sg["bonus_done"].sem, 1)

        @block.vector
        def _(dve):
            dve.sem_inc(lin_used.sem, 2)
            for c in range(KC):
                dve.wait_ge(sg["mean_ready"].sem, sg["mean_ready"].at(c + 1))
                dve.scalar_tensor_tensor(out=halves(y[:, c, :]), in0=acc[c % 2][:, :, 0:HALF], scalar=-1.0 / HD,
                                         in1=halves(y[:, c, :]), op0=ALU.mult, op1=ALU.add
                                         ).then_inc(sg["yc_ready"].sem, 1)
            dve.wait_ge(sg["std_ready"].sem, sg["std_ready"].at(1))
            dve.reciprocal(inv[:, :], inv[:, :]).then_inc(sg["inv_ready"].sem, 1)
            for c in range(KC):
                dve.wait_ge(sg["bc_ready"].sem, sg["bc_ready"].at(c + 1))
                dve.wait_ge(sg["sq_ready"].sem, sg["sq_ready"].at(c + 1))
                dve.tensor_tensor(halves(y[:, c, :]), halves(y[:, c, :]), acc[c % 2][:, :, 0:HALF], ALU.mult
                                  ).then_inc(sg["n_ready"].sem, 1)
            for c in range(2):
                w.cut_lo(dve, KC, c)
            for c in range(KC + 1):
                if c < KC:
                    dve.wait_ge(sg["bonus_done"].sem, sg["bonus_done"].at(c + 1))
                    dve.tensor_tensor(y[:, c, :], y[:, c, :], g[:, c, :], ALU.mult).then_inc(sg["z_full"].sem, 1)
                if c:
                    dve.wait_ge(sg["z_hi"].sem, sg["z_hi"].at(c))
                    dve.tensor_tensor(z_lo[:, c - 1, :], y[:, c - 1, :], z_hi[:, c - 1, :].bitcast(F32), ALU.subtract
                                      ).then_inc(sg["z_ready"].sem, 1)
            split_linear_dve(core, dve, w, acc, KC)

    w.close(KC)
    lin_used.close(KC + 2)
    in_.close(48)
    bonus_in.close(32)
    for n in names:
        sg[n].close({"std_ready": 1, "inv_ready": 1}.get(n, KC))
    core.end_stage()


def rwkv_stage(core, _):
    with ExitStack() as stage:
        sb, _ps = tiles(core, stage)
        par = sb("rwkv_par", [P, len(MIX), KC])
        wc = sb("wc", [P, KC, NCH])
        r, k, v, a = (sb(n, [P, KC, T]) for n in "rkva")
        with ExitStack() as early:
            s = tiles(core, early)[0]("s", [P, KC, T])
            rwkv_project(core, early, r, k, v, s, a, par)
            rwkv_prepare(core, early, r, k, v, s, a, wc, par)
            rwkv_sample(core, early, r, k, v, s, a)
        rwkv_chunks(core, stage, r, k, v, a, wc)
        rwkv_finish(core, stage, r, par)



HG = NH // NG
CMP_LP = 16
SEG = 16
NSEG_P = SEQ // SEG
NC_P = NSEG_P - 1
NSEG_S = PAST // SEG
NC_S = NSEG_S - 1
NSLC = PAST // HD + 1
NSEL = 16
Q_COL, KV_COL, GATE_COL = 0, D, D + 6 * KVW
NWT = 4
NK = NPAGE + NWT
PGC = 2 * NG * 8 * 8
PW = 256
PROJ_W = [PW] * (PROJ // PW) + [PROJ % PW]


def nsa_project(core, j, layer, proj, o, cmp_in):
    nc, io = core.nc, core.io
    h_ready = core.sig("norm_h_ready")
    ready, done = core.sig("nsa_proj_ready"), core.sig("nsa_proj_done")
    loaded, stored = core.sig("nsa_cmp_loaded"), core.sig("nsa_win_stored")
    gain = core.gains[:, 2 * layer, :]
    n_out = len(PROJ_W) * (NT + 1)
    with ExitStack() as inner:
        sb, ps = tiles(core, inner)
        sq = core.hT
        h_hi, h_lo = sb("h_hi", [P, KC, T], F32R), sb("h_lo", [P, KC, T], F32R)
        std = sb("std", [P, T])
        full = [sb(f"full{u}", [P, T]) for u in range(2)]
        raw = o[:].rearrange("p t d -> p (t d)")[:, 0:2 * KC * PW].rearrange("p (u k n) -> p u k n", u=2, k=KC)
        w = SplitWeights(core, sb, "nsa_w", KC, PW, [raw[:, u] for u in range(2)], ready, NT + 1)
        bank = ps("bank", [P, 8, 512])
        block = inner.enter_context(nc.Block())

        @block.sync
        def _(sync):
            for c, width in enumerate(PROJ_W):
                w.load(sync, io["nsa_w_in"][j, :, :, PW * c:PW * c + width], c)
                if c == 3:
                    for tile, name in cmp_in:
                        sync.dma_start(tile[:], io[name][j]).then_inc(loaded.sem, 16)
            sync.dma_start(io["win_sample"][j, :, 0:SEQ - 1], io["cache_win"][j, :, 1:SEQ]).then_inc(stored.sem, 16)
            sync.wait_ge(loaded.sem, loaded.at(16 * len(cmp_in)))
            sync.wait_ge(stored.sem, stored.at(16))

        @block.tensor
        def _(pe):
            norm_pe(core, pe, sq, bank)
            pe.wait_ge(h_ready.sem, h_ready.at(KC))
            for c, width in enumerate(PROJ_W):
                pe.wait_ge(w.lo_ready.sem, w.lo_ready.at(c + 1))
                for t in range(NT + 1):
                    n = (NT + 1) * c + t
                    rows = min(P, T - P * t)
                    if n >= 8:
                        pe.wait_ge(done.sem, done.at(n - 7))
                    for k in range(KC):
                        for i, (h, wt) in enumerate(((h_hi, w.lo), (h_lo, w.hi), (h_hi, w.hi))):
                            mm = pe.matmul(bank[0:rows, n % 8, 0:width], h[:, k, P * t:P * t + rows],
                                           wt[c % 2][:, k, 0:width], start=(k == 0 and i == 0),
                                           stop=(k == KC - 1 and i == 2))
                    mm.then_inc(ready.sem, 1)

        @block.scalar
        def _(act):
            norm_act(core, act, sq, std, bank, lambda: [w.cut_hi(act, KC, c, width=PROJ_W[c]) for c in range(2)])
            norm_split_act(core, act, full, h_hi)
            for n in range(n_out):
                c, t = n // (NT + 1), n % (NT + 1)
                rows, width = min(P, T - P * t), PROJ_W[c]
                act.wait_ge(ready.sem, ready.at(n + 1))
                func = ACT.Sigmoid if c == len(PROJ_W) - 1 else ACT.Copy
                act.activation(proj[0:rows, t, PW * c:PW * c + width], bank[0:rows, n % 8, 0:width], func
                               ).then_inc(done.sem, 1)
                if t == NT and c + 2 < len(PROJ_W):
                    w.cut_hi(act, KC, c + 2, width=PROJ_W[c + 2])

        @block.vector
        def _(dve):
            norm_sum_dve(core, dve, sq)
            for c in range(2):
                w.cut_lo(dve, KC, c, width=PROJ_W[c])
            norm_split_dve(core, dve, std, gain, full, h_hi, h_lo)
            for c in range(2, len(PROJ_W)):
                w.cut_lo(dve, KC, c, width=PROJ_W[c])

    norm_split_close(core)
    w.close(len(PROJ_W))
    ready.close(n_out)
    done.close(n_out)
    loaded.close(16 * len(cmp_in))
    stored.close(16)
    core.end_stage()


def nsa_heads(core, j, proj, qnT, qrT, kT, qblk):
    nc, io = core.nc, core.io
    names = ("gain", "sq", "ss", "rt", "kd", "rope", "inv", "krope", "tr", "tr_done")
    sg = {n: core.sig("nsh_" + n) for n in names}
    in_, stored = core.sig("nsh_in"), core.sig("nsh_stored")
    NTT = NT + 1
    with ExitStack() as inner:
        sb, ps = tiles(core, inner)
        cos, sin = sb("cos", [P, NTT, HD]), sb("sin", [P, NTT, HD])
        gq, gk = sb("gq", [P, HD]), sb("gk", [P, 2, HD])
        sq = [core.hT[:].rearrange("p k t -> p (k t)")[:, 24 * HD * u:24 * HD * (u + 1)].rearrange("p (h d) -> p h d", d=HD)
              for u in range(2)]
        ss = [sb(f"ss{u}", [P, 24]) for u in range(2)]
        qr = [sb(f"qr{u}", [P, NH, HD]) for u in range(2)]
        tmp = sb("tmp", [P, NH, HD])
        tmpk = sb("tmpk", [P, 2, NG, HD])
        kd = [sb(f"kd{u}", [P, 2 * NG, 2, HD]) for u in range(2)]
        qs = sb("qs", [NB, 2, 2, HG, 2, HD])
        bank = ps("bank", [P, 8, 512])
        block = inner.enter_context(nc.Block())

        def rows_of(t):
            return min(P, T - P * t)

        def q_of(t):
            return proj[0:rows_of(t), t, 0:D].rearrange("p (h d) -> p h d", d=HD)

        def k_of(t):
            return proj[0:rows_of(t), t, KV_COL + 2 * KVW:KV_COL + 6 * KVW].rearrange(
                "p (a x) -> p a x", a=2)[:, :, 0:KVW].rearrange("p a (g d) -> p a g d", d=HD)

        @block.sync
        def _(sync):
            sync.dma_start(cos[:], io["c_cos"]).then_inc(in_.sem, 16)
            sync.dma_start(sin[:], io["c_sin"]).then_inc(in_.sem, 16)
            sync.dma_start(gq[:], io["nsa_gq"][j]).then_inc(in_.sem, 16)
            sync.dma_start(gk[:], io["nsa_gk"][j]).then_inc(in_.sem, 16)
            for t in range(NTT):
                n = rows_of(t)
                sync.wait_ge(sg["krope"].sem, sg["krope"].at(t + 1))
                rows = io["rows_prompt"][j, P * t:P * t + P] if t < NT else io["rows_sample"][j]
                sync.dma_start(rows, proj[0:n, t, KV_COL:KV_COL + 4 * KVW]).then_inc(stored.sem, 16)
                if t < NT:
                    sync.dma_start(io["win_prompt"][j, P * t:P * t + P], proj[0:n, t, KV_COL + 4 * KVW:KV_COL + 6 * KVW]
                                   ).then_inc(stored.sem, 16)
            sync.dma_start(io["s_new"].rearrange("s b x -> b s x"),
                           proj[0:NB, NT, KV_COL + 2 * KVW:KV_COL + 6 * KVW].rearrange("b (s x) -> b s x", s=4)
                           ).then_inc(stored.sem, 16)
            sync.dma_start(io["win_sample"][j, :, SEQ - 1], proj[0:NB, NT, KV_COL + 4 * KVW:KV_COL + 6 * KVW]
                           ).then_inc(stored.sem, 16)
            sync.wait_ge(sg["rope"].sem, sg["rope"].at(NTT))
            sync.dma_start(io["s_q"].rearrange("b (h d) -> b h d", d=HD), qr[NT % 2][0:NB]).then_inc(stored.sem, 16)
            sync.dma_start(io["s_g3"], proj[0:NB, NT, GATE_COL:PROJ]).then_inc(stored.sem, 16)
            sync.wait_ge(stored.sem, stored.at(16 * (2 * NTT + 3)))

        @block.tensor
        def _(pe):
            for t in range(NT):
                pe.wait_ge(sg["rope"].sem, sg["rope"].at(t + 1))
                for i in range(3):
                    n = 3 * t + i
                    if n >= 4:
                        pe.wait_ge(sg["tr_done"].sem, sg["tr_done"].at(n - 3))
                    for c in range(8):
                        if i == 0:
                            src = proj[:, t, c * P:(c + 1) * P]
                        elif i == 1:
                            src = qr[t % 2][:, 2 * c:2 * c + 2, :]
                        else:
                            pe.wait_ge(sg["kd"].sem, sg["kd"].at(2 * t + 2))
                            src = kd[t % 2][:, c]
                        mm = pe.transpose(bank[:, 2 * (n % 4) + c // 4, (c % 4) * P:(c % 4 + 1) * P], src,
                                          core.ident[:, :])
                    mm.then_inc(sg["tr"].sem, 1)
            pe.wait_ge(sg["kd"].sem, sg["kd"].at(2 * NT + 4))
            pe.wait_ge(sg["tr_done"].sem, sg["tr_done"].at(3 * NT))
            for i in range(2):
                for c in range(8):
                    gp, n = c // HG, c % HG
                    mm = pe.transpose(bank[:, i, c * NB:(c + 1) * NB], qs[:, i, gp, n], core.ident[0:NB, 0:NB])
                mm.then_inc(sg["tr"].sem, 1)

        def copies(act, t):
            tok = slice(P * t, P * t + P)
            for i, dst in enumerate((qnT[:, :, tok], qrT[:, :, tok], kT[:, :, tok])):
                n = 3 * t + i
                b = 2 * (n % 4)
                act.wait_ge(sg["tr"].sem, sg["tr"].at(n + 1))
                act.activation(dst, bank[:, b:b + 2, :].rearrange("p a (h t) -> p (a h) t", t=P), ACT.Copy
                               ).then_inc(sg["tr_done"].sem, 1)

        @block.scalar
        def _(act):
            def squares(t):
                n = rows_of(t)
                if t >= 2:
                    act.wait_ge(sg["ss"].sem, sg["ss"].at(t - 1))
                act.activation(sq[t % 2][0:n, 0:NH], q_of(t), ACT.Square)
                act.activation(sq[t % 2][0:n, NH:24].rearrange("p (a g) d -> p a g d", a=2), k_of(t), ACT.Square
                               ).then_inc(sg["sq"].sem, 1)

            squares(0)
            for t in range(NTT):
                n = rows_of(t)
                if t + 1 < NTT:
                    squares(t + 1)
                act.wait_ge(sg["ss"].sem, sg["ss"].at(t + 1))
                act.activation(ss[t % 2][0:n, :], ss[t % 2][0:n, :], ACT.Sqrt, bias=core.col("eps_rms")[0:n],
                               scale=1.0 / HD).then_inc(sg["rt"].sem, 1)
                if t >= 1:
                    copies(act, t - 1)
            for i in range(2):
                act.wait_ge(sg["tr"].sem, sg["tr"].at(3 * NT + i + 1))
                for e in range(2):
                    d = slice(64 * e, 64 * e + 64)
                    act.activation(qblk[i][d, :, :, 4 * e:4 * e + 4],
                                   bank[d, i, 0:64].rearrange("p (gp n b) -> p gp b n", gp=2, n=HG), ACT.Copy
                                   ).then_inc(sg["tr_done"].sem, 1)

        def table(x, t, lo, hi, heads):
            n = rows_of(t)
            return x[0:n, t, lo:hi].rearrange("p (o d) -> p o d", o=1).broadcast_to([n, heads, hi - lo])

        half = HD // 2

        @block.gpsimd
        def _(pool):
            chain = Chain(core, pool, "pool_chain")
            for i in range(2):
                pool.memset(qblk[i][:], 0.0).then_inc(sg["gain"].sem, 1)
            pool.wait_ge(in_.sem, in_.at(64))
            for t in range(NTT):
                n = rows_of(t)
                k = k_of(t)
                pool.wait_ge(sg["inv"].sem, sg["inv"].at(t + 1))
                chain.link(pool.tensor_tensor(k, k, ss[t % 2][0:n, NH:24].rearrange("p (a g o) -> p a g o", a=2, o=1)
                                              .broadcast_to([n, 2, NG, HD]), ALU.mult))
                chain.link(pool.tensor_tensor(k, k, gk[0:n].rearrange("p a (o d) -> p a o d", o=1)
                                              .broadcast_to([n, 2, NG, HD]), ALU.mult))
                for a in range(2):
                    ka, ta = k[:, a], tmpk[0:n, a]
                    pool.tensor_tensor(ta[:, :, 0:half], ka[:, :, half:HD], table(sin, t, 0, half, NG), ALU.mult)
                    chain.link(pool.tensor_tensor(ta[:, :, half:HD], ka[:, :, 0:half], table(sin, t, half, HD, NG),
                                                  ALU.mult))
                    chain.link(pool.tensor_tensor(ka, ka, table(cos, t, 0, HD, NG), ALU.mult))
                pool.tensor_tensor(k, k, tmpk[0:n], ALU.add).then_inc(sg["krope"].sem, 1)
                pool.wait_ge(sg["krope"].sem, sg["krope"].at(t + 1))
                if t < NT:
                    if t >= 2:
                        pool.wait_ge(sg["tr"].sem, sg["tr"].at(3 * (t - 1)))
                    for a in range(2):
                        pool.tensor_copy(kd[t % 2][:, NG * a:NG * (a + 1)], k[:, a].rearrange(
                            "p g (o d) -> p g o d", o=1).broadcast_to([P, NG, 2, HD])).then_inc(sg["kd"].sem, 1)
            pool.wait_ge(sg["rope"].sem, sg["rope"].at(NTT))
            for i, x in enumerate((q_of(NT), qr[NT % 2][0:NB])):
                for gp in range(2):
                    pool.tensor_copy(qs[:, i, gp], x.rearrange("p (gp g n) d -> p gp n g d", gp=2, g=2)[:, gp]
                                     ).then_inc(sg["kd"].sem, 1)
            chain.close()

        @block.vector
        def _(dve):
            chain = Chain(core, dve, "dve_chain")
            dve.wait_ge(in_.sem, in_.at(64))
            chain.link(dve.tensor_scalar(gq[:, :], gq[:, :], SCALE, None, ALU.mult))
            dve.wait_ge(sg["gain"].sem, sg["gain"].at(2))

            def sums(t):
                n = rows_of(t)
                dve.wait_ge(sg["sq"].sem, sg["sq"].at(t + 1))
                dve.tensor_reduce(ss[t % 2][0:n, :], sq[t % 2][0:n], AXX, ALU.add).then_inc(sg["ss"].sem, 1)

            sums(0)
            for t in range(NTT):
                n = rows_of(t)
                q = q_of(t)
                s = ss[t % 2][0:n, :]
                if t + 1 < NTT:
                    if t:
                        dve.wait_ge(sg["krope"].sem, sg["krope"].at(t))
                    sums(t + 1)
                dve.wait_ge(sg["rt"].sem, sg["rt"].at(t + 1))
                dve.reciprocal(s, s).then_inc(sg["inv"].sem, 1)
                dve.wait_ge(sg["inv"].sem, sg["inv"].at(t + 1))
                chain.link(dve.tensor_tensor(q, q, s[:, 0:NH].rearrange("p (h o) -> p h o", o=1).broadcast_to([n, NH, HD]),
                                             ALU.mult))
                chain.link(dve.tensor_tensor(q, q, gq[0:n, :].rearrange("p (o d) -> p o d", o=1).broadcast_to([n, NH, HD]),
                                             ALU.mult))
                if t >= 2:
                    dve.wait_ge(sg["tr"].sem, sg["tr"].at(3 * (t - 2) + 2))
                out = qr[t % 2][0:n]
                dve.tensor_tensor(tmp[0:n, :, 0:half], q[:, :, half:HD], table(sin, t, 0, half, NH), ALU.mult)
                dve.tensor_tensor(tmp[0:n, :, half:HD], q[:, :, 0:half], table(sin, t, half, HD, NH), ALU.mult)
                chain.link(dve.tensor_tensor(out, q, table(cos, t, 0, HD, NH), ALU.mult))
                ins = dve.tensor_tensor(out, out, tmp[0:n], ALU.add)
                ins.then_inc(sg["rope"].sem, 1)
                dve.wait_ge(sg["rope"].sem, sg["rope"].at(t + 1))
            chain.close()

    for n, c in zip(names, (2, NTT, NTT, NTT, 2 * NT + 4, NTT, NTT, NTT, 3 * NT + 2, 3 * NT + 4)):
        sg[n].close(c)
    in_.close(64)
    stored.close(16 * (2 * NTT + 3))
    core.end_stage()


def nsa_compress_prompt(core, j, w1, w2, pe_emb, bias, g0, kcT, vc):
    nc, io = core.nc, core.io
    names = ("b", "b_done", "tr", "tr_done", "h", "h_done", "o", "v_done", "sq", "ss", "rt", "kn", "t", "t_done")
    sg = {n: core.sig("ncp_" + n) for n in names}
    in_ = core.sig("ncp_in")
    with ExitStack() as inner:
        sb, ps = tiles(core, inner)
        seg = sb("seg", [NSEG_P, 2 * NG, SEG, HD])
        segT = core.hT[:].rearrange("p k t -> p (k t)")[:, 0:16 * NG * NSEG_P].rearrange(
            "p (s g l n) -> p s g l n", s=2, g=NG, l=8)
        hid = sb("hid", [P, 2, NG, NC_P])
        kn, sq = sb("kn", [NC_P, NG, HD]), sb("sq", [NC_P, NG, HD])
        kd = core.hT[:].rearrange("p k t -> p (k t)")[0:NC_P, 2048:2048 + 2 * KVW].rearrange(
            "p (g e d) -> p g e d", g=NG, e=2)
        ss = sb("ss", [NC_P, NG])
        bank = ps("bank", [P, 8, 512])
        block = inner.enter_context(nc.Block())

        def at(n, c):
            return sg[n].sem, sg[n].at(c)

        @block.sync
        def _(sync):
            for g in range(2 * NG):
                sync.dma_start(seg[:, g], io["rows_prompt"][j].rearrange("(n l) c -> n l c", l=SEG)
                               [:, :, g * HD:(g + 1) * HD]).then_inc(in_.sem, 16)

        @block.tensor
        def _(pe):
            for s in range(2):
                for i in range(CMP_LP):
                    mm = pe.matmul(bank[:, 4, s:s + 1], w1[:, s, i, :], pe_emb[:, s, i:i + 1],
                                   start=(i == 0), stop=(i == CMP_LP - 1))
            mm.then_inc(sg["b"].sem, 1)
            pe.wait_ge(in_.sem, in_.at(16 * 2 * NG))
            for n in range(64):
                s, g, lp = n // 32, n // 8 % NG, n % 8
                mm = pe.transpose(bank[:, n // 16, (n % 16) * NSEG_P:(n % 16 + 1) * NSEG_P],
                                  seg[:, s * NG + g, 2 * lp:2 * lp + 2, :],
                                  core.ident[0:NSEG_P, 0:NSEG_P])
                if n % 16 == 15:
                    mm.then_inc(sg["tr"].sem, 1)
            pe.wait_ge(*at("tr_done", 4))
            for s in range(2):
                for i in range(CMP_LP):
                    r, lp = i // 8, i % 8
                    mm = pe.matmul(bank[:, 5 + s, 0:NG * NC_P], w1[:, s, i, :], segT[:, s, :, lp, r:r + NC_P],
                                   start=(i == 0), stop=(i == CMP_LP - 1))
                mm.then_inc(sg["h"].sem, 1)
            pe.wait_ge(*at("h_done", 2))
            for s in range(2):
                for g in range(NG):
                    mm = pe.matmul(bank[0:NC_P, 7, (s * NG + g) * HD:(s * NG + g + 1) * HD], hid[:, s, g, :], w2[:, s, :],
                                   start=True, stop=True)
            mm.then_inc(sg["o"].sem, 1)
            pe.wait_ge(*at("kn", 1))
            for g in range(NG):
                mm = pe.transpose(bank[:, 0, g * NC_P:(g + 1) * NC_P],
                                  kd[:, g],
                                  core.ident[0:NC_P, 0:NC_P])
            mm.then_inc(sg["t"].sem, 1)

        @block.scalar
        def _(act):
            act.wait_ge(*at("b", 1))
            act.activation(bias[:, :], bank[:, 4, 0:2], ACT.Copy).then_inc(sg["b_done"].sem, 1)
            for i in range(4):
                act.wait_ge(*at("tr", i + 1))
                act.activation(segT[:, i // 2, 2 * (i % 2):2 * (i % 2) + 2].rearrange("p g l n -> p (g l n)"),
                               bank[:, i, :], ACT.Copy).then_inc(sg["tr_done"].sem, 1)
            act.wait_ge(*at("b_done", 1))
            for s in range(2):
                act.wait_ge(*at("h", s + 1))
                act.activation(hid[:, s].rearrange("p g n -> p (g n)"), bank[:, 5 + s, 0:NG * NC_P], ACT.Silu,
                               bias=bias[:, s:s + 1]).then_inc(sg["h_done"].sem, 1)
            act.wait_ge(*at("o", 1))
            act.activation(vc[:], bank[0:NC_P, 7, 256:512].rearrange("p (g d) -> p g d", d=HD), ACT.Copy
                           ).then_inc(sg["v_done"].sem, 1)
            act.activation(sq[:], bank[0:NC_P, 7, 0:256].rearrange("p (g d) -> p g d", d=HD), ACT.Square
                           ).then_inc(sg["sq"].sem, 1)
            act.wait_ge(*at("ss", 1))
            act.activation(ss[:], ss[:], ACT.Sqrt, bias=core.col("eps_rms")[0:NC_P], scale=1.0 / HD
                           ).then_inc(sg["rt"].sem, 1)
            act.wait_ge(*at("t", 1))
            act.activation(kcT[:].rearrange("p g n -> p (g n)"), bank[:, 0, 0:NG * NC_P], ACT.Copy
                           ).then_inc(sg["t_done"].sem, 1)

        @block.vector
        def _(dve):
            chain = Chain(core, dve, "dve_chain")
            dve.wait_ge(*at("sq", 1))
            dve.tensor_reduce(ss[:], sq[:], AXX, ALU.add).then_inc(sg["ss"].sem, 1)
            dve.wait_ge(*at("rt", 1))
            chain.link(dve.reciprocal(ss[:], ss[:]))
            chain.link(dve.tensor_tensor(kn[:], bank[0:NC_P, 7, 0:256].rearrange("p (g d) -> p g d", d=HD),
                                         ss[:].rearrange("p (g o) -> p g o", o=1).broadcast_to([NC_P, NG, HD]), ALU.mult))
            for e in range(2):
                ins = dve.tensor_tensor(kd[:, :, e, :], kn[:], g0[0:NC_P, :].rearrange("p (o d) -> p o d", o=1)
                                        .broadcast_to([NC_P, NG, HD]), ALU.mult)
            ins.then_inc(sg["kn"].sem, 1)
            chain.close()

    for n, c in {"tr": 4, "tr_done": 4, "h": 2, "h_done": 2}.items():
        sg[n].close(c)
    for n in names:
        if n not in ("tr", "tr_done", "h", "h_done"):
            sg[n].close(1)
    in_.close(16 * 2 * NG)
    core.end_stage()


def nsa_attend_compressed(core, proj, qnT, kcT, vc, o):
    nc, io = core.nc, core.io
    names = ("s", "smax", "exp", "p", "tr", "tr_done", "o", "o_done")
    sg = {n: core.sig("nac_" + n) for n in names}
    in_ = core.sig("nac_in")
    with ExitStack() as inner:
        sb, ps = tiles(core, inner)
        madd, mone = sb("madd", [P, NT, NC_P]), sb("mone", [P, NT, NC_P])
        S = [sb(f"S{u}", [P, 2, HP, NC_P]) for u in range(2)]
        mx, den = sb("mx", [P, 2, HP]), sb("den", [P, 2, HP])
        pT = sb("pT", [NC_P, NH, P])
        bank = ps("bank", [P, 8, 512])
        block = inner.enter_context(nc.Block())

        def at(n, c):
            return sg[n].sem, sg[n].at(c)

        @block.sync
        def _(sync):
            sync.dma_start(madd[:], io["c_cmp_add"]).then_inc(in_.sem, 16)
            sync.dma_start(mone[:], io["c_cmp_one"]).then_inc(in_.sem, 16)

        @block.tensor
        def _(pe):
            def scores(t):
                if t:
                    pe.wait_ge(*at("smax", t))
                for h in range(NH):
                    d = slice(64 * (h % 2), 64 * (h % 2) + 64)
                    mm = pe.matmul(bank[:, h % 2, (h // 2) * 32:(h // 2) * 32 + NC_P], qnT[d, h // 2, P * t:P * t + P],
                                   kcT[d, h // HG, :], start=True, stop=True)
                mm.then_inc(sg["s"].sem, 1)

            scores(0)
            scores(1)
            for t in range(NT):
                pe.wait_ge(*at("p", t + 1))
                if t:
                    pe.wait_ge(*at("tr_done", 2 * t))
                for h in range(NH):
                    mm = pe.transpose(bank[0:NC_P, 2 + h // 4, (h % 4) * P:(h % 4 + 1) * P], S[t % 2][:, h % 2, h // 2, :],
                                      core.ident[:, :])
                mm.then_inc(sg["tr"].sem, 1)
                if t + 2 < NT:
                    scores(t + 2)
                pe.wait_ge(*at("tr_done", 2 * t + 2))
                if t:
                    pe.wait_ge(*at("o_done", t))
                for h in range(NH):
                    mm = pe.matmul(bank[:, 6 + h // 8, (h % 8) * HD:(h % 8 + 1) * HD], pT[:, h, :], vc[:, h // HG, :],
                                   start=True, stop=True)
                mm.then_inc(sg["o"].sem, 1)

        @block.scalar
        def _(act):
            def exps(t):
                act.wait_ge(*at("smax", t + 1))
                act.activation(S[t % 2][:], S[t % 2][:], ACT.Exp).then_inc(sg["exp"].sem, 1)

            exps(0)
            for t in range(NT):
                if t + 1 < NT:
                    exps(t + 1)
                act.wait_ge(*at("tr", t + 1))
                if t:
                    act.wait_ge(*at("o", t))
                for i in range(2):
                    act.activation(pT[:, 8 * i:8 * i + 8, :], bank[0:NC_P, 2 + 2 * i:4 + 2 * i, :].rearrange(
                        "p a (h t) -> p (a h) t", t=P), ACT.Copy).then_inc(sg["tr_done"].sem, 1)

        @block.vector
        def _(dve):
            chain = Chain(core, dve, "dve_chain")
            dve.wait_ge(in_.sem, in_.at(32))
            mxf, denf = mx[:].rearrange("p e h -> p (e h)"), den[:].rearrange("p e h -> p (e h)")

            def below_max(t):
                Sf = S[t % 2][:].rearrange("p e h c -> p (e h) c")
                dve.wait_ge(*at("s", t + 1))
                if t >= 2:
                    dve.wait_ge(*at("tr", t - 1))
                for e in range(2):
                    chain.link(dve.tensor_tensor(S[t % 2][:, e], bank[:, e, 0:256].rearrange("p (h c) -> p h c", c=32)
                                                 [:, :, 0:NC_P], madd[:, t:t + 1, :].broadcast_to([P, HP, NC_P]), ALU.add))
                chain.link(dve.tensor_reduce(mxf, Sf, AXX, ALU.max))
                dve.tensor_tensor(Sf, Sf, mxf.rearrange("p (h o) -> p h o", o=1).broadcast_to([P, NH, NC_P]), ALU.subtract
                                  ).then_inc(sg["smax"].sem, 1)

            def weights(t):
                Sf = S[t % 2][:].rearrange("p e h c -> p (e h) c")
                dve.wait_ge(*at("exp", t + 1))
                chain.link(dve.tensor_tensor(Sf, Sf, mone[:, t:t + 1, :].broadcast_to([P, NH, NC_P]), ALU.mult))
                chain.link(dve.tensor_reduce(denf, Sf, AXX, ALU.add))
                chain.link(dve.tensor_scalar(denf, denf, 0.5, None, ALU.max))
                chain.link(dve.reciprocal(denf, denf))
                dve.tensor_tensor(Sf, Sf, denf.rearrange("p (h o) -> p h o", o=1).broadcast_to([P, NH, NC_P]), ALU.mult
                                  ).then_inc(sg["p"].sem, 1)

            def gated(t):
                dve.wait_ge(*at("o", t + 1))
                gate = proj[:, t, GATE_COL:PROJ].rearrange("p (h j) -> p h j", j=3)[:, :, 0:1].broadcast_to([P, NH, HD])
                dve.tensor_tensor(o[:, t, :].rearrange("p (h d) -> p h d", d=HD),
                                  bank[:, 6:8, :].rearrange("p a (h d) -> p (a h) d", d=HD), gate, ALU.mult
                                  ).then_inc(sg["o_done"].sem, 1)

            below_max(0)
            for t in range(NT):
                if t + 1 < NT:
                    below_max(t + 1)
                weights(t)
                if t:
                    gated(t - 1)
            gated(NT - 1)
            chain.close()

    in_.close(32)
    for n in names:
        sg[n].close(2 * NT if n == "tr_done" else NT)
    core.end_stage()


def nsa_attend_causal(core, proj, qrT, kT, o):
    nc, io = core.nc, core.io
    names = ("s", "mask", "max", "exp", "tr", "pd", "pa", "o", "o_done")
    sg = {n: core.sig("nat_" + n) for n in names}
    in_ = core.sig("nat_in")
    units = [(br, t, h) for br in range(2) for t in range(NT) for h in range(NH)]
    NU = len(units)
    AHEAD = 2
    LAG = 2
    NS = 4
    NPT = 3
    HH = NH // 2
    with ExitStack() as inner:
        sb, ps = tiles(core, inner)
        diag = sb("diag", [P, P])
        pr = [sb(f"pr{u}", [P, SEQ]) for u in range(NS)]
        prT = [sb(f"prT{u}", [P, NT, P]) for u in range(NPT)]
        nm = sb("nm", [P, NS])
        den = [sb(f"den{u}", [P, NH]) for u in range(2)]
        coef = sb("coef", [P, HH])
        part = sb("part", [P, HH, HD])
        bs = ps("bs", [P, NS, 512])
        bt = ps("bt", [P, 2, 512])
        bo = ps("bo", [P, 2, 512])
        block = inner.enter_context(nc.Block())

        def at(n, c):
            return sg[n].sem, sg[n].at(c)

        @block.sync
        def _(sync):
            sync.dma_start(diag[:], io["c_causal"]).then_inc(in_.sem, 16)

        @block.tensor
        def _(pe):
            def scores(u):
                br, t, h = units[u]
                if u >= NS:
                    pe.wait_ge(*at("exp", u - NS + 1))
                d = slice(64 * (h % 2), 64 * (h % 2) + 64)
                pe.matmul(bs[:, u % NS, 0:P * (t + 1)], qrT[d, h // 2, P * t:P * t + P],
                          kT[d, br * NG + h // HG, 0:P * (t + 1)], start=True, stop=True).then_inc(sg["s"].sem, 1)

            def values(u):
                br, t, h = units[u]
                pe.wait_ge(*at("pd" if u % 2 == 0 else "pa", u // 2 + 1))
                if h % HH == 0 and u >= NH:
                    pe.wait_ge(*at("o_done", u // HH - 1))
                at_v = KV_COL + (3 + 2 * br) * KVW + (h // HG) * HD
                for b in range(t + 1):
                    mm = pe.matmul(bo[:, h // HH, (h % HH) * HD:(h % HH + 1) * HD], prT[u % NPT][:, b, :],
                                   proj[:, b, at_v:at_v + HD], start=(b == 0), stop=(b == t))
                mm.then_inc(sg["o"].sem, 1)

            for u in range(AHEAD):
                scores(u)
            for u in range(NU):
                br, t, h = units[u]
                if u + AHEAD < NU:
                    scores(u + AHEAD)
                pe.wait_ge(*at("exp", u + 1))
                if u >= 2:
                    pe.wait_ge(*at("pd" if u % 2 == 0 else "pa", u // 2))
                for b in range(t + 1):
                    mm = pe.transpose(bt[:, u % 2, b * P:(b + 1) * P], pr[u % NS][:, b * P:(b + 1) * P], core.ident[:, :])
                mm.then_inc(sg["tr"].sem, 1)
                if u >= LAG:
                    values(u - LAG)
            for u in range(NU - LAG, NU):
                values(u)

        @block.scalar
        def _(act):
            def copy_back(u):
                t = units[u][1]
                act.wait_ge(*at("tr", u + 1))
                if u >= NPT:
                    act.wait_ge(*at("o", u - NPT + 1))
                act.activation(prT[u % NPT][:, 0:t + 1, :], bt[:, u % 2, 0:P * (t + 1)].rearrange("p (b q) -> p b q", q=P),
                               ACT.Copy).then_inc(sg["pa"].sem, 1)

            for u in range(NU):
                br, t, h = units[u]
                act.wait_ge(*at("max", u + 1))
                if u >= NS:
                    act.wait_ge(*at("tr", u - NS + 1))
                if h == 0 and u >= 2 * NH:
                    act.wait_ge(*at("o_done", 2 * (u // NH - 1)))
                act.activation(pr[u % NS][:, 0:P * (t + 1)], bs[:, u % NS, 0:P * (t + 1)], ACT.Exp,
                               bias=nm[:, u % NS:u % NS + 1],
                               accum_out=den[u // NH % 2][:, h:h + 1]).then_inc(sg["exp"].sem, 1)
                if u % 2 == 1 and u >= 2:
                    copy_back(u - 2)
            copy_back(NU - 1)

        @block.vector
        def _(dve):
            chain = Chain(core, dve, "dve_chain")
            dve.wait_ge(in_.sem, in_.at(16))

            def finish(m):
                n, half = m // 2, m % 2
                br, t = n // NT, n % NT
                heads = slice(half * HH, half * HH + HH)
                dve.wait_ge(*at("o", HH * (m + 1)))
                chain.link(dve.reciprocal(coef[:, :], den[n % 2][:, heads]))
                gate = proj[:, t, GATE_COL:PROJ].rearrange("p (h j) -> p h j", j=3)[:, heads, 1 + br:2 + br]
                chain.link(dve.tensor_tensor(coef[:, :].rearrange("p (h o) -> p h o", o=1),
                                             coef[:, :].rearrange("p (h o) -> p h o", o=1), gate, ALU.mult))
                chain.link(dve.tensor_tensor(part[:], bo[:, half].rearrange("p (h d) -> p h d", d=HD),
                                             coef[:, :].rearrange("p (h o) -> p h o", o=1).broadcast_to([P, HH, HD]),
                                             ALU.mult))
                ot = o[:, t, :].rearrange("p (h d) -> p h d", d=HD)[:, heads]
                dve.tensor_tensor(ot, ot, part[:], ALU.add).then_inc(sg["o_done"].sem, 1)

            def copy_back(u):
                t = units[u][1]
                dve.wait_ge(*at("tr", u + 1))
                if u >= NPT:
                    dve.wait_ge(*at("o", u - NPT + 1))
                dve.tensor_copy(prT[u % NPT][:, 0:t + 1, :], bt[:, u % 2, 0:P * (t + 1)].rearrange("p (b q) -> p b q", q=P)
                                ).then_inc(sg["pd"].sem, 1)

            for u in range(NU):
                br, t, h = units[u]
                dve.wait_ge(*at("s", u + 1))
                block_ = bs[:, u % NS, P * t:P * t + P]
                dve.tensor_tensor(block_, block_, diag[:, :], ALU.add).then_inc(sg["mask"].sem, 1)
                dve.wait_ge(*at("mask", u + 1))
                if u >= NS:
                    dve.wait_ge(*at("exp", u - NS + 1))
                dve.tensor_reduce(nm[:, u % NS:u % NS + 1], bs[:, u % NS, 0:P * (t + 1)], AXX, ALU.max, negate=True
                                  ).then_inc(sg["max"].sem, 1)
                if u % 2 == 0 and u >= 2:
                    copy_back(u - 2)
                if h % HH == LAG + 2 and u > HH:
                    finish(u // HH - 1)
            copy_back(NU - 2)
            finish(NU // HH - 1)
            chain.close()

    in_.close(16)
    for n in names:
        sg[n].close({"pd": NU // 2, "pa": NU // 2, "o_done": NU // HH}.get(n, NU))
    core.end_stage()


def nsa_sample_scores(core, j, w1, w2, bias, g0, qblk, qz, Sc, vcs, prob, new_k, new_v):
    nc, io = core.nc, core.io
    names = ("h", "h_done", "sc", "sc_done", "o", "v_done", "sq", "ss", "rt", "kn", "t", "t_done", "c", "c_done", "qz")
    sg = {n: core.sig("nss_" + n) for n in names}
    pt_in, new_in = core.sig("nss_pt_in"), core.sig("nss_new_in")
    pg_in = [core.sig(f"nss_pg_in{u}") for u in range(2)]
    with ExitStack() as inner:
        sb, ps = tiles(core, inner)
        pt = sb("pt", [1, NB * NPAGE], I32)
        pages = [sb(f"pages{u}", [P, NPAGE, PGC + 2 * P]) for u in range(2)]
        hid = [sb(f"hid{u}", [P, 2, NG, NC_S]) for u in range(2)]
        kn, sq = sb("kn", [NC_S, NG, HD]), sb("sq", [NC_S, NG, HD])
        ss = sb("ss", [NC_S, NG])
        kcT = sb("kcT", [P, 2, NC_S])
        bh = [ps(f"bh{u}", [P, 512]) for u in range(2)]
        bs, bo, btc = ps("bs", [P, NPAGE // 4, 512]), ps("bo", [P, 512]), ps("btc", [P, 512])
        bt, bc = btc[:, 0:2 * NC_S], btc[:, 2 * NC_S:2 * NC_S + NH]
        block = inner.enter_context(nc.Block())

        def at(n, c):
            return sg[n].sem, sg[n].at(c)

        def load_pages(eng, b, first, end):
            with eng.Fori(first, end) as p:
                page = eng.value_load(pt[0:1, bass.ds(p + NPAGE * b, 1)], min_val=0, max_val=io["cache_kT"].shape[1] - 1)
                eng.dma_start(pages[b % 2][:, bass.ds(p, 1), :],
                              io["cache_kT"][j, bass.ds(page, 1)].rearrange("o p n -> p o n")
                              ).then_inc(pg_in[b % 2].sem, 16)

        @block.sync
        def _(sync):
            sync.dma_start(pt[:], io["page_table"]).then_inc(pt_in.sem, 16)
            sync.wait_ge(pt_in.sem, pt_in.at(16))
            for b in range(NB):
                if b >= 2:
                    sync.wait_ge(*at("h", 4 * (b - 1)))
                    sync.wait_ge(*at("sc", b - 1))
                load_pages(sync, b, 0, NPAGE // 2 if b == 0 else NPAGE)

        @block.tensor
        def _(pe):
            def compress(b):
                pe.wait_ge(*at("h_done", 4 * b + 4))
                if b:
                    pe.wait_ge(*at("v_done", b))
                    pe.wait_ge(*at("kn", b))
                for s in range(2):
                    for g in range(NG):
                        mm = pe.matmul(bo[0:NC_S, (s * NG + g) * HD:(s * NG + g + 1) * HD], hid[b % 2][:, s, g, :], w2[:, s, :],
                                       start=True, stop=True)
                mm.then_inc(sg["o"].sem, 1)

            def turn(b):
                pe.wait_ge(*at("kn", b + 1))
                if b:
                    pe.wait_ge(*at("t_done", b))
                for gp in range(2):
                    mm = pe.transpose(bt[:, gp * NC_S:(gp + 1) * NC_S], kn[:, 2 * gp:2 * gp + 2, :],
                                      core.ident[0:NC_S, 0:NC_S])
                mm.then_inc(sg["t"].sem, 1)

            def score(b):
                pe.wait_ge(*at("t_done", b + 1))
                if b:
                    pe.wait_ge(*at("c_done", b))
                for gp in range(2):
                    mm = pe.matmul(bc[0:NC_S, gp * 8:gp * 8 + 8], kcT[:, gp, :], qblk[0][:, gp, b, :], start=True, stop=True)
                mm.then_inc(sg["c"].sem, 1)

            for b in range(NB):
                u = b % 2
                pe.wait_ge(pg_in[u].sem, pg_in[u].at(16 * NPAGE * (b // 2 + 1)))
                for q in range(4):
                    s, gp = q // 2, q % 2
                    n = 4 * b + q
                    if n >= 2:
                        pe.wait_ge(*at("h_done", n - 1))
                    o = bh[n % 2][:, 0:2 * (NSEG_S + 1)].rearrange("p (g c) -> p g c", g=2)
                    x = pages[u][:, :, 0:PGC].rearrange("p pg (s g l n) -> p s g l pg n", s=2, g=NG, l=8)
                    for i in range(CMP_LP):
                        r, lp = i // 8, i % 8
                        mm = pe.matmul(o[:, :, 1 - r:1 - r + NSEG_S].rearrange("p g (pg n) -> p g pg n", n=8),
                                       w1[:, s, i, :], x[:, s, 2 * gp:2 * gp + 2, lp], start=(i == 0),
                                       stop=(i == CMP_LP - 1), skip_group_check=True)
                    mm.then_inc(sg["h"].sem, 1)
                    if b and q < 3:
                        (compress, turn, score)[q](b - 1)
                if b == 0:
                    pe.wait_ge(*at("qz", 2))
                for q in range(NPAGE // 4):
                    for gp in range(2):
                        mm = pe.matmul(bs[:, q, :].rearrange("p (k n) -> p k n", k=4), qz[:, gp, b, :],
                                       pages[u][:, 4 * q:4 * q + 4, PGC + gp * P:PGC + (gp + 1) * P],
                                       start=(b == 0 and gp == 0), stop=(b == NB - 1 and gp == 1))
                mm.then_inc(sg["sc"].sem, 1)
            for step in (compress, turn, score):
                step(NB - 1)

        @block.scalar
        def _(act):
            def compress(b):
                act.wait_ge(*at("o", b + 1))
                if b:
                    act.wait_ge(*at("ss", b))
                act.activation(sq[:], bo[0:NC_S, 0:256].rearrange("p (g d) -> p g d", d=HD), ACT.Square
                               ).then_inc(sg["sq"].sem, 1)
                act.activation(vcs[:, b, :], bo[0:NC_S, 256:512], ACT.Copy).then_inc(sg["v_done"].sem, 1)
                act.wait_ge(*at("ss", b + 1))
                act.activation(ss[:], ss[:], ACT.Sqrt, bias=core.col("eps_rms")[0:NC_S], scale=1.0 / HD
                               ).then_inc(sg["rt"].sem, 1)

            def turn(b):
                act.wait_ge(*at("t", b + 1))
                act.activation(kcT[:], bt[:, 0:2 * NC_S].rearrange("p (g c) -> p g c", g=2), ACT.Copy
                               ).then_inc(sg["t_done"].sem, 1)

            def score(b):
                act.wait_ge(*at("c", b + 1))
                act.activation(Sc[:, b * NH:(b + 1) * NH], bc[0:NC_S, 0:NH], ACT.Copy).then_inc(sg["c_done"].sem, 1)

            act.wait_ge(pt_in.sem, pt_in.at(16))
            load_pages(act, 0, NPAGE // 2, NPAGE)
            for b in range(NB):
                for q in range(4):
                    s, gp = q // 2, q % 2
                    n = 4 * b + q
                    act.wait_ge(*at("h", n + 1))
                    if q == 0 and b >= 2:
                        act.wait_ge(*at("o", b - 1))
                    act.activation(hid[b % 2][:, s, 2 * gp:2 * gp + 2, :],
                                   bh[n % 2][:, 0:2 * (NSEG_S + 1)].rearrange("p (g c) -> p g c", g=2)[:, :, 1:NSEG_S],
                                   ACT.Silu, bias=bias[:, s:s + 1]).then_inc(sg["h_done"].sem, 1)
                    if b and q < 3:
                        (compress, turn, score)[q](b - 1)
                if b == 0:
                    new = io["s_new"].rearrange("s b (g d) -> s (b g) d", g=NG)
                    for i in range(4):
                        for n in range(HG):
                            act.dma_start((new_k, new_v)[i % 2][n::HG, i // 2, :], new[i]).then_inc(new_in.sem, 16)
            act.wait_ge(*at("sc", NB))
            act.activation(prob[:, 0:PAST], bs[:].rearrange("p q n -> p (q n)"), ACT.Copy).then_inc(sg["sc_done"].sem, 1)
            for step in (compress, turn, score):
                step(NB - 1)
            act.wait_ge(new_in.sem, new_in.at(16 * 4 * HG))

        @block.vector
        def _(dve):
            chain = Chain(core, dve, "dve_chain")
            dve.memset(qz[:], 0.0).then_inc(sg["qz"].sem, 1)
            dve.wait_ge(*at("qz", 1))
            for b in range(NB):
                for gp in range(2):
                    ins = dve.tensor_copy(qz[:, gp, b, b * NH + gp * 8:b * NH + gp * 8 + 8], qblk[1][:, gp, b, :])
            ins.then_inc(sg["qz"].sem, 1)
            for b in range(NB):
                dve.wait_ge(*at("sq", b + 1))
                dve.tensor_reduce(ss[:], sq[:], AXX, ALU.add).then_inc(sg["ss"].sem, 1)
                dve.wait_ge(*at("rt", b + 1))
                chain.link(dve.reciprocal(ss[:], ss[:]))
                if b:
                    dve.wait_ge(*at("t", b))
                chain.link(dve.tensor_tensor(kn[:], bo[0:NC_S, 0:256].rearrange("p (g d) -> p g d", d=HD),
                                             ss[:].rearrange("p (g o) -> p g o", o=1).broadcast_to([NC_S, NG, HD]),
                                             ALU.mult))
                dve.tensor_tensor(kn[:], kn[:], g0[0:NC_S, :].rearrange("p (o d) -> p o d", o=1)
                                  .broadcast_to([NC_S, NG, HD]), ALU.mult).then_inc(sg["kn"].sem, 1)
            chain.close()

    pt_in.close(16)
    new_in.close(16 * 4 * HG)
    for u in range(2):
        pg_in[u].close(16 * NPAGE * NB // 2)
    for n in names:
        sg[n].close({"h": 4 * NB, "h_done": 4 * NB, "sc_done": 1, "qz": 2}.get(n, NB))
    core.end_stage()


def nsa_sample_attend(core, j, qz, Sc, vcs, prob, kn, vn, o):
    nc, io = core.nc, core.io
    names = ("scT", "nmx", "ecmp", "p", "pT", "pT_done", "blk", "blk_done", "grp", "win", "max", "e", "weights", "wT",
             "wT_done", "pv", "y_used", "out")
    sg = {n: core.sig("nsv_" + n) for n in names}
    in_, loc_in, spilled, back = (core.sig("nsv_" + n + "_dma") for n in ("in", "loc", "spilled", "back"))
    pt_in, wk_in = core.sig("nsv_pt_in"), core.sig("nsv_wk_in")
    NVS = 3
    NYB = 3
    v_in = [core.sig(f"nsv_v_in{u}") for u in range(NVS)]
    with ExitStack() as inner:
        sb, ps = tiles(core, inner)
        pt = sb("pt", [1, NB * NPAGE], I32)
        V = [sb(f"V{u}", [P, NK, KVW]) for u in range(NVS)]
        wk = sb("wk", [P, NB, 2, NWT * P])
        c2s, grp = sb("c2s", [NC_S, NSLC]), sb("grp", [P, P])
        keep, force = sb("keep", [P, NSLC]), sb("force", [P, NSLC])
        before = sb("before", [P, NSLC, NSLC])
        own = sb("own", [NH, NG])
        q = sb("q", [P, HD])
        gate = sb("gate", [P, 3])
        pc, pT = sb("pc", [P, NC_S]), sb("pT", [NC_S, 2, P])
        small = sb("small", [P, 20])
        blk, score = sb("blk", [P, NSLC]), sb("score", [P, NSLC])
        gt, eq = sb("gt", [P, NSLC, NSLC]), sb("eq", [P, NSLC, NSLC])
        madd = sb("madd", [P, NSLC])
        dg = sb("dg", [P, 2, P])
        prod = sb("prod", [P, 2, HD])
        probT = wk[:].rearrange("p b g n -> p (b g n)")[:, 0:NK * P].rearrange("p (k n) -> p k n", n=P)
        fin = sb("fin", [NH, NB, HD])
        bank = ps("bank", [P, 8, 512])
        block = inner.enter_context(nc.Block())
        NMX, DEN_C, R_C, SN, M, EN, DEN, RD, NM, WN = (slice(0, 1), slice(1, 2), slice(2, 3), slice(3, 5), slice(5, 7),
                                                       slice(7, 9), slice(9, 11), slice(11, 13), slice(13, 15), slice(15, 17))
        past, win = prob[:, 0:PAST], prob[:, PAST:NK * P]

        def at(n, c=1):
            return sg[n].sem, sg[n].at(c)

        consts = ((c2s, "c_c2s"), (grp, "c_grp"), (keep, "c_keep"), (force, "c_force"), (before, "c_before"), (own, "c_own"))

        def load_pages(eng, b, first, end):
            with eng.Fori(first, end) as p:
                page = eng.value_load(pt[0:1, bass.ds(p + NPAGE * b, 1)], min_val=0, max_val=io["cache_v"].shape[1] - 1)
                eng.dma_start(V[b % NVS][:, bass.ds(p, 1), :], io["cache_v"][j, bass.ds(page, 1)].rearrange("o p n -> p o n")
                              ).then_inc(v_in[b % NVS].sem, 16)

        @block.sync
        def _(sync):
            sync.dma_start(pt[:], io["page_table"]).then_inc(pt_in.sem, 16)
            sync.wait_ge(pt_in.sem, pt_in.at(16))
            for b in range(NB):
                if b >= NVS:
                    sync.wait_ge(*at("pv", b - NVS + 1))
                sync.dma_start(V[b % NVS][:, NPAGE:NK, :], io["cache_wv"][j, b]).then_inc(v_in[b % NVS].sem, 16)
                load_pages(sync, b, 0, NPAGE if b < NVS else NPAGE // 2)
            sync.wait_ge(*at("out"))
            sync.dma_start(io["s_o"].rearrange("b (h d) -> h b d", d=HD), fin[:]).then_inc(spilled.sem, 16)
            sync.wait_ge(spilled.sem, spilled.at(16))
            sync.dma_start(o[0:NB, NT, :], io["s_o"]).then_inc(back.sem, 16)
            sync.wait_ge(back.sem, back.at(16))

        @block.scalar
        def _(act):
            act.dma_start(q[:, :], io["s_q"].rearrange("b (h d) -> (b h) d", d=HD)).then_inc(loc_in.sem, 16)
            act.dma_start(gate[:, :], io["s_g3"].rearrange("b (h g) -> (b h) g", g=3)).then_inc(loc_in.sem, 16)
            for d, n in consts:
                act.dma_start(d[:], io[n]).then_inc(in_.sem, 16)
            for b in range(NB):
                act.dma_start(wk[:, b], io["cache_wkT"][j, b].rearrange("p g t n -> p g (t n)")).then_inc(wk_in.sem, 16)
            act.wait_ge(*at("nmx"))
            act.activation(pc[:, :], bank[:, 0, 0:NC_S], ACT.Exp, bias=small[:, NMX], accum_out=small[:, DEN_C]
                           ).then_inc(sg["ecmp"].sem, 1)
            for i in range(2):
                act.wait_ge(*at("pT", i + 1))
                act.activation(pT[:, i, :], bank[0:NC_S, 1, i * P:(i + 1) * P], ACT.Copy).then_inc(sg["pT_done"].sem, 1)
                if i == 0:
                    act.wait_ge(*at("blk"))
                    act.activation(blk[:, :], bank[:, 2, 0:NSLC], ACT.Copy).then_inc(sg["blk_done"].sem, 1)
            act.wait_ge(*at("max"))
            act.activation(past, past, ACT.Exp, bias=small[:, 13:14], accum_out=small[:, 9:10])
            act.activation(win, win, ACT.Exp, bias=small[:, 14:15], accum_out=small[:, 10:11])
            act.activation(small[:, EN], small[:, EN], ACT.Exp).then_inc(sg["e"].sem, 1)
            for i in range(NK // 4):
                act.wait_ge(*at("wT", i + 1))
                act.activation(probT[:, 4 * i:4 * i + 4, :].rearrange("p k n -> p (k n)"), bank[:, 3 + i, :], ACT.Copy
                               ).then_inc(sg["wT_done"].sem, 1)
            act.wait_ge(pt_in.sem, pt_in.at(16))
            for b in range(NVS, NB):
                act.wait_ge(*at("pv", b - NVS + 1))
                load_pages(act, b, NPAGE // 2, NPAGE)

        @block.tensor
        def _(pe):
            pe.transpose(bank[:, 0, 0:NC_S], Sc[:, :], core.ident[0:NC_S, 0:NC_S]).then_inc(sg["scT"].sem, 1)
            pe.wait_ge(*at("p"))
            pe.transpose(bank[0:NC_S, 1, 0:P], pc[:, :], core.ident[:, :]).then_inc(sg["pT"].sem, 1)
            pe.wait_ge(*at("pT_done"))
            pe.wait_ge(in_.sem, in_.at(16 * len(consts)))
            pe.matmul(bank[:, 2, 0:NSLC], pT[:, 0, :], c2s[:, :], start=True, stop=True).then_inc(sg["blk"].sem, 1)
            pe.wait_ge(*at("blk_done"))
            pe.matmul(bank[:, 2, 64:64 + NSLC], grp[:, :], blk[:, :], start=True, stop=True).then_inc(sg["grp"].sem, 1)
            pe.wait_ge(*at("p", 2))
            pe.transpose(bank[0:NC_S, 1, P:2 * P], pc[:, :], core.ident[:, :]).then_inc(sg["pT"].sem, 1)
            pe.wait_ge(wk_in.sem, wk_in.at(16 * NB))
            for b in range(NB):
                for gp in range(2):
                    mm = pe.matmul(bank[:, 3, :], qz[:, gp, b, :], wk[:, b, gp, :], start=(b == 0 and gp == 0),
                                   stop=(b == NB - 1 and gp == 1))
            mm.then_inc(sg["win"].sem, 1)
            pe.wait_ge(*at("weights"))
            for k in range(NK):
                mm = pe.transpose(bank[:, 3 + k // 4, (k % 4) * P:(k % 4 + 1) * P], prob[:, k * P:(k + 1) * P],
                                  core.ident[:, :])
                if k % 4 == 3:
                    mm.then_inc(sg["wT"].sem, 1)
            pe.wait_ge(*at("wT_done", NK // 4))
            pe.wait_ge(*at("pT_done", 2))
            for b in range(NB):
                u, y = b % NVS, bank[0:NH, b % NYB, :]
                cols = slice(b * NH, b * NH + NH)
                if b >= NYB:
                    pe.wait_ge(*at("y_used", b - NYB + 1))
                pe.wait_ge(v_in[u].sem, v_in[u].at(16 * (NPAGE + 1) * (b // NVS + 1)))
                for k in range(NK):
                    pe.matmul(y[:, 0:KVW], probT[:, k, cols], V[u][:, k, :], start=(k == 0), stop=False)
                pe.matmul(y[:, 0:KVW], pT[:, 1, cols], vcs[:, b, :], start=False, stop=True)
                for a in range(2):
                    mm = pe.matmul(y[:, KVW:KVW + HD], dg[:, a, cols], vn[:, a, :], start=(a == 0), stop=(a == 1))
                mm.then_inc(sg["pv"].sem, 1)

        @block.vector
        def _(dve):
            chain = Chain(core, dve, "dve_chain")
            link = chain.link
            dve.wait_ge(*at("scT"))
            dve.tensor_reduce(small[:, NMX], bank[:, 0, 0:NC_S], AXX, ALU.max, negate=True).then_inc(sg["nmx"].sem, 1)
            dve.wait_ge(*at("ecmp"))
            link(dve.reciprocal(small[:, R_C], small[:, DEN_C]))
            dve.tensor_scalar(pc[:, :], pc[:, :], small[:, R_C], None, ALU.mult).then_inc(sg["p"].sem, 1)
            dve.wait_ge(in_.sem, in_.at(16 * len(consts)))
            dve.wait_ge(loc_in.sem, loc_in.at(32))
            dve.wait_ge(*at("grp"))
            dve.tensor_scalar(pc[:, :], pc[:, :], gate[:, 0:1], None, ALU.mult).then_inc(sg["p"].sem, 1)
            link(dve.tensor_tensor(score[:, :], bank[:, 2, 64:64 + NSLC], keep[:, :], ALU.mult))
            link(dve.tensor_tensor(score[:, :], score[:, :], force[:, :], ALU.add))
            other = score[:, :].rearrange("p (o i) -> p o i", o=1).broadcast_to([P, NSLC, NSLC])
            mine = score[:, :].rearrange("p (j o) -> p j o", o=1).broadcast_to([P, NSLC, NSLC])
            dve.tensor_tensor(gt[:], other, mine, ALU.is_gt)
            link(dve.tensor_tensor(eq[:], other, mine, ALU.is_equal))
            link(dve.tensor_tensor(eq[:], eq[:], before[:], ALU.mult))
            link(dve.tensor_tensor(gt[:], gt[:], eq[:], ALU.add))
            link(dve.tensor_reduce(madd[:, :], gt[:], AXX, ALU.add))
            link(dve.tensor_scalar(madd[:, :], madd[:, :], NSEL - 0.5, None, ALU.is_gt))
            link(dve.tensor_scalar(madd[:, :], madd[:, :], NEG, None, ALU.mult))
            blocks = past.rearrange("p (j n) -> p j n", n=HD)
            link(dve.tensor_tensor(blocks, blocks, madd[:, 0:NSLC - 1].rearrange("p (j o) -> p j o", o=1)
                                   .broadcast_to([P, NSLC - 1, HD]), ALU.add))
            link(dve.tensor_tensor(prod[:], kn[:], q[:, :].rearrange("p (o d) -> p o d", o=1).broadcast_to([P, 2, HD]),
                                   ALU.mult))
            link(dve.tensor_reduce(small[:, SN], prod[:], AXX, ALU.add))
            dve.wait_ge(*at("win"))
            link(dve.tensor_copy(win, bank[:, 3, :]))
            link(dve.tensor_scalar(win[:, 0:1], win[:, 0:1], NEG, None, ALU.add))
            dve.tensor_reduce(small[:, 5:6], past, AXX, ALU.max)
            link(dve.tensor_reduce(small[:, 6:7], win, AXX, ALU.max))
            link(dve.tensor_tensor(small[:, M], small[:, M], small[:, SN], ALU.max))
            link(dve.tensor_scalar(small[:, NM], small[:, M], -1.0, None, ALU.mult))
            dve.tensor_tensor(small[:, EN], small[:, SN], small[:, M], ALU.subtract).then_inc(sg["max"].sem, 1)
            dve.wait_ge(*at("e"))
            link(dve.tensor_tensor(small[:, DEN], small[:, DEN], small[:, EN], ALU.add))
            link(dve.reciprocal(small[:, RD], small[:, DEN]))
            link(dve.tensor_tensor(small[:, RD], small[:, RD], gate[:, 1:3], ALU.mult))
            link(dve.tensor_tensor(small[:, WN], small[:, RD], small[:, EN], ALU.mult))
            for a in range(2):
                dve.tensor_scalar(dg[:, a, :], core.ident[:, :], small[:, 15 + a:16 + a], None, ALU.mult)
            dve.tensor_scalar(past, past, small[:, 11:12], None, ALU.mult)
            dve.tensor_scalar(win, win, small[:, 12:13], None, ALU.mult).then_inc(sg["weights"].sem, 1)
            for b in range(NB):
                y = bank[0:NH, b % NYB, :]
                dve.wait_ge(*at("pv", b + 1))
                link(dve.tensor_copy(fin[:, b, :], y[:, KVW:KVW + HD]))
                for g in range(NG):
                    ins = dve.scalar_tensor_tensor(out=fin[:, b, :], in0=y[:, g * HD:(g + 1) * HD], scalar=own[:, g:g + 1],
                                                   in1=fin[:, b, :], op0=ALU.mult, op1=ALU.add)
                    if g < NG - 1:
                        link(ins)
                ins.then_inc(sg["y_used"].sem, 1)
            dve.wait_ge(*at("y_used", NB))
            dve.engine_nop().then_inc(sg["out"].sem, 1)
            chain.close()

    pt_in.close(16)
    wk_in.close(16 * NB)
    in_.close(16 * len(consts))
    loc_in.close(32)
    spilled.close(16)
    back.close(16)
    for u in range(NVS):
        v_in[u].close(16 * (NPAGE + 1) * len(range(u, NB, NVS)))
    for n in names:
        sg[n].close({"p": 2, "pT": 2, "pT_done": 2, "wT": NK // 4, "wT_done": NK // 4, "pv": NB, "y_used": NB}.get(n, 1))
    core.end_stage()


def nsa_out(core, j, o):
    nc, io = core.nc, core.io
    tr, tr_hi, tr_done = core.sig("nso_tr"), core.sig("nso_tr_hi"), core.sig("nso_tr_done")
    lin_used = core.sig("lin_used")
    with ExitStack() as inner:
        sb, ps = tiles(core, inner)
        o_hi, o_lo = sb("o_hi", [P, KC, T], F32R), sb("o_lo", [P, KC, T], F32R)
        w = SplitWeights(core, sb, "nso_w", KC)
        acc = [ps(f"acc{u}", [P, 4, 512]) for u in range(2)]
        block = inner.enter_context(nc.Block())

        def turned(t):
            rows = min(P, T - P * t)
            src = acc[t // 2 % 2][:, 2 * (t % 2):2 * (t % 2) + 2, :].rearrange("p a (c t) -> p (a c) t", t=P)
            return src[:, :, 0:rows], slice(P * t, P * t + rows)

        @block.sync
        def _(sync):
            split_linear_sync(sync, w, io["nsa_wo"][j], KC)

        @block.tensor
        def _(pe):
            for t in range(NT + 1):
                rows = min(P, T - P * t)
                if t >= 4:
                    pe.wait_ge(tr_done.sem, tr_done.at(t - 3))
                for c in range(KC):
                    mm = pe.transpose(acc[t // 2 % 2][:, 2 * (t % 2) + c // 4, (c % 4) * P:(c % 4) * P + rows],
                                      o[0:rows, t, c * P:(c + 1) * P], core.ident[0:rows, 0:rows])
                mm.then_inc(tr.sem, 1)
            pe.wait_ge(tr_done.sem, tr_done.at(NT + 1))
            split_linear_pe(core, pe, w, o_hi, o_lo, acc, KC)

        @block.scalar
        def _(act):
            for t in range(NT + 1):
                src, cols = turned(t)
                act.wait_ge(tr.sem, tr.at(t + 1))
                act.activation(o_hi[:, :, cols], src, ACT.Copy).then_inc(tr_hi.sem, 1)
                if t in (1, 2):
                    w.cut_hi(act, KC, t - 1)
            for c in range(2, KC):
                w.cut_hi(act, KC, c)

        @block.vector
        def _(dve):
            dve.sem_inc(lin_used.sem, 2)
            for t in range(NT + 1):
                src, cols = turned(t)
                dve.wait_ge(tr_hi.sem, tr_hi.at(t + 1))
                dve.tensor_tensor(o_lo[:, :, cols], src, o_hi[:, :, cols].bitcast(F32), ALU.subtract
                                  ).then_inc(tr_done.sem, 1)
            for c in range(2):
                w.cut_lo(dve, KC, c)
            split_linear_dve(core, dve, w, acc, KC)

    w.close(KC)
    lin_used.close(KC + 2)
    for s in (tr, tr_hi, tr_done):
        s.close(NT + 1)
    core.end_stage()


def nsa_stage(core, layer):
    j = layer // 3
    with ExitStack() as stage:
        sb, _ps = tiles(core, stage)
        o = sb("o", [P, NT + 1, D])
        w1, w2 = sb("cmp_w1", [P, 2, CMP_LP, P]), sb("cmp_w2", [P, 2, HD])
        pe_emb = sb("pe_emb", [P, 2, CMP_LP])
        bias, g0 = sb("cmp_bias", [P, 2]), sb("cmp_gain", [P, HD])
        qblk = [sb(f"qblk{i}", [P, 2, NB, 8]) for i in range(2)]
        with ExitStack() as prompt:
            sbp, _ps = tiles(core, prompt)
            proj = sbp("proj", [P, NT + 1, PROJ])
            nsa_project(core, j, layer, proj, o,
                        ((w1, "nsa_w1"), (w2, "nsa_w2"), (pe_emb, "nsa_pe"), (g0, "nsa_g0")))
            qnT, qrT = sbp("qnT", [P, HP, SEQ]), sbp("qrT", [P, HP, SEQ])
            kT = sbp("kT", [P, 2 * NG, SEQ])
            kcT, vc = sbp("kcT", [P, NG, NC_P]), sbp("vc", [NC_P, NG, HD])
            nsa_heads(core, j, proj, qnT, qrT, kT, qblk)
            nsa_compress_prompt(core, j, w1, w2, pe_emb, bias, g0, kcT, vc)
            nsa_attend_compressed(core, proj, qnT, kcT, vc, o)
            nsa_attend_causal(core, proj, qrT, kT, o)
        Sc, vcs = sb("Sc", [NC_S, P]), sb("vcs", [NC_S, NB, KVW])
        prob = sb("prob", [P, NK * P])
        qz = core.hT[:].rearrange("p k t -> p (k t)")[:, 0:2 * NB * P].rearrange("p (g b n) -> p g b n", g=2, b=NB)
        kn, vn = sb("new_k", [P, 2, HD]), sb("new_v", [P, 2, HD])
        nsa_sample_scores(core, j, w1, w2, bias, g0, qblk, qz, Sc, vcs, prob, kn, vn)
        nsa_sample_attend(core, j, qz, Sc, vcs, prob, kn, vn, o)
        nsa_out(core, j, o)


CONST_COLS = ["eps_rms", "eps_ln", "eps_gn", "neg_half_exp", "one", "tiny"]


def begin_stage(core):
    nc, io = core.nc, core.io
    ctx = core.ctx

    def sb(name, shape, dt=F32):
        return ctx.enter_context(nc.sbuf_tensor(name, shape, dt))

    core.xT = sb("xT", [P, KC, T])
    core.hT = sb("hT", [P, KC, T])
    core.gains = sb("gains", [P, 2 * DEPTH, KC])
    core.ones = sb("ones", [P, P])
    core.ident = sb("ident", [P, P])
    core.cols = sb("cols", [P, len(CONST_COLS)])
    core.col = lambda name: core.cols[:, CONST_COLS.index(name):CONST_COLS.index(name) + 1]
    loaded = core.sig("begin_loaded")
    with ExitStack() as stage:
        block = stage.enter_context(nc.Block())

        @block.sync
        def _(sync):
            sync.dma_start(core.xT[:], io["xT"]).then_inc(loaded.sem, 16)
            sync.dma_start(core.gains[:], io["gains"]).then_inc(loaded.sem, 16)
            sync.dma_start(core.ones[:], io["c_ones"]).then_inc(loaded.sem, 16)
            sync.dma_start(core.ident[:], io["c_ident"]).then_inc(loaded.sem, 16)
            sync.dma_start(core.cols[:], io["c_cols"]).then_inc(loaded.sem, 16)
            sync.wait_ge(loaded.sem, loaded.at(80))
    loaded.close(80)
    core.end_stage()


def end_stage(core):
    nc, io = core.nc, core.io
    stored = core.sig("end_stored")
    with ExitStack() as stage:
        block = stage.enter_context(nc.Block())

        @block.sync
        def _(sync):
            sync.dma_start(io["yT"], core.xT[:]).then_inc(stored.sem, 16)
            sync.wait_ge(stored.sem, stored.at(16))
    stored.close(16)
    core.end_stage()


def program(nc, io, plan):
    with ExitStack() as ctx:
        core = Core(nc, ctx, io)
        begin_stage(core)
        for name, arg in plan:
            STAGES[name](core, arg)
        end_stage(core)


STAGES = {"ffn": ffn_stage, "conv": conv_stage, "rwkv": rwkv_stage, "nsa": nsa_stage}
PLAN = [("nsa", 0), ("ffn", 0), ("rwkv", 1), ("ffn", 1), ("conv", 2), ("ffn", 2), ("nsa", 3), ("ffn", 3)]



def chunked(w, k, n):
    K, N = w.shape[-2:]
    lead = w.shape[:-2]
    w = w.reshape(*lead, K // k, k, N // n, n)
    m = len(lead)
    return np.ascontiguousarray(w.transpose(*range(m), m + 2, m + 1, m, m + 3))


def by_lane(v):
    v = v.reshape(*v.shape[:-1], KC, P)
    return np.moveaxis(v, -1, 0)


def layouts(x_prompt, x_sample, norms, ffn_w_gu, ffn_w_down, **rest):
    a = {}
    nsa_layouts(a, **rest)
    conv_layouts(a, **rest)
    rwkv_layouts(a, **rest)
    x = np.concatenate([x_prompt[0], x_sample[:, 0]], 0)
    a["xT"] = x.T.reshape(KC, P, T).transpose(1, 0, 2)
    a["gains"] = norms.reshape(2 * DEPTH, KC, P).transpose(2, 0, 1)
    gu = chunked(ffn_w_gu, P, P)
    a["w_gu"] = np.stack([gu[:, :FC], gu[:, FC:]], 3)
    a["w_down"] = chunked(ffn_w_down, P, P)
    a["c_ones"] = np.ones((P, P), np.float32)
    a["c_ident"] = np.eye(P, dtype=np.float32)
    col = dict(eps_rms=RMS_EPS, eps_ln=LN_EPS, eps_gn=GN_EPS, neg_half_exp=-np.exp(-0.5), one=1.0, tiny=1e-12)
    a["c_cols"] = np.tile(np.array([col[c] for c in CONST_COLS], np.float32), (P, 1))
    return {k: np.ascontiguousarray(v) for k, v in a.items()}


def conv_layouts(a, state_conv, conv_w_pw1, conv_b_pw1, conv_w_dw, conv_b_dw, conv_ln_w, conv_ln_b, conv_w_pw2,
                 conv_b_pw2, **rest):
    w = chunked(conv_w_pw1[0], P, P)
    a["conv_w1"] = np.stack([w[:KC], w[KC:]], 2)
    a["conv_w2"] = chunked(conv_w_pw2[0], P, P)
    a["conv_par"] = by_lane(np.stack([conv_b_pw1[0, :D], conv_b_pw1[0, D:], conv_b_dw[0], conv_ln_w[0], conv_ln_b[0],
                                      conv_b_pw2[0]]))
    a["conv_taps"] = by_lane(conv_w_dw[0]).transpose(0, 2, 1)
    a["conv_hist"] = by_lane(state_conv[0]).transpose(0, 3, 1, 2)


def rwkv_layouts(a, state_rwkv_wkv, state_rwkv_shift, rwkv_mix, rwkv_w_rkv, rwkv_w0, rwkv_w1, rwkv_w2, rwkv_a0, rwkv_a1,
                 rwkv_a2, rwkv_g1, rwkv_g2, rwkv_k_k, rwkv_k_a, rwkv_r_k, rwkv_ln_w, rwkv_ln_b, rwkv_w_out, **rest):
    vectors = dict(k_k=rwkv_k_k[0], k_a=rwkv_k_a[0], r_k=rwkv_r_k[0].reshape(D), ln_w=rwkv_ln_w[0], ln_b=rwkv_ln_b[0],
                   w0=rwkv_w0[0], a0=rwkv_a0[0], **{f"mix{m}": rwkv_mix[0, m] for m in range(6)})
    a["rwkv_par"] = by_lane(np.stack([vectors[n] for n in MIX]))
    a["rwkv_shift"] = by_lane(state_rwkv_shift[0]).transpose(0, 2, 1)
    a["rwkv_rkv"] = chunked(rwkv_w_rkv[0], P, P).reshape(3 * KC, P, KC, P)
    a["rwkv_wo"] = chunked(rwkv_w_out[0], P, P)
    for m, (down, up) in enumerate(((rwkv_w1, rwkv_w2), (rwkv_a1, rwkv_a2), (rwkv_g1, rwkv_g2))):
        a[f"rwkv_down{m}"] = down[0].reshape(KC, P, -1).transpose(1, 0, 2)
        a[f"rwkv_up{m}"] = up[0]
    a["rwkv_state"] = state_rwkv_wkv[0].reshape(NB * NH, HD, HD)
    head = np.arange(P) // HD
    sel = (2 * np.arange(KC)[None, :, None] + head[:, None, None] == np.arange(NH)).astype(np.float32)
    a["c_sel"], a["c_selT"] = sel, sel.transpose(2, 1, 0)
    a["c_blk"] = (head[:, None] == head).astype(np.float32)
    a["c_reset"] = np.tile((np.arange(SEQ) % CH != 0).astype(np.float32), (P, 1))
    s, t = np.arange(P)[:, None], np.arange(P)[None, :]
    same = s // CH == t // CH
    a["c_mask4"] = np.stack([same & (s < t), -1.0 * (same & (s <= t)), same & (s < t), same & (s <= t)],
                            1).astype(np.float32)
    a["c_level"] = np.stack([(s >> l + 1 == t >> l + 1) & ((t >> l) % 2 == 1) & ((s >> l) % 2 == 0)
                             for l in range(LEVELS)], 1).astype(np.float32)


def nsa_layouts(a, cache_nsa, cache_nsa_win, page_table, nsa_w_in, nsa_q_norm, nsa_k_norm, nsa_cmp_pe, nsa_cmp_w1,
                nsa_cmp_w2, nsa_w_out, **rest):
    n, pool = cache_nsa.shape[:2]
    a["page_table"] = page_table.reshape(1, NB * NPAGE)
    c = cache_nsa[:, :, :, 0:2].reshape(n, pool, 8, 8, 2, 2, NG, HD)
    cmp_ = c.transpose(0, 1, 4, 7, 5, 6, 3, 2).reshape(n, pool, P, PGC)
    ks = cache_nsa[:, :, :, 2].reshape(n, pool, P, 2, 2, HD).transpose(0, 1, 4, 5, 3, 2).reshape(n, pool, P, 2 * P)
    a["cache_kT"] = np.concatenate([cmp_, ks], 3)
    a["cache_v"] = cache_nsa[:, :, :, 3].reshape(n, pool, P, KVW)
    w = cache_nsa_win.reshape(n, NB, NWT, P, 2, KVW)
    a["cache_win"] = cache_nsa_win.reshape(n, NB, NWT * P, 2 * KVW)
    a["cache_wkT"] = w[:, :, :, :, 0].reshape(n, NB, NWT, P, 2, P).transpose(0, 1, 5, 4, 2, 3)
    a["cache_wv"] = w[:, :, :, :, 1].transpose(0, 1, 3, 2, 4)
    a["nsa_w_in"] = nsa_w_in.reshape(n, KC, P, PROJ).transpose(0, 2, 1, 3)
    a["nsa_wo"] = chunked(nsa_w_out, P, P)
    a["nsa_gq"] = np.broadcast_to(nsa_q_norm[:, None], (n, P, HD))
    a["nsa_g0"] = np.broadcast_to(nsa_k_norm[:, None, 0], (n, P, HD))
    a["nsa_gk"] = np.broadcast_to(nsa_k_norm[:, None, 1:3], (n, P, 2, HD))
    a["nsa_pe"] = nsa_cmp_pe.reshape(n, 2, CMP_LP, P).transpose(0, 3, 1, 2)
    a["nsa_w1"] = nsa_cmp_w1.reshape(n, 2, CMP_LP, P, P).transpose(0, 3, 1, 2, 4)
    a["nsa_w2"] = nsa_cmp_w2.transpose(0, 2, 1, 3)
    f = np.float32
    half = HD // 2
    inv = f(10000.0) ** (-np.arange(half, dtype=f) / f(half))
    pos = np.concatenate([np.arange(SEQ), np.full(P, PAST)]).astype(f)
    ang = (pos[:, None] * inv).astype(f)
    cos, sin = np.cos(ang).astype(f), np.sin(ang).astype(f)
    a["c_cos"] = np.concatenate([cos, cos], 1).reshape(NT + 1, P, HD).transpose(1, 0, 2)
    a["c_sin"] = np.concatenate([-sin, sin], 1).reshape(NT + 1, P, HD).transpose(1, 0, 2)
    ok = (np.arange(NC_P) * SEG + 2 * SEG - 1)[None, :] <= np.arange(SEQ)[:, None]
    a["c_cmp_one"] = ok.astype(f).reshape(NT, P, NC_P).transpose(1, 0, 2)
    a["c_cmp_add"] = np.where(ok, 0, NEG).astype(f).reshape(NT, P, NC_P).transpose(1, 0, 2)
    i = np.arange(P)
    a["c_causal"] = np.where(i[None, :] <= i[:, None], 0, NEG).astype(f)
    c0, j0 = np.arange(NC_S)[:, None] * SEG, np.arange(NSLC)[None, :] * HD
    a["c_c2s"] = ((c0 < j0 + HD) & (c0 + 2 * SEG > j0)).astype(f)
    a["c_grp"] = (i[:, None] // HG == i[None, :] // HG).astype(f)
    b = np.arange(NSLC)
    forced = (b == 0) | (b == NSLC - 1) | (b == NSLC - 2)
    a["c_keep"] = np.tile(1 - forced.astype(f), (P, 1))
    a["c_force"] = np.tile(np.where(forced, -NEG, 0).astype(f), (P, 1))
    a["c_before"] = np.tile((b[None, :] < b[:, None]).astype(f)[None], (P, 1, 1))
    a["c_own"] = (np.arange(NH)[:, None] // HG == np.arange(NG)[None, :]).astype(f)


OUTPUTS = {"yT": (P, KC, T), "conv_prompt": (P, KC, HIST), "conv_sample": (P, KC, NB, HIST), "shift_out": (P, KC, NB + 1),
           "wkv_prompt": (P, HP, HD), "wkv_sample": (NB * NH, HD, HD),
           "rows_prompt": (2, SEQ, 4 * KVW), "rows_sample": (2, NB, 4 * KVW), "win_prompt": (2, SEQ, 2 * KVW),
           "win_sample": (2, NB, SEQ, 2 * KVW)}
SCRATCH = {"s_gate": (P, KC, T), "s_bonus": (P, KC, T), "s_vec": (NB, 6, D), "s_y": (NB, D),
           "s_new": (4, NB, KVW), "s_q": (NB, D), "s_g3": (NB, 3 * NH), "s_o": (NB, D)}


def results(o):

    def tokens(v):
        return v.transpose(2, 1, 0).reshape(v.shape[2], D)

    y, shift = tokens(o["yT"]), tokens(o["shift_out"])
    wkv = o["wkv_prompt"].reshape(2, HD, HP, HD).transpose(2, 0, 1, 3).reshape(1, 1, NH, HD, HD)
    return tuple(np.ascontiguousarray(v) for v in (
        y[None, 0:SEQ], y[SEQ:T, None],
        o["rows_prompt"].reshape(2, 1, SEQ, 4, NG, HD), o["rows_sample"].reshape(2, NB, 1, 4, NG, HD),
        o["win_prompt"].reshape(2, 1, SEQ, 2, NG, HD), o["win_sample"].reshape(2, NB, SEQ, 2, NG, HD),
        wkv, o["wkv_sample"].reshape(1, NB, NH, HD, HD),
        shift[None, 0:1], shift[None, 1:],
        tokens(o["conv_prompt"])[None, None], o["conv_sample"].transpose(2, 3, 1, 0).reshape(1, NB, HIST, D)))


def kernel(**inputs):
    import concourse.bacc as _bacc
    from concourse import mybir as _mybir
    from concourse.bass_utils import run_bass_kernel_spmd as _run

    nc = _bacc.Bacc("TRN2", target_bir_lowering=False, num_devices=1)
    arrays = layouts(**{name: np.asarray(a) for name, a in inputs.items()})
    io = {}
    for name, a in arrays.items():
        io[name] = nc.dram_tensor(f"in_{name}", a.shape, _mybir.dt.from_np(a.dtype), kind="ExternalInput").ap()
    for name, shape in OUTPUTS.items():
        io[name] = nc.dram_tensor(f"out_{name}", shape, F32, kind="ExternalOutput").ap()
    for name, shape in SCRATCH.items():
        io[name] = nc.dram_tensor(name, shape, F32, kind="Internal").ap()
    program(nc, io, PLAN)
    r = _run(nc, [{f"in_{name}": a for name, a in arrays.items()}], core_ids=[0])
    return results({name: r.results[0][f"out_{name}"] for name in OUTPUTS})
```
